# Optimizing a Trainium2 kernel written in Bass

```python
import math
import jax, jax.numpy as jnp
from jax import lax
import numpy as np

D_MODEL = 2048
BATCH = 1
SEQ = 512
DEPTH = 1

D_MIX = D_MODEL
D_POOL = D_MIX // 2
D_SSM = D_MIX - D_POOL
POOL_WINDOWS = (2, 4, 8, 16)
N_POOL_GROUPS = len(POOL_WINDOWS)
POOL_GROUP = D_POOL // N_POOL_GROUPS
SSM_GROUP = 16
N_SSM_GROUPS = D_SSM // SSM_GROUP
SSM_STATE = 64
DT_MIN = 1e-3
DT_MAX = 1e-1
N_EXPERT_GROUPS = 4
EXPERTS_PER_GROUP = 8
N_EXPERTS = N_EXPERT_GROUPS * EXPERTS_PER_GROUP
TOP_K_INNER = 2
D_EXPERT = D_MODEL // 4
MOE_BLOCK = 128
LN_EPS = 1e-5

kernel_name = "hybrid_pool_s5_hmoe_deepnorm_encoder"

def layer_norm(h, g, b):
    hf = h.astype(jnp.float32)
    mu = jnp.mean(hf, axis=-1, keepdims=True)
    var = jnp.mean(jnp.square(hf - mu), axis=-1, keepdims=True)
    out = (hf - mu) * lax.rsqrt(var + LN_EPS) * g.astype(jnp.float32) + b.astype(jnp.float32)
    return out.astype(h.dtype)

def pool_mixer(u, pool_w, pool_scale):
    bsz, s, _ = u.shape
    uf = u.astype(jnp.float32)
    cs = jnp.concatenate([jnp.zeros((bsz, 1, D_POOL), jnp.float32), jnp.cumsum(uf, axis=1)], axis=1)
    pos = jnp.arange(s, dtype=jnp.int32)
    diffs = []
    for g, w in enumerate(POOL_WINDOWS):
        sl = slice(g * POOL_GROUP, (g + 1) * POOL_GROUP)
        lo = jnp.clip(pos - w // 2, 0, s)
        hi = jnp.clip(pos - w // 2 + w, 0, s)
        csg = cs[..., sl]
        cnt = (hi - lo).astype(jnp.float32)[None, :, None]
        mean = (csg[:, hi] - csg[:, lo]) / cnt
        diffs.append(mean - uf[..., sl])
    d = jnp.stack(diffs, axis=2).astype(u.dtype)
    y = jnp.einsum('bsgc,gcd->bsgd', d, pool_w).reshape(bsz, s, D_POOL)
    return y * pool_scale

def _complex_affine_combine(left, right):
    a1r, a1i, b1r, b1i = left
    a2r, a2i, b2r, b2i = right
    return (a1r * a2r - a1i * a2i,
            a1r * a2i + a1i * a2r,
            a2r * b1r - a2i * b1i + b2r,
            a2r * b1i + a2i * b1r + b2i)

def s5_bidirectional(u, a_re, a_im, log_dt, b_re, b_im, c_re, c_im, d_skip):
    bsz, s, _ = u.shape
    uf = u.astype(jnp.float32).reshape(bsz, s, N_SSM_GROUPS, SSM_GROUP).transpose(1, 0, 2, 3)
    y = d_skip.astype(jnp.float32).reshape(N_SSM_GROUPS, SSM_GROUP) * uf
    for dr in range(2):
        lr = a_re[dr].astype(jnp.float32)
        li = a_im[dr].astype(jnp.float32)
        dt = jnp.exp(log_dt[dr].astype(jnp.float32))[:, None]
        mag = jnp.exp(lr * dt)
        abar_r = mag * jnp.cos(li * dt)
        abar_i = mag * jnp.sin(li * dt)
        den = lr * lr + li * li
        zr = ((abar_r - 1.0) * lr + abar_i * li) / den
        zi = (abar_i * lr - (abar_r - 1.0) * li) / den
        br = b_re[dr].astype(jnp.float32)
        bi = b_im[dr].astype(jnp.float32)
        bbar_r = zr[..., None] * br - zi[..., None] * bi
        bbar_i = zr[..., None] * bi + zi[..., None] * br
        bu_r = jnp.einsum('sbgc,gpc->sbgp', uf, bbar_r)
        bu_i = jnp.einsum('sbgc,gpc->sbgp', uf, bbar_i)
        ar = jnp.broadcast_to(abar_r[None, None], (s, 1, N_SSM_GROUPS, SSM_STATE))
        ai = jnp.broadcast_to(abar_i[None, None], (s, 1, N_SSM_GROUPS, SSM_STATE))
        _, _, xr, xi = lax.associative_scan(_complex_affine_combine, (ar, ai, bu_r, bu_i),
                                            reverse=(dr == 1), axis=0)
        y = y + jnp.einsum('sbgp,gcp->sbgc', xr, c_re[dr].astype(jnp.float32)) \
              - jnp.einsum('sbgp,gcp->sbgc', xi, c_im[dr].astype(jnp.float32))
    return y.transpose(1, 0, 2, 3).reshape(bsz, s, D_SSM)

def hier_moe(h, router_g_w, router_g_b, router_e_w, router_e_b, w_gate, w_up, w_down):
    bsz, s, d = h.shape
    t = bsz * s
    xt = h.reshape(t, d)
    gl = (xt @ router_g_w).astype(jnp.float32) + router_g_b.astype(jnp.float32)
    gp = jax.nn.softmax(gl, axis=-1)
    grp = jnp.argmax(gl, axis=-1).astype(jnp.int32)
    p_grp = jnp.take_along_axis(gp, grp[:, None], axis=-1)
    el = (xt @ router_e_w).astype(jnp.float32) + router_e_b.astype(jnp.float32)
    el = el.reshape(t, N_EXPERT_GROUPS, EXPERTS_PER_GROUP)
    el_sel = jnp.take_along_axis(el, grp[:, None, None], axis=1)[:, 0]
    ep = jax.nn.softmax(el_sel, axis=-1)
    top_p, top_i = lax.top_k(ep, TOP_K_INNER)
    gate = p_grp * top_p / jnp.sum(top_p, axis=-1, keepdims=True)
    expert_id = grp[:, None] * EXPERTS_PER_GROUP + top_i.astype(jnp.int32)

    m = t * TOP_K_INNER
    e_flat = expert_id.reshape(m)
    tok = jnp.repeat(jnp.arange(t, dtype=jnp.int32), TOP_K_INNER)
    wt = gate.reshape(m)
    order = jnp.argsort(e_flat)
    e_sorted = e_flat[order]
    counts = jnp.bincount(e_flat, length=N_EXPERTS).astype(jnp.int32)
    starts = jnp.cumsum(counts) - counts
    pcounts = (counts + MOE_BLOCK - 1) // MOE_BLOCK * MOE_BLOCK
    pends = jnp.cumsum(pcounts)
    pstarts = pends - pcounts
    rank = jnp.arange(m, dtype=jnp.int32) - starts[e_sorted]
    dest = pstarts[e_sorted] + rank
    n_blocks = (m + MOE_BLOCK - 1) // MOE_BLOCK + N_EXPERTS
    n_slots = n_blocks * MOE_BLOCK
    slot_tok = jnp.full((n_slots,), t, jnp.int32).at[dest].set(tok[order])
    slot_w = jnp.zeros((n_slots,), jnp.float32).at[dest].set(wt[order])
    block_e = jnp.minimum(jnp.searchsorted(pends, jnp.arange(n_blocks, dtype=jnp.int32) * MOE_BLOCK,
                                           side='right'), N_EXPERTS - 1).astype(jnp.int32)
    x_pad = jnp.concatenate([xt, jnp.zeros((1, d), xt.dtype)], axis=0)
    xb = x_pad[slot_tok].reshape(n_blocks, MOE_BLOCK, d)

    def expert_block(args):
        xb_i, e = args
        hh = jax.nn.silu(xb_i @ w_gate[e]) * (xb_i @ w_up[e])
        return hh @ w_down[e]

    yb = lax.map(expert_block, (xb, block_e))
    yb = yb.reshape(n_slots, d).astype(jnp.float32) * slot_w[:, None]
    out = jnp.zeros((t + 1, d), jnp.float32).at[slot_tok].add(yb)[:t]
    return out.reshape(bsz, s, d).astype(h.dtype)

def setup_inputs(seed: int = 0) -> dict:
    key = jax.random.key(seed)
    ks = jax.random.split(key, 26)
    L = DEPTH
    f32 = jnp.float32
    beta = (8.0 * DEPTH) ** -0.25
    nrm = lambda k, shp, sc: jax.random.normal(k, shp, f32) * sc
    a_im_base = math.pi * jnp.arange(SSM_STATE, dtype=f32)
    return {
        "x": nrm(ks[0], (BATCH, SEQ, D_MODEL), 1.0),
        "w_in": nrm(ks[1], (L, D_MODEL, D_MIX), D_MODEL ** -0.5),
        "pool_w": nrm(ks[2], (L, N_POOL_GROUPS, POOL_GROUP, POOL_GROUP), POOL_GROUP ** -0.5),
        "pool_scale": 1.0 + nrm(ks[3], (L, D_POOL), 0.02),
        "ssm_a_re": -0.5 + nrm(ks[4], (L, 2, N_SSM_GROUPS, SSM_STATE), 0.01),
        "ssm_a_im": a_im_base + nrm(ks[5], (L, 2, N_SSM_GROUPS, SSM_STATE), 0.01),
        "ssm_log_dt": jax.random.uniform(ks[6], (L, 2, N_SSM_GROUPS), f32, math.log(DT_MIN), math.log(DT_MAX)),
        "ssm_b_re": nrm(ks[7], (L, 2, N_SSM_GROUPS, SSM_STATE, SSM_GROUP), (2 * SSM_GROUP) ** -0.5),
        "ssm_b_im": nrm(ks[8], (L, 2, N_SSM_GROUPS, SSM_STATE, SSM_GROUP), (2 * SSM_GROUP) ** -0.5),
        "ssm_c_re": nrm(ks[9], (L, 2, N_SSM_GROUPS, SSM_GROUP, SSM_STATE), SSM_STATE ** -0.5),
        "ssm_c_im": nrm(ks[10], (L, 2, N_SSM_GROUPS, SSM_GROUP, SSM_STATE), SSM_STATE ** -0.5),
        "ssm_d": nrm(ks[11], (L, D_SSM), 1.0),
        "glu_w": nrm(ks[12], (L, D_SSM, D_SSM), D_SSM ** -0.5),
        "glu_b": nrm(ks[13], (L, D_SSM), 0.01),
        "w_out": nrm(ks[14], (L, D_MIX, D_MODEL), beta * D_MIX ** -0.5),
        "ln1_g": 1.0 + nrm(ks[15], (L, D_MODEL), 0.02),
        "ln1_b": nrm(ks[16], (L, D_MODEL), 0.02),
        "router_g_w": nrm(ks[17], (L, D_MODEL, N_EXPERT_GROUPS), D_MODEL ** -0.5),
        "router_g_b": nrm(ks[18], (L, N_EXPERT_GROUPS), 0.01),
        "router_e_w": nrm(ks[19], (L, D_MODEL, N_EXPERTS), D_MODEL ** -0.5),
        "router_e_b": nrm(ks[20], (L, N_EXPERTS), 0.01),
        "w_gate": nrm(ks[21], (L, N_EXPERTS, D_MODEL, D_EXPERT), D_MODEL ** -0.5),
        "w_up": nrm(ks[22], (L, N_EXPERTS, D_MODEL, D_EXPERT), D_MODEL ** -0.5),
        "w_down": nrm(ks[23], (L, N_EXPERTS, D_EXPERT, D_MODEL), beta * D_EXPERT ** -0.5),
        "ln2_g": 1.0 + nrm(ks[24], (L, D_MODEL), 0.02),
        "ln2_b": nrm(ks[25], (L, D_MODEL), 0.02),
    }

def reference(x, w_in, pool_w, pool_scale, ssm_a_re, ssm_a_im, ssm_log_dt, ssm_b_re, ssm_b_im,
              ssm_c_re, ssm_c_im, ssm_d, glu_w, glu_b, w_out, ln1_g, ln1_b, router_g_w, router_g_b,
              router_e_w, router_e_b, w_gate, w_up, w_down, ln2_g, ln2_b):
    alpha = (2.0 * DEPTH) ** 0.25
    h = x
    for l in range(DEPTH):
        proj = h @ w_in[l]
        y_pool = pool_mixer(proj[..., :D_POOL], pool_w[l], pool_scale[l])
        y_ssm = s5_bidirectional(proj[..., D_POOL:], ssm_a_re[l], ssm_a_im[l], ssm_log_dt[l],
                                 ssm_b_re[l], ssm_b_im[l], ssm_c_re[l], ssm_c_im[l], ssm_d[l])
        y_ssm = jax.nn.gelu(y_ssm)
        y_ssm = (y_ssm * jax.nn.sigmoid(y_ssm @ glu_w[l].astype(jnp.float32)
                                        + glu_b[l].astype(jnp.float32))).astype(h.dtype)
        mix = jnp.concatenate([y_pool.astype(h.dtype), y_ssm], axis=-1) @ w_out[l]
        h = layer_norm(alpha * h + mix, ln1_g[l], ln1_b[l])
        ffn = hier_moe(h, router_g_w[l], router_g_b[l], router_e_w[l], router_e_b[l],
                       w_gate[l], w_up[l], w_down[l])
        h = layer_norm(alpha * h + ffn, ln2_g[l], ln2_b[l])
    return h


_drawn_inputs = setup_inputs


def setup_inputs(seed=0):
    import zlib

    import numpy as np

    out = dict(_drawn_inputs(seed))
    spreads = {}
    factors = {'pool_scale': 12.765,
     'ssm_a_re': 64.0,
     'ssm_a_im': 23.36,
     'ssm_log_dt': 23.832,
     'ssm_b_re': 28.96,
     'ssm_b_im': 28.008,
     'ssm_c_re': 31.136,
     'ssm_c_im': 26.32,
     'glu_b': 200.0,
     'router_g_b': 7.472,
     'router_e_b': 16.637,
     'ln2_g': 22.957,
     'ln2_b': 22.05,
     'glu_w': 4.351}
    for name, (base, spread) in spreads.items():
        noise = np.random.default_rng([zlib.crc32(name.encode()), seed]).standard_normal(out[name].shape)
        drawn = base * np.exp(spread * noise) if base else spread * noise
        out[name] = __import__('jax').numpy.asarray(drawn.astype(out[name].dtype))
    for name, factor in factors.items():
        out[name] = (out[name] * factor).astype(out[name].dtype)
    return out
```

```python
import math
from contextlib import ExitStack

import concourse.bass as bass
from concourse import mybir

F32 = mybir.dt.float32
I32 = mybir.dt.int32
U32 = mybir.dt.uint32
ALU = mybir.AluOpType
ACT = mybir.ActivationFunctionType
AX = mybir.AxisListType.X

P = 128
S = 512
D = 2048
KT = D // P
TT = S // P
NCOL = 512
NN = D // NCOL
CH = D // 2
MT = CH // P
WINDOWS = (2, 4, 8, 16)
PGT = MT // len(WINDOWS)
G = 64
C = 16
NST = 64
GP = G // 2
L = P // C
NCH = S // L
NG = 4
EPG = 8
NE = NG * EPG
F = 512
FT = F // P
SLOTS = 64
ROUNDS = S // SLOTS
EMPTY = 2 * S
PAD = 8
ALPHA = 2.0 ** 0.25
EPS = 1e-5
WQ = 4
CHUNK = 2048


def build(nc, x, w_in, pool_w, pool_scale, a_re, a_im, log_dt, b_re, b_im, c_re, c_im, ssm_d, glu_w, glu_b,
          w_out, ln1_g, ln1_b, rg_w, rg_b, re_w, re_b, w_gate, w_up, w_down, ln2_g, ln2_b, out):
    u_dram = nc.dram_tensor("u_scratch", (CH, L, NCH), F32, kind="Internal").ap()
    y_dram = nc.dram_tensor("y_scratch", (G, C, L, NCH), F32, kind="Internal").ap()
    lag_dram = nc.dram_tensor("lag_scratch", ((2 * L - 1) * C, G * C), F32, kind="Internal").ap()
    h_dram = nc.dram_tensor("h_scratch", (S, D), F32, kind="Internal").ap()
    slot_dram = nc.dram_tensor("slot_scratch", (S * NE, 1), I32, kind="Internal").ap()
    ye_dram = nc.dram_tensor("ye_scratch", (4 * S, D // 2), F32, kind="Internal").ap()

    with ExitStack() as ctx:
        def sb(name, shape, dt=F32):
            return ctx.enter_context(nc.sbuf_tensor(name, shape, dt))

        def sem(name):
            return ctx.enter_context(nc.semaphore(name))

        PS = ctx.enter_context(nc.psum_tensor("PS", [P, 8, NCOL], F32))

        r_x = sb("r_x", [P, 8192])
        r_bm0 = sb("r_bm0", [P, 8192])
        r_bm1 = sb("r_bm1", [P, 8192])
        r_t = sb("r_t", [P, 8192])
        r_ssm = sb("r_ssm", [P, 4096])
        r_u = sb("r_u", [P, 4096])
        r_pool = sb("r_pool", [P, 4096])
        r_c = sb("r_c", [P, 2048])
        ring = sb("ring", [P, 2, CHUNK])
        tmp = sb("tmp", [P, 2, S + 2 * PAD])
        ident = sb("ident", [P, P])
        par = sb("par", [P, 4, 2, GP])
        coef = sb("coef", [P, 2, 2, 2 * GP])
        edge = sb("edge", [P, len(WINDOWS), 16])
        vecs = sb("vecs", [P, 3, MT])
        neg_one = sb("neg_one", [P, 1])

        xT = r_x[:].rearrange("p (k t) -> p k t", k=KT)
        xrows = r_bm0[:].rearrange("p (i d) -> p i d", i=TT)
        st = r_x[:].rearrange("p (t r d g) -> p t r d g", t=NCH, r=2, d=2)
        st_flat = r_x[:].rearrange("p (t r e) -> p t r e", t=NCH, r=2)
        BM = [b[:].rearrange("p (g r m) -> p g r m", g=GP, r=2) for b in (r_bm0, r_bm1)]
        BT = r_t[:].rearrange("p (r g s c) -> p r g s c", r=2, g=GP, s=L)
        TP = r_t[:].rearrange("p (s c q g) -> p (s c) q g", s=L, c=C, q=2)
        EC = r_bm0[:].rearrange("p (r d g s c) -> p r d g s c", r=2, d=2, g=GP // 2, s=L)
        h1 = r_bm1[:].rearrange("p (i d) -> p i d", i=TT)
        pw = r_bm1[:, 0:2048].rearrange("p (q r e) -> p q r e", q=2, r=2)
        craw = r_bm1[:, 4096:6144].rearrange("p (r d b n) -> p r d b n", r=2, d=2, b=4)
        braw = r_bm1[:, 2048:4096].rearrange("p (r d g c) -> p r d g c", r=2, d=2, g=GP)
        pre = r_bm1[0:2 * GP, 6144:6144 + 14 * P].rearrange("p (q n) -> p q n", q=14)
        pdt = r_bm1[0:2 * GP, 6144 + 14 * P:6144 + 14 * P + 4]
        bbar = r_u[:, 0:2048].rearrange("p (r d g c) -> p r d g c", r=2, d=2, g=GP)
        ksb = r_u[:, 2048:4096].rearrange("p (d c q g) -> p d c q g", d=2, c=C, q=2)
        uT = r_ssm[:].rearrange("p (m t) -> p m t", m=MT)
        U = r_u[:].rearrange("p (g k) -> p g k", g=G)
        Z = r_u[:].rearrange("p (m t) -> p m t", m=MT)
        pd = r_pool[:].rearrange("p (m t) -> p m t", m=MT)
        FC = r_c[:].rearrange("p (r d g c) -> p r d g c", r=2, d=2, g=GP)

        ident_ready, edge_ready, ones_ready = sem("ident_ready"), sem("edge_ready"), sem("ones_ready")
        x_loaded, par_loaded, b_loaded, c_loaded = sem("x_loaded"), sem("par_loaded"), sem("b_loaded"), sem("c_loaded")
        vec_loaded = sem("vec_loaded")
        ring_loaded = [sem("ring_loaded0"), sem("ring_loaded1")]
        ring_used = sem("ring_used")
        xt_done = sem("xt_done")
        xt_act, xt_dve = sem("xt_act"), sem("xt_dve")
        pool_read = sem("pool_read")
        ssm_read = sem("ssm_read")
        u_stored, u_loaded = sem("u_stored"), sem("u_loaded")
        pre_act, pre_dve = sem("pre_act"), sem("pre_dve")
        pre_ready = sem("pre_ready")
        par_t, par_ready = sem("par_t"), sem("par_ready")
        ct_done, fc_ready = sem("ct_done"), sem("fc_ready")
        dve_chain = sem("dve_chain")
        bt_ready = sem("bt_ready")
        btt_done, bm_ready = sem("btt_done"), sem("bm_ready")
        lag_done, lag_copied = sem("lag_done"), sem("lag_copied")
        lag_stored, t_loaded = sem("lag_stored"), sem("t_loaded")
        pmix_done, pmix_ready = sem("pmix_done"), sem("pmix_ready")
        z_done, z_act, z_dve = sem("z_done"), sem("z_act"), sem("z_dve")
        scan_step, scan_ready = sem("scan_step"), sem("scan_ready")
        xr_loaded = sem("xr_loaded")
        wo_done, wo_read = sem("wo_done"), sem("wo_read")
        ec_ready = sem("ec_ready")
        y_done, y_copied, y_stored, y_loaded = sem("y_done"), sem("y_copied"), sem("y_stored"), sem("y_loaded")
        skip_done, gelu_ready = sem("skip_done"), sem("gelu_ready")
        glu_done, sig_ready, glu_ready = sem("glu_done"), sem("sig_ready"), sem("glu_ready")
        ln_loaded, ln2_loaded = sem("ln_loaded"), sem("ln2_loaded")
        std_asked, std_ready = sem("std_asked"), sem("std_ready")
        h_ready, h_stored = sem("h_ready"), sem("h_stored")
        ht_done, ht_ready = sem("ht_done"), sem("ht_ready")
        logit_done = sem("logit_done")
        exp_asked, exp_ready = sem("exp_asked"), sem("exp_ready")
        onehot_ready, rank_done = sem("onehot_ready"), sem("rank_done")
        iota_ready, table_cleared = sem("iota_ready"), sem("table_cleared")
        pos_ready, table_written, slots_loaded, slots_ready = (
            sem("pos_ready"), sem("table_written"), sem("slots_loaded"), sem("slots_ready"))
        counts_ready = sem("counts_ready")
        wg_loaded = [sem(f"wg_loaded{c}") for c in range(WQ)]
        wu_loaded = [sem(f"wu_loaded{c}") for c in range(WQ)]
        wd_loaded = [sem(f"wd_loaded{c}") for c in range(WQ)]
        w_used = sem("w_used")
        idx_ready = sem("idx_ready")
        rows_cleared = sem("rows_cleared")
        xg_loaded, xg_t, xgT_act, xgT_dve = sem("xg_loaded"), sem("xg_t"), sem("xgT_act"), sem("xgT_dve")
        gu_done, silu_ready, hid_ready = sem("gu_done"), sem("silu_ready"), sem("hid_ready")
        hid_t, hidT_ready = sem("hid_t"), sem("hidT_ready")
        down_done, ye_act, ye_dve, ye_stored = sem("down_done"), sem("ye_act"), sem("ye_dve"), sem("ye_stored")
        h_scaled = sem("h_scaled")
        pe_turn, pool_turn = sem("pe_turn"), sem("pool_turn")
        xs_loaded, xs_ready, xw_loaded, xg2_loaded = sem("xs_loaded"), sem("xs_ready"), sem("xw_loaded"), sem("xg2_loaded")
        xpe, xcopy = sem("xpe"), sem("xcopy")
        res_loaded, out_ready, out_stored = sem("res_loaded"), sem("out_ready"), sem("out_stored")

        wg = r_x[:].rearrange("p (k f) -> p k f", k=KT)
        wu = r_bm0[:].rearrange("p (k f) -> p k f", k=KT)
        wd = r_t[:].rearrange("p (k d) -> p k d", k=FT)
        ln1g = r_c[:]
        ln1b = r_pool[:, 0:2048]
        rw = r_pool[:, 2048:2048 + KT * (NG + NE)].rearrange("p (k e) -> p k e", k=KT)
        rbias = r_pool[:, 2700:2700 + NG + NE]
        hT = r_u[:].rearrange("p (b k t) -> p b k t", b=2, k=KT)
        ln2g, ln2b = ring[:, 0, :], ring[:, 1, :]
        xg = [r_u[0:SLOTS, 0:D], r_u[0:SLOTS, D:2 * D]]
        yb = [r_pool[:, 0:1024], r_pool[:, 1024:2048]]
        sil = r_pool[0:SLOTS, 2048:2560]
        hid = r_pool[0:SLOTS, 2560:3072]
        hidT = r_pool[:, 3072:3072 + FT * SLOTS].rearrange("p (k t) -> p k t", k=FT)
        route = r_ssm
        xgT = [tmp[:].rearrange("p b t -> p (b t)")[:, 0:KT * SLOTS].rearrange("p (k t) -> p k t", k=KT),
               r_c[:, 0:KT * SLOTS].rearrange("p (k t) -> p k t", k=KT)]
        res = [r_x[:, 0:4096], r_x[:, 4096:8192], r_bm0[:, 0:4096], r_bm0[:, 4096:8192]]

        at = [0]

        def small(n, dt=F32):
            v = route[:, at[0]:at[0] + n]
            at[0] += n
            return v if dt is F32 else v.bitcast(dt)

        E1 = NG + NE
        lg = small(TT * E1).rearrange("p (i e) -> p i e", i=TT)
        gmax, gsum, pgrp, vmax = (small(TT) for _ in range(4))
        gd, ge, gv, gm = (small(TT * NG).rearrange("p (i e) -> p i e", i=TT) for _ in range(4))
        prod = small(TT * NE).rearrange("p (i g j) -> p i g j", i=TT, g=NG)
        prod2 = small(TT * NE).rearrange("p (i e) -> p i e", i=TT)
        sel = small(TT * EPG).rearrange("p (i j) -> p i j", i=TT)
        top = small(TT * 8).rearrange("p (i j) -> p i j", i=TT)
        topi = small(TT * 8, U32).rearrange("p (i j) -> p i j", i=TT)
        topf = small(TT * 8).rearrange("p (i j) -> p i j", i=TT)
        gap, egap, epl = small(TT), small(TT), small(TT)
        gate = small(2 * TT).rearrange("p (k i) -> p k i", k=2)
        eid = small(2 * TT).rearrange("p (k i) -> p k i", k=2)
        onek = small(2 * TT * NE).rearrange("p (k i e) -> p k i e", k=2, i=TT)
        one = small(TT * NE).rearrange("p (i e) -> p i e", i=TT)
        one_sum = small(NE)
        gbase = small(TT)
        rank_row = small(TT * NE).rearrange("p (i e) -> p i e", i=TT)
        pos = small(2 * TT).rearrange("p (k i) -> p k i", k=2)
        pos_i = small(2 * TT, I32).rearrange("p (k i) -> p k i", k=2)
        val_i = small(2 * TT, I32).rearrange("p (i k) -> p i k", k=2)
        iota_e = small(NE)
        iota_g = small(NG)
        tri = small(P)
        ones = small(P)
        cnt = small(NE)
        cnt_i = small(NE, I32)
        extra_flag = small(ROUNDS * NE)
        extra_scan = small(ROUNDS * NE)
        extra_no = small(ROUNDS * NE, I32)
        max_i = small(1, I32)
        max_f = small(1)
        slot_i = small(NE, I32)
        slot_g = small(NE, I32)
        slot_s = small(NE, I32)
        half = small(1)
        gidx, sidx = small(2, I32), small(2, I32)
        xslot, xgi, xsi = small(1, I32), small(1, I32), small(1, I32)
        stats = small(4 * 6).rearrange("p (q s) -> p q s", q=4)
        mv = small(2)
        lnt = small(8)
        empties = small(P, I32)
        assert at[0] <= 4096

        block = ctx.enter_context(nc.Block())

        def ring_view(b, k, n):
            return ring[:, b, 0:k * n].rearrange("p (k n) -> p k n", k=k)

        w_in_v = w_in.rearrange("(k p) c -> p k c", p=P)
        N_IN = KT
        N_WO = 2 * NN
        FIRST_WO = N_IN + 1
        FIRST_GLU = FIRST_WO + N_WO
        N_GLU = MT // 2
        FIRST_WO2 = FIRST_GLU + N_GLU
        END = FIRST_WO2 + N_WO

        def ring_source(n):
            b = n % 2
            if n == N_IN:
                return (ring[:, b, :].rearrange("p (q d) -> p q d", d=256),
                        pool_w.rearrange("g (k p) d -> p (g k) d", p=P))
            if FIRST_GLU <= n < FIRST_WO2:
                j = n - FIRST_GLU
                return ring_view(b, MT, 256), glu_w.rearrange("(k p) c -> p k c", p=P)[:, :, 256 * j:256 * j + 256]
            base, j = (0, n - FIRST_WO) if n < FIRST_GLU else (CH, n - FIRST_WO2)
            col, part = j // 2, j % 2
            rows = w_out[base + part * NCOL:base + (part + 1) * NCOL, NCOL * col:NCOL * col + NCOL]
            return ring_view(b, 4, NCOL), rows.rearrange("(k p) c -> p k c", p=P)

        def expert_quarter(m, e, c):
            w, t, k = ((w_gate, wg, KT), (w_up, wu, KT), (w_down, wd, FT))[m]
            q = k // WQ
            src = w[bass.ds(e, 1)].rearrange("o (p k) f -> p (o k) f", k=k)[:, c * q:(c + 1) * q, :]
            return t[:, c * q:(c + 1) * q, :], src

        ORDER = [(m, c) for c in range(WQ) for m in (0, 1)] + [(2, c) for c in range(WQ)]
        LOADED = (wg_loaded, wu_loaded, wd_loaded)

        @block.sync
        def _(sp):
            for i in range(TT):
                sp.dma_start(xrows[:, i, :], x[i * P:(i + 1) * P, :]).then_inc(x_loaded, 16)
            for b in range(2):
                sp.dma_start(ring_view(b, KT, P), w_in_v[:, :, b * P:(b + 1) * P]).then_inc(ring_loaded[b], 16)
            with sp.Fori(1, N_IN // 2) as i:
                for b in range(2):
                    sp.wait_ge(ring_used, 2 * i + (b - 1))
                    sp.dma_start(ring_view(b, KT, P), w_in_v[:, :, bass.ds(i * (2 * P) + b * P, P)]
                                 ).then_inc(ring_loaded[b], 16)
            expert = iter(ORDER)
            for n in range(N_IN, END):
                sp.wait_ge(ring_used, n - 1)
                dst, src = ring_source(n)
                sp.dma_start(dst, src).then_inc(ring_loaded[n % 2], 16)
                if n == FIRST_WO + 1:
                    sp.wait_ge(z_done, GP // 2)
                    sp.dma_start(h1[:, :, :], x.rearrange("(i p) d -> p i d", p=P)).then_inc(xr_loaded, 16)
                if n == FIRST_GLU + 1:
                    sp.wait_ge(y_done, 4)
                if n > FIRST_GLU + 1:
                    for _ in range(2 if n == END - 1 else 1):
                        if (mc := next(expert, None)) is not None:
                            dst, src = expert_quarter(mc[0], 0, mc[1])
                            sp.dma_start(dst, src).then_inc(LOADED[mc[0]][mc[1]], 16)
            for m, c in expert:
                dst, src = expert_quarter(m, 0, c)
                sp.dma_start(dst, src).then_inc(LOADED[m][c], 16)
            sp.wait_ge(ring_used, END)
            sp.dma_start(ln2g, ln2_g.partition_broadcast(P)).then_inc(ln2_loaded, 16)
            sp.dma_start(ln2b, ln2_b.partition_broadcast(P)).then_inc(ln2_loaded, 16)
            for i in range(TT):
                sp.wait_ge(h_ready, i + 1)
                sp.dma_start(h_dram[i * P:(i + 1) * P, :], h1[:, i, :]).then_inc(h_stored, 16)
            with sp.Fori(1, NE) as e:
                for j, (m, c) in enumerate(ORDER):
                    sp.wait_ge(w_used, e * 12 + (j + 1 - 12))
                    dst, src = expert_quarter(m, e, c)
                    sp.dma_start(dst, src).then_inc(LOADED[m][c], 16)
            sp.wait_ge(counts_ready, 1)
            sp.wait_ge(w_used, 12 * NE)
            with sp.If(sp.value_load(max_i[0:1, 0:1], min_val=0, max_val=S) > SLOTS):
                with sp.Fori(1, ROUNDS) as r:
                    with sp.Fori(0, NE) as e:
                        with sp.If(sp.value_load(cnt_i[0:1, bass.ds(e, 1)], min_val=0, max_val=S) > r * SLOTS):
                            no = sp.value_load(extra_no[0:1, bass.ds(r * NE + e, 1)], min_val=0, max_val=16)
                            sp.wait_ge(ye_stored, no * 16 + 16 * NE)
                            for h in range(2):
                                sp.dma_start(xslot[h * SLOTS:(h + 1) * SLOTS, :],
                                             slot_dram.rearrange("(r e) o -> r (e o)", e=NE)[
                                                 bass.ds(r * SLOTS, SLOTS), bass.ds(e, 1)],
                                             allow_slow_non_contiguous=True).then_inc(xs_loaded, 16)
                            for m in range(3):
                                w, t, k = ((w_gate, wg, KT), (w_up, wu, KT), (w_down, wd, FT))[m]
                                sp.dma_start(t, w[bass.ds(e, 1)].rearrange("o (p k) f -> p (o k) f", k=k)
                                             ).then_inc(xw_loaded, 16)
            n_extra = sp.value_load(extra_no[0:1, 0:1], min_val=0, max_val=16)
            sp.wait_ge(ye_stored, n_extra * 16 + 16 * NE)
            for i in range(TT):
                sp.dma_start(res[i].rearrange("p (k d) -> p k d", k=2),
                             ye_dram.rearrange("(i p k h) d -> i p k (h d)", i=TT, p=P, k=2)[i]
                             ).then_inc(res_loaded, 16)
            for i in range(TT):
                sp.wait_ge(out_ready, i + 1)
                sp.dma_start(out[i * P:(i + 1) * P, :], h1[:, i, :]).then_inc(out_stored, 16)
            sp.wait_ge(out_stored, 16 * TT)

        @block.gpsimd
        def _(pool):
            pool.memset(ident[:], 0.0).then_inc(ident_ready, 1)
            pool.wait_ge(ident_ready, 1)
            pool.affine_select(out=ident[:], in_=ident[:], compare_op=ALU.not_equal, fill=1.0, base=0,
                               pattern=[[-1, P]], channel_multiplier=1).then_inc(ident_ready, 1)
            for q, w in enumerate(WINDOWS):
                for j in range(w // 2):
                    pool.memset(edge[:, q, j:j + 1], w / (w // 2 + j))
                for j in range(1, w // 2):
                    at_col = w // 2 + (w // 2 - 1 - j)
                    pool.memset(edge[:, q, at_col:at_col + 1], w / (w // 2 + j))
            pool.memset(neg_one[:], -1.0).then_inc(edge_ready, 1)
            lags = lambda d: ksb[:, d].rearrange("p c q g -> p (c q g)")
            pool.wait_ge(lag_copied, 1)
            pool.dma_start(lag_dram[L * C:(2 * L - 1) * C, :], lags(0)[C:P, :]).then_inc(lag_stored, 16)
            pool.wait_ge(lag_copied, 2)
            pool.dma_start(lag_dram[0:L * C, :], lags(1)).then_inc(lag_stored, 16)
            pool.wait_ge(lag_stored, 32)
            pool.dma_start(lag_dram[(L - 1) * C:L * C, :], ksb[0:C, 0].rearrange("p c q g -> p (c q g)"),
                           accum_op=ALU.add).then_inc(lag_stored, 16)

            pool.wait_ge(glu_ready, MT)
            pool.memset(tri, 0.0)
            pool.memset(ones, 1.0)
            pool.iota(iota_e, [[1, NE]], base=0, channel_multiplier=0, allow_small_or_imprecise_dtypes=True)
            pool.iota(iota_g, [[-1, NG]], base=NG, channel_multiplier=0, allow_small_or_imprecise_dtypes=True)
            pool.iota(val_i, [[2 * P, TT], [1, 2]], base=0, channel_multiplier=2)
            pool.memset(half, 0.0)
            pool.memset(empties, EMPTY).then_inc(iota_ready, 1)
            pool.wait_ge(iota_ready, 1)
            pool.affine_select(out=tri, in_=tri, compare_op=ALU.is_ge, fill=1.0, base=0,
                               pattern=[[-1, P]], channel_multiplier=1)
            pool.affine_select(out=half, in_=half, compare_op=ALU.is_gt, fill=1.0, base=SLOTS,
                               pattern=[[0, 1]], channel_multiplier=-1).then_inc(iota_ready, 1)
            pool.dma_start(slot_dram.rearrange("(p n) o -> p (n o)", p=P), empties).then_inc(table_cleared, 16)
            pool.wait_ge(table_cleared, 16)
            pool.wait_ge(pos_ready, 1)
            pool.wait_ge(iota_ready, 2)
            for k in range(2):
                for i in range(TT):
                    pool.indirect_dma_start(
                        out=slot_dram, out_offset=bass.IndirectOffsetOnAxis(ap=pos_i[:, k, i:i + 1], axis=0),
                        in_=val_i[:, i, k:k + 1], in_offset=None).then_inc(table_written, 16)
            pool.wait_ge(table_written, 16 * 2 * TT)
            table = slot_dram.rearrange("(r e) o -> r (e o)", e=NE)
            for h in range(2):
                pool.dma_start(slot_i[h * SLOTS:(h + 1) * SLOTS, :], table[0:SLOTS, :]).then_inc(slots_loaded, 16)

            def copy_index(e, b):
                pool.tensor_copy(gidx[:, b:b + 1], slot_g[:, bass.ds(e, 1)])
                pool.tensor_copy(sidx[:, b:b + 1], slot_s[:, bass.ds(e, 1)]).then_inc(idx_ready, 1)

            def gather(b):
                pool.indirect_dma_start(
                    out=xg[b], out_offset=None, in_=h_dram,
                    in_offset=bass.IndirectOffsetOnAxis(ap=gidx[0:SLOTS, b:b + 1], axis=0),
                    bounds_check=S - 1, oob_is_err=False).then_inc(xg_loaded, 16)

            def scatter(b, ready, idx):
                pool.indirect_dma_start(
                    out=ye_dram, out_offset=bass.IndirectOffsetOnAxis(ap=idx, axis=0),
                    in_=yb[b], in_offset=None, bounds_check=4 * S - 1, oob_is_err=False).then_inc(ready, 16)

            pool.wait_ge(logit_done, 1)
            for b in range(2):
                last = pool.memset(xg[b], 0.0)
            last.then_inc(rows_cleared, 1)
            pool.wait_ge(rows_cleared, 1)
            pool.wait_ge(slots_ready, 1)
            pool.wait_ge(h_stored, 16 * TT)
            copy_index(0, 0)
            pool.wait_ge(idx_ready, 1)
            gather(0)

            def step(n, b, more, after):
                if more:
                    pool.wait_ge(xg_loaded, n * 16 + 16)
                    if after:
                        pool.wait_ge(xg_t, n)
                        pool.wait_ge(ye_stored, n * 16)
                    copy_index(n + 1, 1 - b)
                    pool.wait_ge(idx_ready, n + 2)
                    pool.nop().then_inc(pool_turn, 1)
                    gather(1 - b)
                pool.wait_ge(ye_act, n + 1)
                pool.wait_ge(ye_dve, n + 1)
                pool.nop().then_inc(pool_turn, 1)
                scatter(b, ye_stored, sidx[:, b:b + 1])

            step(0, 0, True, False)
            step(1, 1, True, True)
            with pool.Fori(1, NE // 2 - 1) as i:
                for b in range(2):
                    step(i * 2 + b, b, True, True)
            step(NE - 2, 0, True, True)
            step(NE - 1, 1, False, True)
            pool.wait_ge(ye_stored, 16 * NE)
            pool.wait_ge(counts_ready, 1)
            with pool.If(pool.value_load(max_i[0:1, 0:1], min_val=0, max_val=S) > SLOTS):
                with pool.Fori(1, ROUNDS) as r:
                    with pool.Fori(0, NE) as e:
                        with pool.If(pool.value_load(cnt_i[0:1, bass.ds(e, 1)], min_val=0, max_val=S) > r * SLOTS):
                            no = pool.value_load(extra_no[0:1, bass.ds(r * NE + e, 1)], min_val=0, max_val=16)
                            pool.wait_ge(xs_ready, no + 1)
                            pool.nop().then_inc(pool_turn, 1)
                            pool.indirect_dma_start(
                                out=xg[0], out_offset=None, in_=h_dram,
                                in_offset=bass.IndirectOffsetOnAxis(ap=xgi[0:SLOTS, :], axis=0),
                                bounds_check=S - 1, oob_is_err=False).then_inc(xg2_loaded, 16)
                            pool.wait_ge(xcopy, no * 5 + 5)
                            pool.nop().then_inc(pool_turn, 1)
                            scatter(0, ye_stored, xsi)

        @block.scalar
        def _(act):
            act.dma_start(pre[:, 0, :], a_re.rearrange("d (g q) n -> (d g) (q n)", q=2)).then_inc(par_loaded, 16)
            act.dma_start(pre[:, 1, :], a_im.rearrange("d (g q) n -> (d g) (q n)", q=2)).then_inc(par_loaded, 16)
            act.dma_start(pdt[:, 0:2], log_dt.rearrange("d (g q) -> (d g) q", q=2)).then_inc(par_loaded, 16)
            with nc.allow_non_contiguous_dma(reason="a few vectors, one value per partition"):
                for j, v in enumerate((pool_scale, ssm_d, glu_b)):
                    act.dma_start(vecs[:, j, :], v.rearrange("(m p) -> p m", p=P)).then_inc(vec_loaded, 16)
            for r, bsrc in enumerate((b_re, b_im)):
                for d in range(2):
                    act.dma_start(braw[:, r, d, :, :], bsrc[d].rearrange("(g q) n c -> (q n) g c", q=2)
                                  ).then_inc(b_loaded, 16)
            for r, csrc in enumerate((c_re, c_im)):
                for d in range(2):
                    for blk in range(4):
                        for q in range(2):
                            src = csrc[d].rearrange("(b g q) c n -> b q g c n", b=4, q=2)[blk, q]
                            act.dma_start(craw[:, r, d, blk, q * NST:(q + 1) * NST], src).then_inc(c_loaded, 16)
            act.wait_ge(par_loaded, 48)
            act.activation(pdt[:, 2:4], pdt[:, 0:2], ACT.Exp).then_inc(pre_act, 1)
            act.wait_ge(pre_dve, 1)
            act.activation(pre[:, 4, :], pre[:, 2, :], ACT.Exp).then_inc(pre_act, 1)
            act.wait_ge(pre_dve, 2)
            act.activation(pre[:, 5, :], pre[:, 3, :], ACT.Sin).then_inc(pre_act, 1)
            act.activation(pre[:, 6, :], pre[:, 7, :], ACT.Sin).then_inc(pre_act, 1)
            for kt in range(0, KT, 2):
                act.wait_ge(xt_done, kt + 1)
                act.copy(xT[:, kt, :], PS[:, kt % 4, :]).then_inc(xt_act, 1)
            for j, (r, d) in enumerate(((0, 0), (0, 1), (1, 0), (1, 1))):
                act.wait_ge(ct_done, j + 1)
                act.activation(FC[:, r, d, :, :].rearrange("p g c -> p (g c)"), PS[:, j, :], ACT.Copy,
                               scale=1.0 if r == 0 else -1.0).then_inc(fc_ready, 1)

            def b_matrices(d):
                for j in range(GP // 2):
                    act.wait_ge(btt_done, d * (GP // 2) + j + 1)
                    act.copy(BM[d][:, 2 * j:2 * j + 2, :, :].rearrange("p g r m -> p (g r m)"), PS[:, j % 4, :]
                             ).then_inc(bm_ready, 1)

            def ssm_tile(m, b):
                act.wait_ge(ring_used, MT + 1 + m)
                act.activation(uT[:, bass.ds(m, 1), :].rearrange("p o (s k) -> p (o s) k", s=L),
                               PS[:, 4 + b, :].rearrange("p (k s) -> p s k", s=L), ACT.Copy).then_inc(ssm_read, 1)
                act.wait_ge(ssm_read, m + 1)
                act.dma_start(u_dram[bass.ds(m * P, P), :, :].rearrange("p s k -> p (s k)"),
                              uT[:, bass.ds(m, 1), :].rearrange("p o t -> p (o t)")).then_inc(u_stored, 16)

            b_matrices(0)
            with act.Fori(0, 2) as i:
                for b in range(2):
                    ssm_tile(i * 2 + b, b)
            b_matrices(1)
            with act.Fori(2, 4) as i:
                for b in range(2):
                    ssm_tile(i * 2 + b, b)
            act.wait_ge(u_stored, 16 * MT)
            act.wait_ge(lag_stored, 48)
            for s in range(L):
                j = L - 1 - s
                act.dma_start(U[j * C:(j + 1) * C, :, :], u_dram.rearrange("(g c) s k -> s c g k", c=C)[s]
                              ).then_inc(u_loaded, 16)
            act.dma_start(r_t[:].rearrange("p (s n) -> p s n", s=L), bass.AP(tensor=lag_dram.tensor, offset=0,
                                               ap=[[G * C, P], [C * G * C, L], [1, G * C]])).then_inc(t_loaded, 16)
            for g in range(len(WINDOWS)):
                act.wait_ge(pmix_done, g + 1)
                if g == 0:
                    act.wait_ge(vec_loaded, 48)
                for h in range(PGT):
                    m = g * PGT + h
                    act.activation(pd[:, m, :], PS[:, 2 * (g % 2) + h, :], ACT.Copy,
                                   scale=vecs[:, 0, m:m + 1]).then_inc(pmix_ready, 1)
            for j in range(0, GP // 2, 2):
                act.wait_ge(z_done, j + 1)
                for d, order in ((0, 1), (1, -1)):
                    src = PS[:, 4 + j % 4, :].rearrange("p (g r d k) -> p d k r g", g=2, r=2, d=2)[:, d]
                    act.activation(st[:, ::order, :, d, 2 * j:2 * j + 2], src, ACT.Copy).then_inc(z_act, 1)
            for j in range(4):
                act.wait_ge(y_done, j + 1)
                for q in range(2):
                    act.activation(
                        U[:, 16 * j:16 * j + 16, :].rearrange("p (g q) k -> p q g k", q=2)[:, q],
                        PS[:, 4 + 2 * (j % 2) + q, :].rearrange("p (g k) -> p g k", k=NCH), ACT.Copy
                    ).then_inc(y_copied, 1)
                act.wait_ge(y_copied, 2 * j + 2)
                for t in range(L):
                    act.dma_start(y_dram[16 * j:16 * j + 16, :, t, :].rearrange("g c k -> c g k"),
                                  U[t * C:(t + 1) * C, 16 * j:16 * j + 16, :]).then_inc(y_stored, 16)
            act.wait_ge(y_stored, 16 * 4 * L)
            for m in range(MT):
                act.dma_start(Z[:, m, :], y_dram[m * L:(m + 1) * L].rearrange("g c s k -> (g c) (s k)")
                              ).then_inc(y_loaded, 16)
            act.wait_ge(ec_ready, 2)
            act.dma_start(ln1g, ln1_g.partition_broadcast(P)).then_inc(ln_loaded, 16)
            act.wait_ge(wo_done, NN)
            act.dma_start(ln1b, ln1_b.partition_broadcast(P)).then_inc(ln_loaded, 16)
            act.dma_start(rw[:, :, 0:NG], rg_w.rearrange("(k p) e -> p k e", p=P)).then_inc(ln_loaded, 16)
            act.dma_start(rw[:, :, NG:E1], re_w.rearrange("(k p) e -> p k e", p=P)).then_inc(ln_loaded, 16)
            act.dma_start(rbias[:, 0:NG], rg_b.partition_broadcast(P)).then_inc(ln_loaded, 16)
            act.dma_start(rbias[:, NG:E1], re_b.partition_broadcast(P)).then_inc(ln_loaded, 16)
            for m in range(MT):
                act.wait_ge(skip_done, m + 1)
                act.activation(uT[:, m, :], uT[:, m, :], ACT.Gelu_apprx_tanh).then_inc(gelu_ready, 1)
            for m in range(MT):
                act.wait_ge(glu_done, m + 1)
                if m >= 2:
                    act.wait_ge(glu_ready, m - 1)
                act.activation(tmp[:, m % 2, 0:S], PS[:, m % 2, :], ACT.Sigmoid, bias=vecs[:, 2, m:m + 1]
                               ).then_inc(sig_ready, 1)
            for i in range(TT):
                act.wait_ge(std_asked, i + 1)
                act.activation(lnt[:, 1:2], lnt[:, 0:1], ACT.Sqrt).then_inc(std_ready, 1)
            for i in range(TT):
                for j in range(0, 4, 2):
                    act.wait_ge(ht_done, 4 * i + j + 1)
                    act.copy(hT[:, i % 2, 4 * j:4 * j + 4, :].rearrange("p k t -> p (k t)"), PS[:, j, :]
                             ).then_inc(xt_act, 1)
            act.wait_ge(exp_asked, 1)
            act.activation(ge[:], gd[:], ACT.Exp).then_inc(exp_ready, 1)
            act.wait_ge(exp_asked, 2)
            act.activation(egap, gap, ACT.Exp).then_inc(exp_ready, 1)

            def rows_copied(n, b):
                act.wait_ge(xg_t, n + 1)
                act.copy(xgT[b][:, 0:8, :].rearrange("p k t -> p (k t)"), PS[:, 2, :]).then_inc(xgT_act, 1)

            def expert(n, b, after, last_pass=False):
                act.wait_ge(gu_done, n + 1)
                if after:
                    act.wait_ge(hid_ready, n)
                act.activation(sil, PS[0:SLOTS, b, :], ACT.Silu).then_inc(silu_ready, 1)
                if not last_pass:
                    rows_copied(n + 1, 1 - b)
                act.wait_ge(down_done, n + 1)
                if after == 2:
                    act.wait_ge(ye_stored, n * 16 - 16)
                act.copy(yb[b][:, 0:NCOL], PS[:, 5, :]).then_inc(ye_act, 1)

            rows_copied(0, 0)
            expert(0, 0, 0)
            expert(1, 1, 1)
            with act.Fori(1, NE // 2 - 1) as i:
                for b in range(2):
                    expert(i * 2 + b, b, 2)
            expert(NE - 2, 0, 2)
            expert(NE - 1, 1, 2, True)
            act.wait_ge(counts_ready, 1)
            with act.If(act.value_load(max_i[0:1, 0:1], min_val=0, max_val=S) > SLOTS):
                with act.Fori(1, ROUNDS) as r:
                    with act.Fori(0, NE) as e:
                        with act.If(act.value_load(cnt_i[0:1, bass.ds(e, 1)], min_val=0, max_val=S) > r * SLOTS):
                            no = act.value_load(extra_no[0:1, bass.ds(r * NE + e, 1)], min_val=0, max_val=16)
                            act.wait_ge(xpe, no * 4 + 2)
                            act.wait_ge(xcopy, no * 5 + 1)
                            act.activation(sil, PS[0:SLOTS, 0, :], ACT.Silu).then_inc(xcopy, 1)
            for i in range(TT):
                act.wait_ge(std_asked, TT + i + 1)
                act.activation(lnt[:, 1:2], lnt[:, 0:1], ACT.Sqrt).then_inc(std_ready, 1)

        @block.tensor
        def _(pe):
            pe.wait_ge(ident_ready, 2)
            pe.wait_ge(x_loaded, 64)
            for kt in range(KT):
                if kt >= 4:
                    pe.wait_ge((xt_act, xt_dve)[kt % 2], (kt - 4) // 2 + 1)
                for i in range(TT):
                    last = pe.transpose(PS[:, kt % 4, i * P:(i + 1) * P], xrows[:, i, kt * P:(kt + 1) * P], ident[:])
                last.then_inc(xt_done, 1)
            pe.wait_ge(xt_act, KT // 2)
            pe.wait_ge(xt_dve, KT // 2)

            def project(i, b):
                pe.wait_ge(ring_loaded[b], i * 16 + 16)
                for kt in range(KT):
                    last = pe.matmul(PS[:, 4 + b, :], ring_view(b, KT, P)[:, kt, :], xT[:, kt, :],
                                     start=kt == 0, stop=kt == KT - 1)
                last.then_inc(ring_used, 1)

            def b_side(d):
                pe.wait_ge(bt_ready, d + 1)
                pe.wait_ge(fc_ready, 4)
                for j in range(GP // 2):
                    if j >= 4 or d == 1:
                        pe.wait_ge(bm_ready, d * (GP // 2) + max(j - 4, -1) + 1)
                    for g in range(2):
                        for r in range(2):
                            last = pe.transpose(PS[:, j % 4, (2 * g + r) * P:(2 * g + r + 1) * P],
                                                BT[:, r, 2 * j + g, :, :].rearrange("p s c -> p (s c)"), ident[:])
                    last.then_inc(btt_done, 1)
                if d == 0:
                    pe.wait_ge(par_ready, 1)
                else:
                    pe.wait_ge(lag_copied, 1)
                for g in range(GP):
                    for r in range(2):
                        for q in range(2):
                            rows = slice(q * NST, (q + 1) * NST)
                            last = pe.matmul(PS[:, 6 + q, g * C:(g + 1) * C],
                                             BT[rows, r, g, :, :].rearrange("p s c -> p (s c)"),
                                             FC[rows, r, d, g, :], start=(g == 0 and r == 0),
                                             stop=(g == GP - 1 and r == 1), skip_group_check=True)
                last.then_inc(lag_done, 1)

            project(0, 0)
            project(0, 1)
            pe.wait_ge(pre_ready, 1)
            for j in range(4):
                last = pe.transpose(PS[:, 6, j * 64:(j + 1) * 64], pre[:, 10 + j, :], ident[0:2 * GP, 0:2 * GP])
            last.then_inc(par_t, 1)
            pe.wait_ge(c_loaded, 16 * 32)
            for j, (r, d) in enumerate(((0, 0), (0, 1), (1, 0), (1, 1))):
                for blk in range(4):
                    last = pe.transpose(PS[:, j, blk * P:(blk + 1) * P], craw[:, r, d, blk, :], ident[:])
                last.then_inc(ct_done, 1)
            with pe.Fori(1, 4) as i:
                for b in range(2):
                    pe.wait_ge(pool_read, i * 2 + (b - 1))
                    project(i, b)
            b_side(0)
            for b in range(2):
                pe.wait_ge(pool_read, MT - 1 + b)
                project(4, b)
            with pe.Fori(5, 6) as i:
                for b in range(2):
                    pe.wait_ge(ssm_read, i * 2 + (b - 1 - MT))
                    project(i, b)
            b_side(1)
            with pe.Fori(6, 8) as i:
                for b in range(2):
                    pe.wait_ge(ssm_read, i * 2 + (b - 1 - MT))
                    project(i, b)

            pe.wait_ge(ring_loaded[0], 16 * (N_IN // 2 + 1))
            pe.wait_ge(bm_ready, GP)
            pe.wait_ge(pool_read, MT)
            for g in range(len(WINDOWS)):
                if g >= 2:
                    pe.wait_ge(pmix_ready, 2 * (g - 1))
                for h in range(PGT):
                    for k in range(PGT):
                        last = pe.matmul(PS[:, 2 * (g % 2) + h, :],
                                         ring[:, 0, :].rearrange("p (q d) -> p q d", d=256)[:, 2 * g + k, h * P:(h + 1) * P],
                                         pd[:, 2 * g + k, :], start=k == 0, stop=k == 1)
                last.then_inc(pmix_done, 1)

            pe.wait_ge(u_loaded, 16 * L)
            pe.wait_ge(ssm_read, MT)
            pe.wait_ge(lag_copied, 2)
            for j in range(GP // 2):
                if j >= 4:
                    pe.wait_ge((z_act, z_dve)[j % 2], 2 * ((j - 4) // 2) + 2)
                for g in range(2):
                    for r in range(2):
                        for d in range(2):
                            for q in range(2):
                                gp = 2 * j + g
                                col = ((g * 2 + r) * 2 + d) * NCH
                                last = pe.matmul(PS[q * NST:(q + 1) * NST, 4 + j % 4, col:col + NCH],
                                                 BM[d][:, gp, r, q * NST:(q + 1) * NST], U[:, 2 * gp + q, :],
                                                 start=True, stop=True)
                last.then_inc(z_done, 1)

            def out_columns(n, first_slot, rhs_of, bank):
                for part in range(2):
                    slot = first_slot + 2 * n + part
                    pe.wait_ge(ring_loaded[slot % 2], 16 * (slot // 2 + 1))
                    for k in range(4):
                        for i in range(TT):
                            last = pe.matmul(PS[:, bank + i, :], rhs_of(4 * part + k, i),
                                             ring_view(slot % 2, 4, NCOL)[:, k, :],
                                             start=(part == 0 and k == 0), stop=(part == 1 and k == 3))
                    if part == 0:
                        last.then_inc(ring_used, 1)
                    else:
                        last.then_inc(wo_done, 1)

            def slot_read(count):
                pe.wait_ge(wo_done, count)
                pe.nop().then_inc(ring_used, 1)

            def out_pool(n, bank):
                out_columns(n, FIRST_WO, lambda k, i: pd[:, k, i * P:(i + 1) * P], bank)
                slot_read(n + 1)

            def outputs(j):
                bank = 4 + 2 * (j % 2)
                for g in range(8):
                    gp = 8 * j + g
                    for q in range(2):
                        pe.matmul(PS[:, bank + q, g * NCH:(g + 1) * NCH],
                                  TP[:, :, q, gp],
                                  U[:, 2 * gp + q, :], start=g == 0, stop=False, skip_group_check=True)
                for g in range(8):
                    gp = 8 * j + g
                    for r in range(2):
                        for q in range(2):
                            rows = slice(q * NST, (q + 1) * NST)
                            lhs = EC[rows, r, :, gp % (GP // 2), :, :].rearrange("p d s c -> p d (s c)")
                            pe.matmul(PS[:, bank + q, g * NCH + 1:(g + 1) * NCH], lhs[:, 0, :],
                                      st[rows, 0:NCH - 1, r, 0, gp], start=False, stop=False, skip_group_check=True)
                            last = pe.matmul(PS[:, bank + q, g * NCH:(g + 1) * NCH - 1], lhs[:, 1, :],
                                             st[rows, NCH - 2::-1, r, 1, gp], start=False,
                                             stop=(g == 7 and r == 1), skip_group_check=True)
                last.then_inc(y_done, 1)

            pe.wait_ge(pmix_ready, MT)
            pe.nop().then_inc(ring_used, 1)
            out_pool(0, 0)
            pe.wait_ge(z_act, GP // 2)
            pe.wait_ge(z_dve, GP // 2)
            out_pool(1, 4)
            pe.wait_ge(wo_read, TT)
            out_pool(2, 0)
            pe.wait_ge(wo_read, 2 * TT)
            pe.wait_ge(t_loaded, 16)
            pe.wait_ge(ec_ready, 1)
            pe.wait_ge(scan_ready, 1)
            outputs(0)
            outputs(1)
            pe.wait_ge(wo_read, 3 * TT)
            out_pool(3, 0)
            pe.wait_ge(ec_ready, 2)
            pe.wait_ge(y_copied, 2)
            outputs(2)
            pe.wait_ge(y_copied, 4)
            outputs(3)

            pe.wait_ge(gelu_ready, MT)
            pe.wait_ge(wo_read, NN * TT)
            for m in range(MT):
                slot = FIRST_GLU + m // 2
                pe.wait_ge(ring_loaded[slot % 2], 16 * (slot // 2 + 1))
                if m >= 2:
                    pe.wait_ge(sig_ready, m - 1)
                for k in range(MT):
                    last = pe.matmul(PS[:, m % 2, :], ring_view(slot % 2, MT, 256)[:, k, (m % 2) * P:(m % 2 + 1) * P],
                                     uT[:, k, :], start=k == 0, stop=k == MT - 1)
                last.then_inc(glu_done, 1)
                if m % 2 == 1:
                    pe.wait_ge(glu_done, m + 1)
                    pe.nop().then_inc(ring_used, 1)

            pe.wait_ge(glu_ready, MT)
            pe.wait_ge(y_copied, 8)
            for n in range(NN):
                bank = 4 - 4 * (n % 2)
                if n >= 2:
                    pe.wait_ge(wo_read, (NN + n - 1) * TT)
                out_columns(n, FIRST_WO2, lambda k, i: Z[:, k, i * P:(i + 1) * P], bank)
                slot_read(NN + n + 1)

            pe.wait_ge(wo_read, 2 * NN * TT)
            pe.wait_ge(ln_loaded, 96)
            for i in range(TT):
                pe.wait_ge(h_ready, i + 1)
                for j in range(4):
                    if i >= 1:
                        pe.wait_ge((xt_act, xt_dve)[j % 2], KT // 2 + 2 * (i - 1) + j // 2 + 1)
                    for k in range(4):
                        kt = 4 * j + k
                        last = pe.transpose(PS[:, j, k * P:(k + 1) * P], h1[:, i, kt * P:(kt + 1) * P], ident[:])
                    last.then_inc(ht_done, 1)
                pe.wait_ge(xt_act, KT // 2 + 2 * (i + 1))
                pe.wait_ge(xt_dve, KT // 2 + 2 * (i + 1))
                for kt in range(KT):
                    last = pe.matmul(PS[:, 4, i * E1:(i + 1) * E1], hT[:, i % 2, kt, :], rw[:, kt, :],
                                     start=kt == 0, stop=kt == KT - 1)
            last.then_inc(logit_done, 1)
            pe.wait_ge(onehot_ready, 1)
            pe.wait_ge(iota_ready, 2)
            for i in range(TT):
                for k in range(i):
                    pe.matmul(PS[:, 5, i * NE:(i + 1) * NE], ones, one[:, k, :], start=k == 0, stop=False)
                pe.matmul(PS[:, 5, i * NE:(i + 1) * NE], tri, one[:, i, :], start=i == 0, stop=True)
            for i in range(TT):
                last = pe.matmul(PS[:, 5, TT * NE:(TT + 1) * NE], ones, one[:, i, :], start=i == 0, stop=i == TT - 1)
            last.then_inc(rank_done, 1)

            def rows_T(n, b):
                pe.wait_ge(xg_loaded, n * 16 + 16)
                pe.nop().then_inc(pe_turn, 1)
                for kt in range(KT):
                    last = pe.transpose(PS[:, 2 + kt // 8, (kt % 8) * SLOTS:(kt % 8 + 1) * SLOTS],
                                        xg[b].rearrange("p (d k) -> p k d", k=KT)[:, kt, :],
                                        ident[0:SLOTS, 0:SLOTS])
                last.then_inc(xg_t, 1)

            def expert(n, b, last_pass):
                pe.wait_ge(xgT_act, n + 1)
                pe.wait_ge(xgT_dve, n + 1)
                for c in range(WQ):
                    pe.wait_ge(wg_loaded[c], n * 16 + 16)
                    pe.wait_ge(wu_loaded[c], n * 16 + 16)
                    for kt in range(4 * c, 4 * c + 4):
                        for m, w in enumerate((wg, wu)):
                            last = pe.matmul(PS[m * SLOTS:(m + 1) * SLOTS, b, :], xgT[b][:, kt, :], w[:, kt, :],
                                             start=kt == 0, stop=kt == KT - 1)
                            if kt % 4 == 3:
                                last.then_inc(w_used, 1)
                pe.wait_ge(w_used, n * 12 + 8)
                pe.nop().then_inc(gu_done, 1)
                if not last_pass:
                    rows_T(n + 1, 1 - b)
                pe.wait_ge(hid_ready, n + 1)
                pe.nop().then_inc(pe_turn, 1)
                for k in range(FT):
                    last = pe.transpose(PS[:, 4, k * SLOTS:(k + 1) * SLOTS],
                                        hid.rearrange("p (f k) -> p k f", k=FT)[:, k, :], ident[0:SLOTS, 0:SLOTS])
                last.then_inc(hid_t, 1)
                pe.wait_ge(hidT_ready, n + 1)
                return last

            def down(n, after):
                if after:
                    pe.wait_ge(ye_act, n)
                    pe.wait_ge(ye_dve, n)
                for k in range(FT):
                    pe.wait_ge(wd_loaded[k], n * 16 + 16)
                    for c in range(2):
                        for m in range(2):
                            last = pe.matmul(PS[m * SLOTS:(m + 1) * SLOTS, 5 + c, :], hidT[:, k, :],
                                             wd[:, k, (2 * m + c) * NCOL:(2 * m + c + 1) * NCOL],
                                             start=k == 0, stop=k == FT - 1)
                    last.then_inc(w_used, 1)
                pe.wait_ge(w_used, n * 12 + 12)
                pe.nop().then_inc(down_done, 1)

            pe.wait_ge(pos_ready, 1)
            rows_T(0, 0)
            expert(0, 0, False)
            down(0, False)
            expert(1, 1, False)
            down(1, True)
            with pe.Fori(1, NE // 2 - 1) as i:
                for b in range(2):
                    expert(i * 2 + b, b, False)
                    down(i * 2 + b, True)
            expert(NE - 2, 0, False)
            down(NE - 2, True)
            expert(NE - 1, 1, True)
            down(NE - 1, True)
            pe.wait_ge(counts_ready, 1)
            pe.wait_ge(ye_act, NE)
            pe.wait_ge(ye_dve, NE)
            with pe.If(pe.value_load(max_i[0:1, 0:1], min_val=0, max_val=S) > SLOTS):
                with pe.Fori(1, ROUNDS) as r:
                    with pe.Fori(0, NE) as e:
                        with pe.If(pe.value_load(cnt_i[0:1, bass.ds(e, 1)], min_val=0, max_val=S) > r * SLOTS):
                            no = pe.value_load(extra_no[0:1, bass.ds(r * NE + e, 1)], min_val=0, max_val=16)
                            pe.wait_ge(xg2_loaded, no * 16 + 16)
                            pe.nop().then_inc(pe_turn, 1)
                            for kt in range(KT):
                                last = pe.transpose(PS[:, 2 + kt // 8, (kt % 8) * SLOTS:(kt % 8 + 1) * SLOTS],
                                                    xg[0].rearrange("p (d k) -> p k d", k=KT)[:, kt, :],
                                                    ident[0:SLOTS, 0:SLOTS])
                            last.then_inc(xpe, 1)
                            pe.wait_ge(xcopy, no * 5 + 1)
                            pe.wait_ge(xw_loaded, no * 48 + 48)
                            for kt in range(KT):
                                for m, w in enumerate((wg, wu)):
                                    last = pe.matmul(PS[m * SLOTS:(m + 1) * SLOTS, 0, :], xgT[0][:, kt, :],
                                                     w[:, kt, :], start=kt == 0, stop=kt == KT - 1)
                            last.then_inc(xpe, 1)
                            pe.wait_ge(xcopy, no * 5 + 3)
                            pe.nop().then_inc(pe_turn, 1)
                            for k in range(FT):
                                last = pe.transpose(PS[:, 4, k * SLOTS:(k + 1) * SLOTS],
                                                    hid.rearrange("p (f k) -> p k f", k=FT)[:, k, :],
                                                    ident[0:SLOTS, 0:SLOTS])
                            last.then_inc(xpe, 1)
                            pe.wait_ge(xcopy, no * 5 + 4)
                            for k in range(FT):
                                for c in range(2):
                                    for m in range(2):
                                        last = pe.matmul(PS[m * SLOTS:(m + 1) * SLOTS, 5 + c, :], hidT[:, k, :],
                                                         wd[:, k, (2 * m + c) * NCOL:(2 * m + c + 1) * NCOL],
                                                         start=k == 0, stop=k == FT - 1)
                            last.then_inc(xpe, 1)

        @block.vector
        def _(dve):
            chain = [0]

            def link(ins):
                chain[0] += 1
                ins.then_inc(dve_chain, 1)
                dve.wait_ge(dve_chain, chain[0])

            def tt(o, a, b, op):
                return dve.tensor_tensor(o, a, b, op)

            def ts(o, a, s1, s2, op0, op1=ALU.bypass):
                return dve.tensor_scalar(o, a, s1, s2, op0, op1)

            lr, li, lrdt, sin_in = (pre[:, j, :] for j in range(4))
            mag, sin, cos, cos_in = (pre[:, j, :] for j in range(4, 8))
            t0, t1 = pre[:, 8, :], pre[:, 9, :]
            ar, ai, zr, zi = (pre[:, 10 + j, :] for j in range(4))
            dve.wait_ge(pre_act, 1)
            for q in range(2):
                n = slice(q * NST, (q + 1) * NST)
                ts(t0[:, n], li[:, n], pdt[:, 2 + q:3 + q], None, ALU.mult)
                last = ts(lrdt[:, n], lr[:, n], pdt[:, 2 + q:3 + q], None, ALU.mult)
            last.then_inc(pre_dve, 1)
            dve.wait_ge(pre_dve, 1)
            magic = 12582912.0
            link(ts(t1, t0, 1.0 / (2.0 * math.pi), magic, ALU.mult, ALU.add))
            link(ts(t1, t1, magic, None, ALU.subtract))
            c1 = 6.28125
            c2 = 8.0 * round((2.0 * math.pi - c1) * 2 ** 19 / 8.0) / 2 ** 19
            c3 = 2.0 * math.pi - c1 - c2
            for cc in (c1, c2, c3):
                link(dve.scalar_tensor_tensor(out=t0, in0=t1, scalar=-cc, in1=t0, op0=ALU.mult, op1=ALU.add))
            link(ts(sin_in, t0, 3.1415925, -3.1415925, ALU.min, ALU.max))
            link(ts(t1, sin_in, -1.0, None, ALU.mult))
            link(tt(t1, t1, sin_in, ALU.max))
            ts(cos_in, t1, -1.0, math.pi / 2.0, ALU.mult, ALU.add).then_inc(pre_dve, 1)
            link(tt(t0, lr, lr, ALU.mult))
            link(tt(t1, li, li, ALU.mult))
            link(tt(t0, t0, t1, ALU.add))
            link(dve.reciprocal(t0, t0))
            dve.wait_ge(pre_act, 4)
            link(tt(ar, mag, cos, ALU.mult))
            link(tt(ai, mag, sin, ALU.mult))
            link(ts(mag, ar, -1.0, None, ALU.add))
            tt(zr, mag, lr, ALU.mult)
            tt(t1, ai, li, ALU.mult)
            tt(zi, ai, lr, ALU.mult)
            link(tt(sin, mag, li, ALU.mult))
            tt(zr, zr, t1, ALU.add)
            link(tt(zi, zi, sin, ALU.subtract))
            tt(zr, zr, t0, ALU.mult)
            tt(zi, zi, t0, ALU.mult).then_inc(pre_ready, 1)
            for kt in range(1, KT, 2):
                dve.wait_ge(xt_done, kt + 1)
                dve.tensor_copy(xT[:, kt, :], PS[:, kt % 4, :]).then_inc(xt_dve, 1)

            wide = S + 2 * PAD
            tA, tB = tmp[:, 0, :], tmp[:, 1, :]

            def pool_tile(m):
                w = WINDOWS[m // PGT]
                bank = 4 + m % 2
                dve.wait_ge(ring_used, m + 1)
                dve.memset(tA[:, 0:PAD], 0.0)
                dve.memset(tA[:, PAD + S:wide], 0.0)
                link(dve.tensor_copy(tA[:, PAD:PAD + S], PS[:, bank, :]))
                src, dst, sh, lo, hi = tA, tB, None, 1, wide - 1
                span = 2
                while True:
                    back, ahead = (1, 0) if span == 2 else (span // 4, span // 4)
                    if span == w:
                        link(tt(pd[:, m, :], src[:, PAD - back:PAD - back + S],
                                src[:, PAD + ahead:PAD + ahead + S], ALU.add))
                        break
                    link(tt(dst[:, lo:hi], src[:, lo - back:hi - back], src[:, lo + ahead:hi + ahead], ALU.add))
                    src, dst = dst, src
                    lo, hi, span = lo + span // 2, hi - span // 2, 2 * span
                q = m // PGT
                tt(pd[:, m, 0:w // 2], pd[:, m, 0:w // 2], edge[:, q, 0:w // 2], ALU.mult).then_inc(dve_chain, 1)
                chain[0] += 1
                if w > 2:
                    tt(pd[:, m, S - w // 2 + 1:S], pd[:, m, S - w // 2 + 1:S], edge[:, q, w // 2:w - 1],
                       ALU.mult).then_inc(dve_chain, 1)
                    chain[0] += 1
                dve.wait_ge(dve_chain, chain[0])
                dve.scalar_tensor_tensor(out=pd[:, m, :], in0=pd[:, m, :], scalar=1.0 / w, in1=PS[:, bank, :],
                                         op0=ALU.mult, op1=ALU.subtract).then_inc(pool_read, 1)

            dve.wait_ge(edge_ready, 1)
            pool_tile(0)
            pool_tile(1)

            dve.wait_ge(par_t, 1)
            dve.tensor_copy(par[:].rearrange("p q d g -> p (q d g)"), PS[:, 6, 0:4 * 2 * GP]).then_inc(par_ready, 1)
            dve.wait_ge(par_ready, 1)
            dve.wait_ge(b_loaded, 64)
            shape = [P, 2 * GP, C]

            def per_pair(q):
                return par[:, q, :, :].rearrange("p d g -> p (d g)").unsqueeze(2).to_broadcast(shape)

            def flat(v, r):
                return v[:, r].rearrange("p d g c -> p (d g) c")

            w0 = pw[:, 0, 0, :].rearrange("p (a c) -> p a c", c=C)
            w1 = pw[:, 0, 1, :].rearrange("p (a c) -> p a c", c=C)
            w2 = pw[:, 1, 0, :].rearrange("p (a c) -> p a c", c=C)
            w3 = pw[:, 1, 1, :].rearrange("p (a c) -> p a c", c=C)
            for hf in range(2):
                sl = slice(hf * GP, (hf + 1) * GP)
                sh = [P, GP, C]
                z_r = par[:, 2, hf, :].unsqueeze(2).to_broadcast(sh)
                z_i = par[:, 3, hf, :].unsqueeze(2).to_broadcast(sh)
                br_, bi_ = braw[:, 0, hf], braw[:, 1, hf]
                tt(w0, br_, z_r, ALU.mult)
                tt(w1, bi_, z_i, ALU.mult)
                tt(w2, bi_, z_r, ALU.mult)
                link(tt(w3, br_, z_i, ALU.mult))
                tt(bbar[:, 0, hf], w0, w1, ALU.subtract)
                link(tt(bbar[:, 1, hf], w2, w3, ALU.add))

            def b_powers(d):
                sh4 = [P, 2, GP, C]
                a_r = par[:, 0, d, :].unsqueeze(1).unsqueeze(3).to_broadcast(sh4)
                a_i = par[:, 1, d, :].unsqueeze(1).unsqueeze(3).to_broadcast(sh4)
                T1 = pw[:, 0].rearrange("p r (g c) -> p r g c", c=C)
                T2 = pw[:, 1].rearrange("p r (g c) -> p r g c", c=C)
                slot = (lambda q: q) if d == 0 else (lambda q: L - 1 - q)
                link(dve.tensor_copy(BT[:, :, :, slot(0), :], bbar[:, :, d]))
                for q in range(1, L):
                    v = BT[:, :, :, slot(q - 1), :]
                    tt(T1, v, a_r, ALU.mult)
                    link(tt(T2, v, a_i, ALU.mult))
                    tt(BT[:, 0, :, slot(q), :], T1[:, 0], T2[:, 1], ALU.subtract)
                    last = tt(BT[:, 1, :, slot(q), :], T1[:, 1], T2[:, 0], ALU.add)
                    if q < L - 1:
                        link(last)
                last.then_inc(bt_ready, 1)

            b_powers(0)
            for m in range(2, MT):
                pool_tile(m)

            def lags_out(d):
                dve.wait_ge(lag_done, d + 1)
                for q in range(2):
                    last = dve.tensor_copy(ksb[:, d, :, q, :], PS[:, 6 + q, :].rearrange("p (g c) -> p c g", c=C))
                last.then_inc(lag_copied, 1)

            lags_out(0)
            dve.wait_ge(btt_done, GP // 2)
            b_powers(1)
            lags_out(1)

            pa = par[:].rearrange("p q d g -> p q (d g)")
            cr, ci = coef[:, 0, 0, :], coef[:, 0, 1, :]
            s0, s1 = tmp[:, 0, 0:2 * GP], tmp[:, 0, 2 * GP:4 * GP]
            s2 = tmp[:, 0, 4 * GP:6 * GP]
            pr, pi_ = tmp[:, 1, 0:2 * GP], tmp[:, 1, 2 * GP:4 * GP]
            dve.tensor_copy(pr, pa[:, 0, :])
            link(dve.tensor_copy(pi_, pa[:, 1, :]))
            for _ in range(int(math.log2(L))):
                tt(s0, pr, pr, ALU.mult)
                tt(s1, pi_, pi_, ALU.mult)
                link(tt(s2, pr, pi_, ALU.mult))
                tt(pr, s0, s1, ALU.subtract)
                link(ts(pi_, s2, 2.0, None, ALU.mult))
            dve.tensor_copy(coef[:, 0, 0, :], pr)
            dve.tensor_copy(coef[:, 0, 1, :], pr)
            dve.tensor_copy(coef[:, 1, 0, :], pi_)
            link(ts(coef[:, 1, 1, :], pi_, -1.0, None, ALU.mult))
            for j in range(1, GP // 2, 2):
                dve.wait_ge(z_done, j + 1)
                for d, order in ((0, 1), (1, -1)):
                    src = PS[:, 4 + j % 4, :].rearrange("p (g r d k) -> p d k r g", g=2, r=2, d=2)[:, d]
                    dve.tensor_copy(st[:, ::order, :, d, 2 * j:2 * j + 2], src).then_inc(z_dve, 1)
            dve.wait_ge(z_dve, GP // 2)
            dve.wait_ge(z_act, GP // 2)
            sT = tmp[:, 0, 0:8 * GP].rearrange("p (q r e) -> p q r e", q=2, r=2)
            sS = tmp[:, 1, 0:4 * GP].rearrange("p (r e) -> p r e", r=2)

            def scan(prev, cur, count):
                tt(sT, prev.unsqueeze(1).to_broadcast([P, 2, 2, 2 * GP]), coef[:], ALU.mult).then_inc(scan_step, 1)
                dve.wait_ge(scan_step, count + 1)
                tt(sS, sT[:, 0], sT[:, 1, ::-1, :], ALU.add).then_inc(scan_step, 1)
                dve.wait_ge(scan_step, count + 2)
                tt(cur, cur, sS, ALU.add).then_inc(scan_step, 1)
                dve.wait_ge(scan_step, count + 3)

            UN = 7
            with dve.Fori(0, (NCH - 1) // UN) as i:
                for j in range(UN):
                    prev = st_flat[:, bass.ds(i * UN + j, 1)].rearrange("p o r e -> p (o r) e")
                    cur = st_flat[:, bass.ds(i * UN + (j + 1), 1)].rearrange("p o r e -> p (o r) e")
                    scan(prev, cur, i * (3 * UN) + 3 * j)
            dve.memset(sS, 0.0).then_inc(scan_ready, 1)

            def add_out(n, count, bank, first):
                dve.wait_ge(wo_done, count)
                for i in range(TT):
                    cols = h1[:, i, n * NCOL:(n + 1) * NCOL]
                    if first:
                        dve.scalar_tensor_tensor(out=cols, in0=cols, scalar=ALPHA, in1=PS[:, bank + i, :],
                                                 op0=ALU.mult, op1=ALU.add).then_inc(wo_read, 1)
                    else:
                        tt(cols, cols, PS[:, bank + i, :], ALU.add).then_inc(wo_read, 1)

            def c_powers(half_no):
                gs = slice(half_no * (GP // 2), (half_no + 1) * (GP // 2))
                sh4 = [P, 2, GP // 2, C]
                T1 = tmp[:, 0, 0:512].rearrange("p (r g c) -> p r g c", r=2, c=C)
                T2 = tmp[:, 1, 0:512].rearrange("p (r g c) -> p r g c", r=2, c=C)
                for d in range(2):
                    a_r = par[:, 0, d, gs].unsqueeze(1).unsqueeze(3).to_broadcast(sh4)
                    a_i = par[:, 1, d, gs].unsqueeze(1).unsqueeze(3).to_broadcast(sh4)
                    slot = (lambda q: q - 1) if d == 0 else (lambda q: L - q)
                    for q in range(1, L + 1):
                        v = FC[:, :, d, gs, :] if q == 1 else EC[:, :, d, :, slot(q - 1), :]
                        tt(T1, v, a_r, ALU.mult)
                        link(tt(T2, v, a_i, ALU.mult))
                        tt(EC[:, 0, d, :, slot(q), :], T1[:, 0], T2[:, 1], ALU.add)
                        last = tt(EC[:, 1, d, :, slot(q), :], T1[:, 1], T2[:, 0], ALU.subtract)
                        if not (d == 1 and q == L):
                            link(last)
                last.then_inc(ec_ready, 1)

            dve.wait_ge(scan_ready, 1)
            dve.wait_ge(xr_loaded, 16)
            add_out(0, 1, 0, True)
            c_powers(0)
            add_out(1, 2, 4, True)
            add_out(2, 3, 0, True)
            dve.wait_ge(y_done, 2)
            dve.wait_ge(ec_ready, 1)
            c_powers(1)
            add_out(3, 4, 0, True)

            dve.wait_ge(vec_loaded, 48)
            dve.wait_ge(y_loaded, 16 * MT)
            for m in range(MT):
                dve.scalar_tensor_tensor(out=uT[:, m, :], in0=uT[:, m, :], scalar=vecs[:, 1, m:m + 1],
                                         in1=Z[:, m, :], op0=ALU.mult, op1=ALU.add).then_inc(skip_done, 1)
            for m in range(MT):
                dve.wait_ge(sig_ready, m + 1)
                tt(Z[:, m, :].rearrange("p (k s) -> p s k", s=L),
                   tmp[:, m % 2, 0:S].rearrange("p (s k) -> p s k", s=L),
                   uT[:, m, :].rearrange("p (s k) -> p s k", s=L), ALU.mult).then_inc(glu_ready, 1)
            for n in range(NN):
                add_out(n, NN + n + 1, 4 - 4 * (n % 2), False)

            def norm(i, gain, bias, asked):
                row = h1[:, i, :]
                for q in range(4):
                    last = dve.bn_stats(stats[:, q, :], row[:, q * NCOL:(q + 1) * NCOL])
                link(last)
                link(dve.bn_aggr(mv, stats[:]))
                ts(lnt[:, 0:1], mv[:, 1:2], EPS, None, ALU.add).then_inc(std_asked, 1)
                dve.wait_ge(std_ready, asked)
                link(dve.reciprocal(lnt[:, 2:3], lnt[:, 1:2]))
                link(tt(lnt[:, 3:4], lnt[:, 2:3], lnt[:, 2:3], ALU.mult))
                link(tt(lnt[:, 3:4], lnt[:, 3:4], lnt[:, 0:1], ALU.mult))
                link(ts(lnt[:, 3:4], lnt[:, 3:4], -0.5, 1.5, ALU.mult, ALU.add))
                link(tt(lnt[:, 2:3], lnt[:, 3:4], lnt[:, 2:3], ALU.mult))
                link(ts(row, row, mv[:, 0:1], lnt[:, 2:3], ALU.subtract, ALU.mult))
                link(tt(row, row, gain, ALU.mult))
                return tt(row, row, bias, ALU.add)

            dve.wait_ge(ln_loaded, 96)
            dve.wait_ge(wo_read, 2 * NN * TT)
            for i in range(TT):
                norm(i, ln1g, ln1b, i + 1).then_inc(h_ready, 1)
            for i in range(TT):
                for j in range(1, 4, 2):
                    dve.wait_ge(ht_done, 4 * i + j + 1)
                    dve.tensor_copy(hT[:, i % 2, 4 * j:4 * j + 4, :].rearrange("p k t -> p (k t)"), PS[:, j, :]
                                    ).then_inc(xt_dve, 1)

            dve.wait_ge(logit_done, 1)
            dve.wait_ge(iota_ready, 2)
            link(tt(lg, PS[:, 4, 0:TT * E1].rearrange("p (i e) -> p i e", i=TT),
                    rbias.unsqueeze(1).to_broadcast([P, TT, E1]), ALU.add))
            sg = [P, TT, NG]
            link(dve.tensor_reduce(gmax, lg[:, :, 0:NG], AX, ALU.max))
            tt(gd, lg[:, :, 0:NG], gmax.unsqueeze(2).to_broadcast(sg), ALU.subtract).then_inc(exp_asked, 1)
            dve.wait_ge(exp_asked, 1)
            link(ts(gv, gd, 0.0, None, ALU.is_equal))
            link(tt(gv, gv, iota_g.unsqueeze(1).to_broadcast(sg), ALU.mult))
            link(dve.tensor_reduce(vmax, gv, AX, ALU.max))
            link(tt(gm, gv, vmax.unsqueeze(2).to_broadcast(sg), ALU.is_equal))
            link(tt(prod, lg[:, :, NG:E1].rearrange("p i (g j) -> p i g j", g=NG),
                    gm.unsqueeze(3).to_broadcast([P, TT, NG, EPG]), ALU.mult))
            link(dve.tensor_reduce(sel, prod.rearrange("p i g j -> p i j g"), AX, ALU.add))
            for i in range(TT):
                last = dve.max(top[:, i, :], sel[:, i, :])
            link(last)
            for i in range(TT):
                last = dve.max_index(topi[:, i, :], top[:, i, :], sel[:, i, :])
            link(last)
            tt(gap, top[:, :, 1], top[:, :, 0], ALU.subtract).then_inc(exp_asked, 1)
            link(ts(gbase, vmax, -float(EPG), float(NG * EPG), ALU.mult, ALU.add))
            link(dve.tensor_copy(topf, topi))
            for k in range(2):
                last = tt(eid[:, k, :], topf[:, :, k], gbase, ALU.add)
            link(last)
            se = [P, TT, NE]
            ie = iota_e.unsqueeze(1).to_broadcast(se)
            for k in range(2):
                last = tt(onek[:, k], ie, eid[:, k, :].unsqueeze(2).to_broadcast(se), ALU.is_equal)
            link(last)
            tt(one, onek[:, 0], onek[:, 1], ALU.add).then_inc(onehot_ready, 1)
            dve.wait_ge(exp_ready, 2)
            link(dve.tensor_reduce(gsum, ge, AX, ALU.add))
            link(dve.reciprocal(pgrp, gsum))
            link(ts(epl, egap, 1.0, None, ALU.add))
            link(dve.reciprocal(epl, epl))
            link(tt(gate[:, 0, :], pgrp, epl, ALU.mult))
            link(tt(gate[:, 1, :], gate[:, 0, :], egap, ALU.mult))
            dve.wait_ge(rank_done, 1)
            link(ts(rank_row, PS[:, 5, 0:TT * NE].rearrange("p (i e) -> p i e", i=TT), float(NE), None, ALU.mult))
            link(tt(rank_row, rank_row, ie, ALU.add))
            for k in range(2):
                link(tt(prod2, rank_row, onek[:, k], ALU.mult))
                link(dve.tensor_reduce(pos[:, k, :], prod2, AX, ALU.add))
            dve.tensor_copy(pos_i, pos).then_inc(pos_ready, 1)
            link(dve.tensor_copy(cnt, PS[:, 5, TT * NE:(TT + 1) * NE]))
            dve.tensor_copy(cnt_i, cnt)
            link(dve.tensor_reduce(max_f, cnt, AX, ALU.max))
            dve.tensor_copy(max_i, max_f)
            dve.memset(extra_flag[:, 0:NE], 0.0)
            for r in range(1, ROUNDS):
                last = ts(extra_flag[:, r * NE:(r + 1) * NE], cnt, float(r * SLOTS), None, ALU.is_gt)
            link(last)
            link(dve.tensor_tensor_scan(extra_scan, ones[:, 0:1].to_broadcast([P, ROUNDS * NE]), extra_flag, 0.0,
                                        ALU.mult, ALU.add))
            link(tt(extra_flag, extra_scan, extra_flag, ALU.subtract))
            link(dve.tensor_copy(extra_flag[:, 0:1], extra_scan[:, ROUNDS * NE - 1:ROUNDS * NE]))
            dve.tensor_copy(extra_no, extra_flag).then_inc(counts_ready, 1)

            def slot_rows(value, rows, halves):
                dve.tensor_scalar(rows, value, 1, None, ALU.logical_shift_right)
                return ts(halves, value, 2.0, half[:, 0:1], ALU.mult, ALU.add)

            dve.wait_ge(slots_loaded, 32)
            slot_rows(slot_i, slot_g, slot_s).then_inc(slots_ready, 1)

            def rows_copied(n, b):
                dve.wait_ge(xg_t, n + 1)
                dve.tensor_copy(xgT[b][:, 8:16, :].rearrange("p k t -> p (k t)"), PS[:, 3, :]).then_inc(xgT_dve, 1)

            def expert(n, b, after, last_pass):
                dve.wait_ge(silu_ready, n + 1)
                tt(hid, sil, PS[SLOTS:P, b, :], ALU.mult).then_inc(hid_ready, 1)
                dve.wait_ge(hid_t, n + 1)
                dve.tensor_copy(hidT.rearrange("p k t -> p (k t)"), PS[:, 4, 0:FT * SLOTS]).then_inc(hidT_ready, 1)
                if not last_pass:
                    rows_copied(n + 1, 1 - b)
                dve.wait_ge(down_done, n + 1)
                if after:
                    dve.wait_ge(ye_stored, n * 16 - 16)
                dve.tensor_copy(yb[b][:, NCOL:2 * NCOL], PS[:, 6, :]).then_inc(ye_dve, 1)

            rows_copied(0, 0)
            expert(0, 0, False, False)
            expert(1, 1, False, False)
            with dve.Fori(1, NE // 2 - 1) as i:
                for b in range(2):
                    expert(i * 2 + b, b, True, False)
            expert(NE - 2, 0, True, False)
            expert(NE - 1, 1, True, True)
            dve.wait_ge(h_stored, 16 * TT)
            for i in range(TT):
                ts(h1[:, i, :], h1[:, i, :], ALPHA, None, ALU.mult).then_inc(h_scaled, 1)
            with dve.If(dve.value_load(max_i[0:1, 0:1], min_val=0, max_val=S) > SLOTS):
                with dve.Fori(1, ROUNDS) as r:
                    with dve.Fori(0, NE) as e:
                        with dve.If(dve.value_load(cnt_i[0:1, bass.ds(e, 1)], min_val=0, max_val=S) > r * SLOTS):
                            no = dve.value_load(extra_no[0:1, bass.ds(r * NE + e, 1)], min_val=0, max_val=16)
                            dve.wait_ge(xs_loaded, no * 32 + 32)
                            slot_rows(xslot, xgi, xsi).then_inc(xs_ready, 1)
                            dve.wait_ge(xpe, no * 4 + 1)
                            dve.tensor_copy(xgT[0].rearrange("p (a k) t -> p a (k t)", a=2), PS[:, 2:4, :]
                                            ).then_inc(xcopy, 1)
                            dve.wait_ge(xcopy, no * 5 + 2)
                            tt(hid, sil, PS[SLOTS:P, 0, :], ALU.mult).then_inc(xcopy, 1)
                            dve.wait_ge(xpe, no * 4 + 3)
                            dve.tensor_copy(hidT.rearrange("p k t -> p (k t)"), PS[:, 4, 0:FT * SLOTS]
                                            ).then_inc(xcopy, 1)
                            dve.wait_ge(xpe, no * 4 + 4)
                            dve.tensor_copy(yb[0].rearrange("p (a n) -> p a n", a=2), PS[:, 5:7, :]).then_inc(xcopy, 1)

            dve.wait_ge(h_scaled, TT)
            dve.wait_ge(ln2_loaded, 32)
            dve.wait_ge(res_loaded, 16 * TT)
            for i in range(TT):
                for k in range(2):
                    link(dve.scalar_tensor_tensor(out=h1[:, i, :], in0=res[i][:, k * D:(k + 1) * D],
                                                  scalar=gate[:, k, i:i + 1], in1=h1[:, i, :],
                                                  op0=ALU.mult, op1=ALU.add))
                norm(i, ln2g, ln2b, TT + i + 1).then_inc(out_ready, 1)


_INS = ["x", "w_in", "pool_w", "pool_scale", "ssm_a_re", "ssm_a_im", "ssm_log_dt", "ssm_b_re", "ssm_b_im",
        "ssm_c_re", "ssm_c_im", "ssm_d", "glu_w", "glu_b", "w_out", "ln1_g", "ln1_b", "router_g_w", "router_g_b",
        "router_e_w", "router_e_b", "w_gate", "w_up", "w_down", "ln2_g", "ln2_b"]


def kernel(**inputs):
    import numpy as np
    import concourse.bacc as bacc
    from concourse.bass_utils import run_bass_kernel_spmd

    nc = bacc.Bacc("TRN2", target_bir_lowering=False, num_devices=1)
    arrays, args = {}, []
    for name in _INS:
        a = np.ascontiguousarray(inputs[name])[0]
        arrays[f"in_{name}"] = a
        args.append(nc.dram_tensor(f"in_{name}", a.shape, mybir.dt.from_np(a.dtype), kind="ExternalInput").ap())
    args.append(nc.dram_tensor("out_h", (S, D), F32, kind="ExternalOutput").ap())
    build(nc, *args)
    r = run_bass_kernel_spmd(nc, [arrays], core_ids=[0])
    return r.results[0]["out_h"].reshape(1, S, D)
```

```python
import math
from contextlib import ExitStack

import concourse.bass as bass
from concourse import mybir

F32 = mybir.dt.float32
I32 = mybir.dt.int32
U32 = mybir.dt.uint32
ALU = mybir.AluOpType
ACT = mybir.ActivationFunctionType
AX = mybir.AxisListType.X

P = 128
S = 512
D = 2048
KT = D // P
TT = S // P
NCOL = 512
NN = D // NCOL
CH = D // 2
MT = CH // P
WINDOWS = (2, 4, 8, 16)
PGT = MT // len(WINDOWS)
G = 64
C = 16
NST = 64
GP = G // 2
L = P // C
NCH = S // L
NG = 4
EPG = 8
NE = NG * EPG
F = 512
FT = F // P
SLOTS = 64
ROUNDS = S // SLOTS
EMPTY = 2 * S
PAD = 8
ALPHA = 2.0 ** 0.25
EPS = 1e-5
WQ = 4
CHUNK = 2048


def build(nc, x, w_in, pool_w, pool_scale, a_re, a_im, log_dt, b_re, b_im, c_re, c_im, ssm_d, glu_w, glu_b,
          w_out, ln1_g, ln1_b, rg_w, rg_b, re_w, re_b, w_gate, w_up, w_down, ln2_g, ln2_b, out):
    u_dram = nc.dram_tensor("u_scratch", (CH, L, NCH), F32, kind="Internal").ap()
    y_dram = nc.dram_tensor("y_scratch", (G, C, L, NCH), F32, kind="Internal").ap()
    lag_dram = nc.dram_tensor("lag_scratch", ((2 * L - 1) * C, G * C), F32, kind="Internal").ap()
    h_dram = nc.dram_tensor("h_scratch", (S, D), F32, kind="Internal").ap()
    slot_dram = nc.dram_tensor("slot_scratch", (S * NE, 1), I32, kind="Internal").ap()
    ye_dram = nc.dram_tensor("ye_scratch", (4 * S, D // 2), F32, kind="Internal").ap()

    with ExitStack() as ctx:
        def sb(name, shape, dt=F32):
            return ctx.enter_context(nc.sbuf_tensor(name, shape, dt))

        def sem(name):
            return ctx.enter_context(nc.semaphore(name))

        PS = ctx.enter_context(nc.psum_tensor("PS", [P, 8, NCOL], F32))

        r_x = sb("r_x", [P, 8192])
        r_bm0 = sb("r_bm0", [P, 8192])
        r_bm1 = sb("r_bm1", [P, 8192])
        r_t = sb("r_t", [P, 8192])
        r_ssm = sb("r_ssm", [P, 4096])
        r_u = sb("r_u", [P, 4096])
        r_pool = sb("r_pool", [P, 4096])
        r_c = sb("r_c", [P, 2048])
        ring = sb("ring", [P, 2, CHUNK])
        tmp = sb("tmp", [P, 2, S + 2 * PAD])
        ident = sb("ident", [P, P])
        par = sb("par", [P, 4, 2, GP])
        coef = sb("coef", [P, 2, 2, 2 * GP])
        edge = sb("edge", [P, len(WINDOWS), 16])
        vecs = sb("vecs", [P, 3, MT])
        neg_one = sb("neg_one", [P, 1])

        xT = r_x[:].rearrange("p (k t) -> p k t", k=KT)
        xrows = r_bm0[:].rearrange("p (i d) -> p i d", i=TT)
        st = r_x[:].rearrange("p (t r d g) -> p t r d g", t=NCH, r=2, d=2)
        st_flat = r_x[:].rearrange("p (t r e) -> p t r e", t=NCH, r=2)
        BM = [b[:].rearrange("p (g r m) -> p g r m", g=GP, r=2) for b in (r_bm0, r_bm1)]
        BT = r_t[:].rearrange("p (r g s c) -> p r g s c", r=2, g=GP, s=L)
        TP = r_t[:].rearrange("p (s c q g) -> p (s c) q g", s=L, c=C, q=2)
        EC = r_bm0[:].rearrange("p (r d g s c) -> p r d g s c", r=2, d=2, g=GP // 2, s=L)
        h1 = r_bm1[:].rearrange("p (i d) -> p i d", i=TT)
        pw = r_bm1[:, 0:2048].rearrange("p (q r e) -> p q r e", q=2, r=2)
        craw = r_bm1[:, 4096:6144].rearrange("p (r d b n) -> p r d b n", r=2, d=2, b=4)
        braw = r_bm1[:, 2048:4096].rearrange("p (r d g c) -> p r d g c", r=2, d=2, g=GP)
        pre = r_bm1[0:2 * GP, 6144:6144 + 14 * P].rearrange("p (q n) -> p q n", q=14)
        pdt = r_bm1[0:2 * GP, 6144 + 14 * P:6144 + 14 * P + 4]
        bbar = r_u[:, 0:2048].rearrange("p (r d g c) -> p r d g c", r=2, d=2, g=GP)
        ksb = r_u[:, 2048:4096].rearrange("p (d c q g) -> p d c q g", d=2, c=C, q=2)
        uT = r_ssm[:].rearrange("p (m t) -> p m t", m=MT)
        U = r_u[:].rearrange("p (g k) -> p g k", g=G)
        Z = r_u[:].rearrange("p (m t) -> p m t", m=MT)
        pd = r_pool[:].rearrange("p (m t) -> p m t", m=MT)
        FB = r_ssm[:, 2048:4096].rearrange("p (r g q c) -> p r g q c", r=2, g=GP, q=2)
        FC = r_c[:].rearrange("p (r d g c) -> p r d g c", r=2, d=2, g=GP)

        ident_ready, edge_ready, ones_ready = sem("ident_ready"), sem("edge_ready"), sem("ones_ready")
        x_loaded = [sem(f"x_loaded{i}") for i in range(TT)]
        par_loaded, b_loaded, c_loaded = sem("par_loaded"), sem("b_loaded"), sem("c_loaded")
        vec_loaded = sem("vec_loaded")
        ring_loaded = [sem("ring_loaded0"), sem("ring_loaded1")]
        ring_used = sem("ring_used")
        xt_done = sem("xt_done")
        xt_act, xt_dve = sem("xt_act"), sem("xt_dve")
        pool_read = sem("pool_read")
        ssm_read = sem("ssm_read")
        u_stored, u_loaded = sem("u_stored"), sem("u_loaded")
        pre_act, pre_dve = sem("pre_act"), sem("pre_dve")
        pre_ready = sem("pre_ready")
        par_t, par_ready = sem("par_t"), sem("par_ready")
        ct_done, fc_ready, fb_clear, fb_ready = sem("ct_done"), sem("fc_ready"), sem("fb_clear"), sem("fb_ready")
        dve_chain = sem("dve_chain")
        bt_ready = sem("bt_ready")
        btt_done, bm_ready = sem("btt_done"), sem("bm_ready")
        lag_done, lag_copied = sem("lag_done"), sem("lag_copied")
        lag_stored, t_loaded = sem("lag_stored"), sem("t_loaded")
        pmix_done, pmix_ready = sem("pmix_done"), sem("pmix_ready")
        z_done, z_act, z_dve = sem("z_done"), sem("z_act"), sem("z_dve")
        scan_step, scan_ready = sem("scan_step"), sem("scan_ready")
        xr_loaded, w2_loaded, logit_read = sem("xr_loaded"), sem("w2_loaded"), sem("logit_read")
        wo_done, wo_read = sem("wo_done"), sem("wo_read")
        ec_ready = sem("ec_ready")
        y_done, y_copied, y_stored, y_loaded = sem("y_done"), sem("y_copied"), sem("y_stored"), sem("y_loaded")
        skip_done, gelu_ready = sem("skip_done"), sem("gelu_ready")
        glu_done, sig_ready, glu_ready = sem("glu_done"), sem("sig_ready"), sem("glu_ready")
        ln_loaded, ln2_loaded = sem("ln_loaded"), sem("ln2_loaded")
        std_asked, std_ready = sem("std_asked"), sem("std_ready")
        h_ready, h_stored = sem("h_ready"), sem("h_stored")
        ht_done, ht_ready = sem("ht_done"), sem("ht_ready")
        logit_done = sem("logit_done")
        exp_asked, exp_ready = sem("exp_asked"), sem("exp_ready")
        onehot_ready, rank_done, table_ready, table_done = (
            sem("onehot_ready"), sem("rank_done"), sem("table_ready"), sem("table_done"))
        iota_ready, table_cleared = sem("iota_ready"), sem("table_cleared")
        pos_ready, table_written, slots_ready = sem("pos_ready"), sem("table_written"), sem("slots_ready")
        counts_ready = sem("counts_ready")
        wg_loaded = [sem(f"wg_loaded{c}") for c in range(WQ)]
        wu_loaded = [sem(f"wu_loaded{c}") for c in range(WQ)]
        wd_loaded = [sem(f"wd_loaded{c}") for c in range(WQ)]
        w_used = sem("w_used")
        idx_ready, sidx_ready = sem("idx_ready"), sem("sidx_ready")
        rows_cleared = sem("rows_cleared")
        xg_loaded, xg_t, xgT_act, xgT_dve = sem("xg_loaded"), sem("xg_t"), sem("xgT_act"), sem("xgT_dve")
        gu_done, silu_ready, hid_ready = sem("gu_done"), sem("silu_ready"), sem("hid_ready")
        hid_t, hidT_ready = sem("hid_t"), sem("hidT_ready")
        down_done, ye_act, ye_dve, ye_stored = sem("down_done"), sem("ye_act"), sem("ye_dve"), sem("ye_stored")
        h_scaled, scale_ready, normed, gained = sem("h_scaled"), sem("scale_ready"), sem("normed"), sem("gained")
        pe_turn, pool_turn = sem("pe_turn"), sem("pool_turn")
        xs_loaded, xs_ready, xw_loaded, xg2_loaded = sem("xs_loaded"), sem("xs_ready"), sem("xw_loaded"), sem("xg2_loaded")
        xpe, xcopy = sem("xpe"), sem("xcopy")
        res_loaded = [sem(f"res_loaded{i}") for i in range(TT)]
        out_ready, out_stored = sem("out_ready"), sem("out_stored")

        w2 = [b[:].rearrange("p (k d) -> p k d", k=4) for b in (r_x, r_bm0)]
        wg = r_x[:].rearrange("p (k f) -> p k f", k=KT)
        wu = r_bm0[:].rearrange("p (k f) -> p k f", k=KT)
        wd = r_t[:].rearrange("p (k d) -> p k d", k=FT)
        ln1g = r_c[:]
        ln1b = r_pool[:, 0:2048]
        rw = r_pool[:, 2048:2048 + KT * (NG + NE)].rearrange("p (k e) -> p k e", k=KT)
        rbias = r_pool[:, 2700:2700 + NG + NE]
        hT = ring[:].rearrange("p b (k t) -> p b k t", k=KT)
        ln2g, ln2b = ring[:, 0, :], ring[:, 1, :]
        xg = [r_u[0:SLOTS, 0:D], r_u[0:SLOTS, D:2 * D]]
        yb = [r_pool[:, 0:1024], r_pool[:, 1024:2048]]
        sil = r_pool[0:SLOTS, 2048:2560]
        hid = r_pool[0:SLOTS, 2560:3072]
        hidT = r_pool[:, 3072:3072 + FT * SLOTS].rearrange("p (k t) -> p k t", k=FT)
        route = r_ssm
        xgT = [tmp[:].rearrange("p b t -> p (b t)")[:, 0:KT * SLOTS].rearrange("p (k t) -> p k t", k=KT),
               r_c[:, 0:KT * SLOTS].rearrange("p (k t) -> p k t", k=KT)]
        res = [r_x[:, 0:4096], r_x[:, 4096:8192], r_bm0[:, 0:4096], r_bm0[:, 4096:8192]]

        at = [0]

        def small(n, dt=F32):
            v = route[:, at[0]:at[0] + n]
            at[0] += n
            return v if dt is F32 else v.bitcast(dt)

        E1 = NG + NE
        lg = small(TT * E1).rearrange("p (i e) -> p i e", i=TT)
        gmax, gsum, pgrp, vmax = (small(TT) for _ in range(4))
        gd, ge, gv, gm = (small(TT * NG).rearrange("p (i e) -> p i e", i=TT) for _ in range(4))
        prod = small(TT * NE).rearrange("p (i g j) -> p i g j", i=TT, g=NG)
        prod2 = small(TT * NE).rearrange("p (i e) -> p i e", i=TT)
        sel = small(TT * EPG).rearrange("p (i j) -> p i j", i=TT)
        top = small(TT * 8).rearrange("p (i j) -> p i j", i=TT)
        topi = small(TT * 8, U32).rearrange("p (i j) -> p i j", i=TT)
        topf = small(TT * 8).rearrange("p (i j) -> p i j", i=TT)
        gap, egap, epl = small(TT), small(TT), small(TT)
        gate = small(2 * TT).rearrange("p (k i) -> p k i", k=2)
        eid = small(2 * TT).rearrange("p (k i) -> p k i", k=2)
        onek = small(2 * TT * NE).rearrange("p (k i e) -> p k i e", k=2, i=TT)
        one = small(TT * NE).rearrange("p (i e) -> p i e", i=TT)
        one_sum = small(NE)
        gbase = small(TT)
        rank_row = small(TT * NE).rearrange("p (i e) -> p i e", i=TT)
        pos = small(2 * TT).rearrange("p (k i) -> p k i", k=2)
        pos_i = small(2 * TT, I32).rearrange("p (k i) -> p k i", k=2)
        val_i = small(2 * TT, I32).rearrange("p (i k) -> p i k", k=2)
        val_f = small(2 * TT).rearrange("p (i k) -> p i k", k=2)
        iota_m = small(P)
        rank_k = small(2 * TT).rearrange("p (k i) -> p k i", k=2)
        rank_eq = small(2 * TT * P).rearrange("p (k i m) -> p k i m", k=2, i=TT)
        val_e = small(2 * TT * NE).rearrange("p (k i e) -> p k i e", k=2, i=TT)
        iota_e = small(NE)
        iota_g = small(NG)
        tri = small(P)
        ones = small(P)
        cnt = small(NE)
        cnt_i = small(NE, I32)
        extra_flag = small(ROUNDS * NE)
        extra_scan = small(ROUNDS * NE)
        extra_no = small(ROUNDS * NE, I32)
        max_i = small(1, I32)
        max_f = small(1)
        slot_i = small(NE, I32)
        slot_g = small(NE, I32)
        slot_s = small(NE, I32)
        half = small(1)
        gidx, sidx = small(2, I32), small(2, I32)
        xslot, xgi, xsi = small(1, I32), small(1, I32), small(1, I32)
        stats = small(4 * 6).rearrange("p (q s) -> p q s", q=4)
        lnt = small(8 * TT).rearrange("p (i s) -> p i s", i=TT)
        empties = small(P, I32)
        assert at[0] <= 4096

        block = ctx.enter_context(nc.Block())

        def ring_view(b, k, n):
            return ring[:, b, 0:k * n].rearrange("p (k n) -> p k n", k=k)

        w_in_v = w_in.rearrange("(k p) c -> p k c", p=P)
        N_IN = KT
        N_WO = 2 * NN
        FIRST_WO = N_IN + 1
        FIRST_GLU = FIRST_WO + N_WO
        N_GLU = MT // 2
        END = FIRST_GLU + N_GLU

        def ring_source(n):
            b = n % 2
            if n == N_IN:
                return (ring[:, b, :].rearrange("p (q d) -> p q d", d=256),
                        pool_w.rearrange("g (k p) d -> p (g k) d", p=P))
            if FIRST_GLU <= n:
                j = n - FIRST_GLU
                return ring_view(b, MT, 256), glu_w.rearrange("(k p) c -> p k c", p=P)[:, :, 256 * j:256 * j + 256]
            col, part = (n - FIRST_WO) // 2, (n - FIRST_WO) % 2
            rows = w_out[part * NCOL:(part + 1) * NCOL, NCOL * col:NCOL * col + NCOL]
            return ring_view(b, 4, NCOL), rows.rearrange("(k p) c -> p k c", p=P)

        def expert_quarter(m, e, c):
            w, t, k = ((w_gate, wg, KT), (w_up, wu, KT), (w_down, wd, FT))[m]
            q = k // WQ
            src = w[bass.ds(e, 1)].rearrange("o (p k) f -> p (o k) f", k=k)[:, c * q:(c + 1) * q, :]
            return t[:, c * q:(c + 1) * q, :], src

        ORDER = [(m, c) for c in range(WQ) for m in (0, 1)] + [(2, c) for c in range(WQ)]
        LOADED = (wg_loaded, wu_loaded, wd_loaded)

        @block.sync
        def _(sp):
            for i in range(TT):
                sp.dma_start(xrows[:, i, :], x[i * P:(i + 1) * P, :]).then_inc(x_loaded[i], 16)
            for b in range(2):
                sp.dma_start(ring_view(b, KT, P), w_in_v[:, :, b * P:(b + 1) * P]).then_inc(ring_loaded[b], 16)
            with sp.Fori(1, N_IN // 2) as i:
                for b in range(2):
                    sp.wait_ge(ring_used, 2 * i + (b - 1))
                    sp.dma_start(ring_view(b, KT, P), w_in_v[:, :, bass.ds(i * (2 * P) + b * P, P)]
                                 ).then_inc(ring_loaded[b], 16)
            for n in range(N_IN, END):
                sp.wait_ge(ring_used, n - 1)
                dst, src = ring_source(n)
                sp.dma_start(dst, src).then_inc(ring_loaded[n % 2], 16)
                if n == FIRST_WO + 1:
                    sp.wait_ge(z_done, GP // 2)
                    sp.dma_start(h1[:, :, :], x.rearrange("(i p) d -> p i d", p=P)).then_inc(xr_loaded, 16)
                if n == FIRST_GLU + 1:
                    sp.wait_ge(y_done, 4)
                if n >= FIRST_GLU + 1:
                    for k in range(4 * (n - FIRST_GLU - 1), min(4 * (n - FIRST_GLU), MT)):
                        sp.dma_start(w2[k // 4][:, k % 4, :], w_out[CH + k * P:CH + (k + 1) * P, :]
                                     ).then_inc(w2_loaded, 16)
            first = [(2, c) for c in range(WQ)] + [mc for mc in ORDER if mc[0] != 2]
            for j, (m, c) in enumerate(first):
                if j == WQ:
                    sp.wait_ge(wo_done, NN + TT)
                if j == 2 * WQ:
                    sp.wait_ge(h_ready, TT)
                    sp.dma_start(h_dram[(TT - 1) * P:TT * P, :], h1[:, TT - 1, :]).then_inc(h_stored, 16)
                dst, src = expert_quarter(m, 0, c)
                sp.dma_start(dst, src).then_inc(LOADED[m][c], 16)
            sp.wait_ge(logit_done, TT)
            sp.dma_start(ln2g, ln2_g.partition_broadcast(P)).then_inc(ln2_loaded, 16)
            sp.dma_start(ln2b, ln2_b.partition_broadcast(P)).then_inc(ln2_loaded, 16)
            with sp.Fori(1, NE) as e:
                for j, (m, c) in enumerate(ORDER):
                    sp.wait_ge(w_used, e * 12 + (j + 1 - 12))
                    dst, src = expert_quarter(m, e, c)
                    sp.dma_start(dst, src).then_inc(LOADED[m][c], 16)
            sp.wait_ge(counts_ready, 1)
            sp.wait_ge(w_used, 12 * NE)
            with sp.If(sp.value_load(max_i[0:1, 0:1], min_val=0, max_val=S) > SLOTS):
                sp.wait_ge(table_written, 16 * 2 * TT)
                with sp.Fori(1, ROUNDS) as r:
                    with sp.Fori(0, NE) as e:
                        with sp.If(sp.value_load(cnt_i[0:1, bass.ds(e, 1)], min_val=0, max_val=S) > r * SLOTS):
                            no = sp.value_load(extra_no[0:1, bass.ds(r * NE + e, 1)], min_val=0, max_val=16)
                            sp.wait_ge(ye_stored, no * 16 + 16 * NE)
                            for h in range(2):
                                sp.dma_start(xslot[h * SLOTS:(h + 1) * SLOTS, :],
                                             slot_dram.rearrange("(r e) o -> r (e o)", e=NE)[
                                                 bass.ds(r * SLOTS, SLOTS), bass.ds(e, 1)],
                                             allow_slow_non_contiguous=True).then_inc(xs_loaded, 16)
                            for m in range(3):
                                w, t, k = ((w_gate, wg, KT), (w_up, wu, KT), (w_down, wd, FT))[m]
                                sp.dma_start(t, w[bass.ds(e, 1)].rearrange("o (p k) f -> p (o k) f", k=k)
                                             ).then_inc(xw_loaded, 16)
            n_extra = sp.value_load(extra_no[0:1, 0:1], min_val=0, max_val=16)
            sp.wait_ge(ye_stored, n_extra * 16 + 16 * NE)
            for i in range(TT):
                sp.dma_start(res[i].rearrange("p (k d) -> p k d", k=2),
                             ye_dram.rearrange("(i p k h) d -> i p k (h d)", i=TT, p=P, k=2)[i]
                             ).then_inc(res_loaded[i], 16)
            for i in range(TT):
                sp.wait_ge(out_ready, i + 1)
                sp.dma_start(out[i * P:(i + 1) * P, :], h1[:, i, :]).then_inc(out_stored, 16)
            sp.wait_ge(out_stored, 16 * TT)

        @block.gpsimd
        def _(pool):
            pool.memset(ident[:], 0.0).then_inc(ident_ready, 1)
            pool.wait_ge(ident_ready, 1)
            pool.affine_select(out=ident[:], in_=ident[:], compare_op=ALU.not_equal, fill=1.0, base=0,
                               pattern=[[-1, P]], channel_multiplier=1).then_inc(ident_ready, 1)
            for q, w in enumerate(WINDOWS):
                for j in range(w // 2):
                    pool.memset(edge[:, q, j:j + 1], w / (w // 2 + j))
                for j in range(1, w // 2):
                    at_col = w // 2 + (w // 2 - 1 - j)
                    pool.memset(edge[:, q, at_col:at_col + 1], w / (w // 2 + j))
            pool.memset(neg_one[:], -1.0).then_inc(edge_ready, 1)
            lags = lambda d: ksb[:, d].rearrange("p c q g -> p (c q g)")
            pool.wait_ge(lag_copied, 1)
            pool.dma_start(lag_dram[L * C:(2 * L - 1) * C, :], lags(0)[C:P, :]).then_inc(lag_stored, 16)
            pool.wait_ge(lag_copied, 2)
            pool.dma_start(lag_dram[0:L * C, :], lags(1)).then_inc(lag_stored, 16)
            pool.wait_ge(lag_stored, 32)
            pool.dma_start(lag_dram[(L - 1) * C:L * C, :], ksb[0:C, 0].rearrange("p c q g -> p (c q g)"),
                           accum_op=ALU.add).then_inc(lag_stored, 16)

            pool.wait_ge(glu_ready, MT)
            pool.memset(tri, 0.0)
            pool.memset(ones, 1.0)
            pool.iota(iota_e, [[1, NE]], base=0, channel_multiplier=0, allow_small_or_imprecise_dtypes=True)
            pool.iota(iota_g, [[-1, NG]], base=NG, channel_multiplier=0, allow_small_or_imprecise_dtypes=True)
            pool.iota(val_i, [[2 * P, TT], [1, 2]], base=0, channel_multiplier=2)
            pool.iota(val_f, [[2 * P, TT], [1, 2]], base=-EMPTY, channel_multiplier=2,
                      allow_small_or_imprecise_dtypes=True)
            pool.iota(iota_m, [[0, 2], [1, SLOTS]], base=0, channel_multiplier=0, allow_small_or_imprecise_dtypes=True)
            pool.memset(half, 0.0)
            pool.memset(empties, EMPTY).then_inc(iota_ready, 1)
            pool.wait_ge(iota_ready, 1)
            pool.affine_select(out=tri, in_=tri, compare_op=ALU.is_ge, fill=1.0, base=0,
                               pattern=[[-1, P]], channel_multiplier=1)
            pool.affine_select(out=half, in_=half, compare_op=ALU.is_gt, fill=1.0, base=SLOTS,
                               pattern=[[0, 1]], channel_multiplier=-1).then_inc(iota_ready, 1)
            def gather(b):
                pool.indirect_dma_start(
                    out=xg[b], out_offset=None, in_=h_dram,
                    in_offset=bass.IndirectOffsetOnAxis(ap=gidx[0:SLOTS, b:b + 1], axis=0),
                    bounds_check=S - 1, oob_is_err=False).then_inc(xg_loaded, 16)

            def scatter(b, ready, idx):
                pool.indirect_dma_start(
                    out=ye_dram, out_offset=bass.IndirectOffsetOnAxis(ap=idx, axis=0),
                    in_=yb[b], in_offset=None, bounds_check=4 * S - 1, oob_is_err=False).then_inc(ready, 16)

            pool.wait_ge(wo_done, NN + TT)
            for b in range(2):
                last = pool.memset(xg[b], 0.0)
            last.then_inc(rows_cleared, 1)
            pool.wait_ge(rows_cleared, 1)
            pool.wait_ge(slots_ready, 1)
            pool.wait_ge(h_stored, 16 * TT)

            def next_rows(n, b):
                pool.tensor_copy(gidx[:, b:b + 1], slot_g[:, bass.ds(n, 1)]).then_inc(idx_ready, 1)
                pool.wait_ge(idx_ready, n + 1)
                pool.nop().then_inc(pool_turn, 1)
                gather(b)

            def results(n, b, after):
                if after:
                    pool.wait_ge(ye_stored, n * 16)
                pool.tensor_copy(sidx[:, b:b + 1], slot_s[:, bass.ds(n, 1)]).then_inc(sidx_ready, 1)
                pool.wait_ge(sidx_ready, n + 1)
                pool.wait_ge(ye_act, n + 1)
                pool.wait_ge(ye_dve, n + 1)
                pool.nop().then_inc(pool_turn, 1)
                scatter(b, ye_stored, sidx[:, b:b + 1])

            next_rows(0, 0)
            pool.wait_ge(xg_loaded, 16)
            next_rows(1, 1)

            def step(n, b, more, after):
                if more:
                    pool.wait_ge(xg_loaded, n * 16 + 32)
                    pool.wait_ge(xg_t, n + 1)
                    next_rows(n + 2, b)
                results(n, b, after)

            step(0, 0, True, False)
            step(1, 1, True, True)
            with pool.Fori(1, NE // 2 - 1) as i:
                for b in range(2):
                    step(i * 2 + b, b, True, True)
            step(NE - 2, 0, False, True)
            step(NE - 1, 1, False, True)
            pool.wait_ge(ye_stored, 16 * NE)
            pool.wait_ge(counts_ready, 1)
            with pool.If(pool.value_load(max_i[0:1, 0:1], min_val=0, max_val=S) > SLOTS):
                pool.dma_start(slot_dram.rearrange("(p n) o -> p (n o)", p=P), empties).then_inc(table_cleared, 16)
                pool.wait_ge(table_cleared, 16)
                pool.wait_ge(pos_ready, 1)
                for k in range(2):
                    for i in range(TT):
                        pool.indirect_dma_start(
                            out=slot_dram, out_offset=bass.IndirectOffsetOnAxis(ap=pos_i[:, k, i:i + 1], axis=0),
                            in_=val_i[:, i, k:k + 1], in_offset=None).then_inc(table_written, 16)
                with pool.Fori(1, ROUNDS) as r:
                    with pool.Fori(0, NE) as e:
                        with pool.If(pool.value_load(cnt_i[0:1, bass.ds(e, 1)], min_val=0, max_val=S) > r * SLOTS):
                            no = pool.value_load(extra_no[0:1, bass.ds(r * NE + e, 1)], min_val=0, max_val=16)
                            pool.wait_ge(xs_ready, no + 1)
                            pool.nop().then_inc(pool_turn, 1)
                            pool.indirect_dma_start(
                                out=xg[0], out_offset=None, in_=h_dram,
                                in_offset=bass.IndirectOffsetOnAxis(ap=xgi[0:SLOTS, :], axis=0),
                                bounds_check=S - 1, oob_is_err=False).then_inc(xg2_loaded, 16)
                            pool.wait_ge(xcopy, no * 5 + 5)
                            pool.nop().then_inc(pool_turn, 1)
                            scatter(0, ye_stored, xsi)

            pool.wait_ge(ln2_loaded, 32)
            for i in range(TT):
                pool.wait_ge(gained, i + 1)
                pool.tensor_tensor(h1[:, i, :], h1[:, i, :], ln2b, ALU.add).then_inc(out_ready, 1)

        @block.scalar
        def _(act):
            act.dma_start(pre[:, 0, :], a_re.rearrange("d (g q) n -> (d g) (q n)", q=2)).then_inc(par_loaded, 16)
            act.dma_start(pre[:, 1, :], a_im.rearrange("d (g q) n -> (d g) (q n)", q=2)).then_inc(par_loaded, 16)
            act.dma_start(pdt[:, 0:2], log_dt.rearrange("d (g q) -> (d g) q", q=2)).then_inc(par_loaded, 16)
            with nc.allow_non_contiguous_dma(reason="a few vectors, one value per partition"):
                for j, v in enumerate((pool_scale, ssm_d, glu_b)):
                    act.dma_start(vecs[:, j, :], v.rearrange("(m p) -> p m", p=P)).then_inc(vec_loaded, 16)
            for r, bsrc in enumerate((b_re, b_im)):
                for d in range(2):
                    act.dma_start(braw[:, r, d, :, :], bsrc[d].rearrange("(g q) n c -> (q n) g c", q=2)
                                  ).then_inc(b_loaded, 16)
            act.wait_ge(par_loaded, 48)
            act.activation(pdt[:, 2:4], pdt[:, 0:2], ACT.Exp).then_inc(pre_act, 1)
            act.wait_ge(pre_dve, 1)
            act.activation(pre[:, 4, :], pre[:, 2, :], ACT.Exp).then_inc(pre_act, 1)
            act.wait_ge(pre_dve, 2)
            act.activation(pre[:, 5, :], pre[:, 3, :], ACT.Sin).then_inc(pre_act, 1)
            act.activation(pre[:, 6, :], pre[:, 7, :], ACT.Sin).then_inc(pre_act, 1)
            for i in range(TT):
                for j in range(0, 4, 2):
                    act.wait_ge(xt_done, 4 * i + j + 1)
                    act.copy(xT[:, 4 * j:4 * j + 4, i * P:(i + 1) * P],
                             PS[:, j, :].rearrange("p (k t) -> p k t", k=4)).then_inc(xt_act, 1)
            for r, csrc in enumerate((c_re, c_im)):
                for d in range(2):
                    for blk in range(4):
                        for q in range(2):
                            src = csrc[d].rearrange("(b g q) c n -> b q g c n", b=4, q=2)[blk, q]
                            act.dma_start(craw[:, r, d, blk, q * NST:(q + 1) * NST], src).then_inc(c_loaded, 16)
            for j, (r, d) in enumerate(((0, 0), (0, 1), (1, 0), (1, 1))):
                act.wait_ge(ct_done, j + 1)
                act.activation(FC[:, r, d, :, :].rearrange("p g c -> p (g c)"), PS[:, j, :], ACT.Copy,
                               scale=1.0 if r == 0 else -1.0).then_inc(fc_ready, 1)

            def b_matrices(d):
                for j in range(GP // 2):
                    act.wait_ge(btt_done, d * (GP // 2) + j + 1)
                    act.copy(BM[d][:, 2 * j:2 * j + 2, :, :].rearrange("p g r m -> p (g r m)"), PS[:, j % 4, :]
                             ).then_inc(bm_ready, 1)

            def ssm_tile(m, b):
                act.wait_ge(ring_used, MT + 1 + m)
                act.activation(uT[:, bass.ds(m, 1), :].rearrange("p o (s k) -> p (o s) k", s=L),
                               PS[:, 4 + b, :].rearrange("p (k s) -> p s k", s=L), ACT.Copy).then_inc(ssm_read, 1)
                act.wait_ge(ssm_read, m + 1)
                act.dma_start(u_dram[bass.ds(m * P, P), :, :].rearrange("p s k -> p (s k)"),
                              uT[:, bass.ds(m, 1), :].rearrange("p o t -> p (o t)")).then_inc(u_stored, 16)

            b_matrices(0)
            with act.Fori(0, 2) as i:
                for b in range(2):
                    ssm_tile(i * 2 + b, b)
            b_matrices(1)
            with act.Fori(2, 4) as i:
                for b in range(2):
                    ssm_tile(i * 2 + b, b)
            act.wait_ge(u_stored, 16 * MT)
            act.wait_ge(lag_stored, 48)
            for s in range(L):
                j = L - 1 - s
                act.dma_start(U[j * C:(j + 1) * C, :, :], u_dram.rearrange("(g c) s k -> s c g k", c=C)[s]
                              ).then_inc(u_loaded, 16)
            act.dma_start(r_t[:].rearrange("p (s n) -> p s n", s=L), bass.AP(tensor=lag_dram.tensor, offset=0,
                                               ap=[[G * C, P], [C * G * C, L], [1, G * C]])).then_inc(t_loaded, 16)
            for g in range(len(WINDOWS)):
                act.wait_ge(pmix_done, g + 1)
                if g == 0:
                    act.wait_ge(vec_loaded, 48)
                for h in range(PGT):
                    m = g * PGT + h
                    act.activation(pd[:, m, :], PS[:, 2 * (g % 2) + h, :], ACT.Copy,
                                   scale=vecs[:, 0, m:m + 1]).then_inc(pmix_ready, 1)
            for j in range(0, GP // 2, 2):
                act.wait_ge(z_done, j + 1)
                for d, order in ((0, 1), (1, -1)):
                    src = PS[:, 4 + j % 4, :].rearrange("p (g r d k) -> p d k r g", g=2, r=2, d=2)[:, d]
                    act.activation(st[:, ::order, :, d, 2 * j:2 * j + 2], src, ACT.Copy).then_inc(z_act, 1)
            for j in range(4):
                act.wait_ge(y_done, j + 1)
                for q in range(2):
                    act.activation(
                        U[:, 16 * j:16 * j + 16, :].rearrange("p (g q) k -> p q g k", q=2)[:, q],
                        PS[:, 4 + 2 * (j % 2) + q, :].rearrange("p (g k) -> p g k", k=NCH), ACT.Copy
                    ).then_inc(y_copied, 1)
                act.wait_ge(y_copied, 2 * j + 2)
                for t in range(L):
                    act.dma_start(y_dram[16 * j:16 * j + 16, :, t, :].rearrange("g c k -> c g k"),
                                  U[t * C:(t + 1) * C, 16 * j:16 * j + 16, :]).then_inc(y_stored, 16)
            act.wait_ge(y_stored, 16 * 4 * L)
            for m in range(MT):
                act.dma_start(Z[:, m, :], y_dram[m * L:(m + 1) * L].rearrange("g c s k -> (g c) (s k)")
                              ).then_inc(y_loaded, 16)
            act.wait_ge(ec_ready, 2)
            act.dma_start(ln1g, ln1_g.partition_broadcast(P)).then_inc(ln_loaded, 16)
            act.wait_ge(wo_done, NN)
            act.dma_start(ln1b, ln1_b.partition_broadcast(P)).then_inc(ln_loaded, 16)
            act.dma_start(rw[:, :, 0:NG], rg_w.rearrange("(k p) e -> p k e", p=P)).then_inc(ln_loaded, 16)
            act.dma_start(rw[:, :, NG:E1], re_w.rearrange("(k p) e -> p k e", p=P)).then_inc(ln_loaded, 16)
            act.dma_start(rbias[:, 0:NG], rg_b.partition_broadcast(P)).then_inc(ln_loaded, 16)
            act.dma_start(rbias[:, NG:E1], re_b.partition_broadcast(P)).then_inc(ln_loaded, 16)
            for m in range(MT):
                act.wait_ge(skip_done, m + 1)
                act.activation(uT[:, m, :], uT[:, m, :], ACT.Gelu_apprx_tanh).then_inc(gelu_ready, 1)
            for m in range(MT):
                act.wait_ge(glu_done, m + 1)
                if m >= 2:
                    act.wait_ge(glu_ready, m - 1)
                act.activation(tmp[:, m % 2, 0:S], PS[:, m % 2, :], ACT.Sigmoid, bias=vecs[:, 2, m:m + 1]
                               ).then_inc(sig_ready, 1)
            for i in range(TT):
                act.wait_ge(std_asked, i + 1)
                act.activation(lnt[:, 0, 1:2], lnt[:, 0, 0:1], ACT.Sqrt).then_inc(std_ready, 1)
                if i < TT - 1:
                    act.wait_ge(h_ready, i + 1)
                    act.dma_start(h_dram[i * P:(i + 1) * P, :], h1[:, i, :]).then_inc(h_stored, 16)
                for q in ([i - 1] if 1 <= i < TT - 1 else [TT - 2, TT - 1] if i == TT - 1 else []):
                    for j in range(0, 4, 2):
                        act.wait_ge(ht_done, 4 * q + j + 1)
                        act.copy(hT[:, q % 2, 4 * j:4 * j + 4, :].rearrange("p k t -> p (k t)"),
                                 PS[:, 4 - 4 * (q % 2) + j, :]).then_inc(xt_act, 1)
            act.wait_ge(exp_asked, 1)
            act.activation(ge[:], gd[:], ACT.Exp).then_inc(exp_ready, 1)
            act.wait_ge(exp_asked, 2)
            act.activation(egap, gap, ACT.Exp).then_inc(exp_ready, 1)

            def rows_copied(n, b):
                act.wait_ge(xg_t, n + 1)
                act.copy(xgT[b][:, 0:8, :].rearrange("p k t -> p (k t)"), PS[:, 2, :]).then_inc(xgT_act, 1)

            def expert(n, b, after, last_pass=False):
                act.wait_ge(gu_done, n + 1)
                if after:
                    act.wait_ge(hid_ready, n)
                act.activation(sil, PS[0:SLOTS, b, :], ACT.Silu).then_inc(silu_ready, 1)
                if not last_pass:
                    rows_copied(n + 1, 1 - b)
                act.wait_ge(down_done, n + 1)
                if after == 2:
                    act.wait_ge(ye_stored, n * 16 - 16)
                act.copy(yb[b][:, 0:NCOL], PS[:, 5, :]).then_inc(ye_act, 1)

            rows_copied(0, 0)
            expert(0, 0, 0)
            expert(1, 1, 1)
            with act.Fori(1, NE // 2 - 1) as i:
                for b in range(2):
                    expert(i * 2 + b, b, 2)
            expert(NE - 2, 0, 2)
            expert(NE - 1, 1, 2, True)
            act.wait_ge(counts_ready, 1)
            with act.If(act.value_load(max_i[0:1, 0:1], min_val=0, max_val=S) > SLOTS):
                with act.Fori(1, ROUNDS) as r:
                    with act.Fori(0, NE) as e:
                        with act.If(act.value_load(cnt_i[0:1, bass.ds(e, 1)], min_val=0, max_val=S) > r * SLOTS):
                            no = act.value_load(extra_no[0:1, bass.ds(r * NE + e, 1)], min_val=0, max_val=16)
                            act.wait_ge(xpe, no * 4 + 2)
                            act.wait_ge(xcopy, no * 5 + 1)
                            act.activation(sil, PS[0:SLOTS, 0, :], ACT.Silu).then_inc(xcopy, 1)
            def normalise(i):
                act.wait_ge(scale_ready, i + 1)
                act.activation(h1[:, i, :], h1[:, i, :], ACT.Identity, scale=lnt[:, i, 2:3], bias=lnt[:, i, 6:7]
                               ).then_inc(normed, 1)

            for i in range(TT):
                act.wait_ge(std_asked, TT + i + 1)
                act.activation(lnt[:, i, 1:2], lnt[:, i, 0:1], ACT.Sqrt).then_inc(std_ready, 1)
                if i >= 1:
                    normalise(i - 1)
            normalise(TT - 1)

        @block.tensor
        def _(pe):
            pe.wait_ge(ident_ready, 2)
            for i in range(TT):
                pe.wait_ge(x_loaded[i], 16)
                for j in range(4):
                    if i >= 1:
                        pe.wait_ge((xt_act, xt_dve)[j % 2], 2 * (i - 1) + j // 2 + 1)
                    for k in range(4):
                        kt = 4 * j + k
                        last = pe.transpose(PS[:, j, k * P:(k + 1) * P], xrows[:, i, kt * P:(kt + 1) * P], ident[:])
                    last.then_inc(xt_done, 1)
            pe.wait_ge(xt_act, KT // 2)
            pe.wait_ge(xt_dve, KT // 2)

            def project(i, b):
                pe.wait_ge(ring_loaded[b], i * 16 + 16)
                for kt in range(KT):
                    last = pe.matmul(PS[:, 4 + b, :], ring_view(b, KT, P)[:, kt, :], xT[:, kt, :],
                                     start=kt == 0, stop=kt == KT - 1)
                last.then_inc(ring_used, 1)

            def b_side(d):
                pe.wait_ge(bt_ready, d + 1)
                pe.wait_ge(fc_ready, 4)
                for j in range(GP // 2):
                    if j >= 4 or d == 1:
                        pe.wait_ge(bm_ready, d * (GP // 2) + max(j - 4, -1) + 1)
                    for g in range(2):
                        for r in range(2):
                            last = pe.transpose(PS[:, j % 4, (2 * g + r) * P:(2 * g + r + 1) * P],
                                                BT[:, r, 2 * j + g, :, :].rearrange("p s c -> p (s c)"), ident[:])
                    last.then_inc(btt_done, 1)
                if d == 0:
                    pe.wait_ge(par_ready, 1)
                else:
                    pe.wait_ge(lag_copied, 1)
                pe.wait_ge(fb_ready, d + 1)
                for g in range(GP):
                    h, g_in = g // (GP // 2), g % (GP // 2)
                    for r in range(2):
                        last = pe.matmul(PS[:, 6 + h, g_in * 2 * C:(g_in + 1) * 2 * C],
                                         BT[:, r, g, :, :].rearrange("p s c -> p (s c)"),
                                         FB[:, r, g, :, :].rearrange("p q c -> p (q c)"),
                                         start=(g_in == 0 and r == 0), stop=(g_in == GP // 2 - 1 and r == 1),
                                         skip_group_check=True)
                last.then_inc(lag_done, 1)

            project(0, 0)
            project(0, 1)
            pe.wait_ge(pre_ready, 1)
            for j in range(4):
                last = pe.transpose(PS[:, 6, j * 64:(j + 1) * 64], pre[:, 10 + j, :], ident[0:2 * GP, 0:2 * GP])
            last.then_inc(par_t, 1)
            pe.wait_ge(c_loaded, 16 * 32)
            for j, (r, d) in enumerate(((0, 0), (0, 1), (1, 0), (1, 1))):
                for blk in range(4):
                    last = pe.transpose(PS[:, j, blk * P:(blk + 1) * P], craw[:, r, d, blk, :], ident[:])
                last.then_inc(ct_done, 1)
            with pe.Fori(1, 4) as i:
                for b in range(2):
                    pe.wait_ge(pool_read, i * 2 + (b - 1))
                    project(i, b)
            b_side(0)
            for b in range(2):
                pe.wait_ge(pool_read, MT - 1 + b)
                project(4, b)
            with pe.Fori(5, 6) as i:
                for b in range(2):
                    pe.wait_ge(ssm_read, i * 2 + (b - 1 - MT))
                    project(i, b)
            b_side(1)
            with pe.Fori(6, 8) as i:
                for b in range(2):
                    pe.wait_ge(ssm_read, i * 2 + (b - 1 - MT))
                    project(i, b)

            pe.wait_ge(ring_loaded[0], 16 * (N_IN // 2 + 1))
            pe.wait_ge(bm_ready, GP)
            pe.wait_ge(pool_read, MT)
            for g in range(len(WINDOWS)):
                if g >= 2:
                    pe.wait_ge(pmix_ready, 2 * (g - 1))
                for h in range(PGT):
                    for k in range(PGT):
                        last = pe.matmul(PS[:, 2 * (g % 2) + h, :],
                                         ring[:, 0, :].rearrange("p (q d) -> p q d", d=256)[:, 2 * g + k, h * P:(h + 1) * P],
                                         pd[:, 2 * g + k, :], start=k == 0, stop=k == 1)
                last.then_inc(pmix_done, 1)

            pe.wait_ge(u_loaded, 16 * L)
            pe.wait_ge(ssm_read, MT)
            pe.wait_ge(lag_copied, 2)
            for j in range(GP // 2):
                if j >= 4:
                    pe.wait_ge((z_act, z_dve)[j % 2], 2 * ((j - 4) // 2) + 2)
                for g in range(2):
                    for r in range(2):
                        for d in range(2):
                            for q in range(2):
                                gp = 2 * j + g
                                col = ((g * 2 + r) * 2 + d) * NCH
                                last = pe.matmul(PS[q * NST:(q + 1) * NST, 4 + j % 4, col:col + NCH],
                                                 BM[d][:, gp, r, q * NST:(q + 1) * NST], U[:, 2 * gp + q, :],
                                                 start=True, stop=True)
                last.then_inc(z_done, 1)

            def out_pool(n, bank):
                for part in range(2):
                    slot = FIRST_WO + 2 * n + part
                    pe.wait_ge(ring_loaded[slot % 2], 16 * (slot // 2 + 1))
                    for k in range(4):
                        for i in range(TT):
                            last = pe.matmul(PS[:, bank + i, :], pd[:, 4 * part + k, i * P:(i + 1) * P],
                                             ring_view(slot % 2, 4, NCOL)[:, k, :],
                                             start=(part == 0 and k == 0), stop=(part == 1 and k == 3))
                    if part == 0:
                        last.then_inc(ring_used, 1)
                    else:
                        last.then_inc(wo_done, 1)
                pe.wait_ge(wo_done, n + 1)
                pe.nop().then_inc(ring_used, 1)

            def outputs(j):
                bank = 4 + 2 * (j % 2)
                for g in range(8):
                    gp = 8 * j + g
                    for q in range(2):
                        pe.matmul(PS[:, bank + q, g * NCH:(g + 1) * NCH],
                                  TP[:, :, q, gp],
                                  U[:, 2 * gp + q, :], start=g == 0, stop=False, skip_group_check=True)
                for g in range(8):
                    gp = 8 * j + g
                    for r in range(2):
                        for q in range(2):
                            rows = slice(q * NST, (q + 1) * NST)
                            lhs = EC[rows, r, :, gp % (GP // 2), :, :].rearrange("p d s c -> p d (s c)")
                            pe.matmul(PS[:, bank + q, g * NCH + 1:(g + 1) * NCH], lhs[:, 0, :],
                                      st[rows, 0:NCH - 1, r, 0, gp], start=False, stop=False, skip_group_check=True)
                            last = pe.matmul(PS[:, bank + q, g * NCH:(g + 1) * NCH - 1], lhs[:, 1, :],
                                             st[rows, NCH - 2::-1, r, 1, gp], start=False,
                                             stop=(g == 7 and r == 1), skip_group_check=True)
                last.then_inc(y_done, 1)

            pe.wait_ge(pmix_ready, MT)
            pe.nop().then_inc(ring_used, 1)
            out_pool(0, 0)
            pe.wait_ge(z_act, GP // 2)
            pe.wait_ge(z_dve, GP // 2)
            out_pool(1, 4)
            pe.wait_ge(wo_read, TT)
            out_pool(2, 0)
            pe.wait_ge(wo_read, 2 * TT)
            pe.wait_ge(t_loaded, 16)
            pe.wait_ge(ec_ready, 1)
            pe.wait_ge(scan_ready, 1)
            outputs(0)
            outputs(1)
            pe.wait_ge(wo_read, 3 * TT)
            out_pool(3, 0)
            pe.wait_ge(ec_ready, 2)
            pe.wait_ge(y_copied, 2)
            outputs(2)
            pe.wait_ge(y_copied, 4)
            outputs(3)

            pe.wait_ge(gelu_ready, MT)
            pe.wait_ge(wo_read, NN * TT)
            for m in range(MT):
                slot = FIRST_GLU + m // 2
                pe.wait_ge(ring_loaded[slot % 2], 16 * (slot // 2 + 1))
                if m >= 2:
                    pe.wait_ge(sig_ready, m - 1)
                for k in range(MT):
                    last = pe.matmul(PS[:, m % 2, :], ring_view(slot % 2, MT, 256)[:, k, (m % 2) * P:(m % 2 + 1) * P],
                                     uT[:, k, :], start=k == 0, stop=k == MT - 1)
                last.then_inc(glu_done, 1)
                if m % 2 == 1:
                    pe.wait_ge(glu_done, m + 1)
                    pe.nop().then_inc(ring_used, 1)

            def out_tile(i):
                bank = 4 - 4 * (i % 2)
                for n in range(NN):
                    for k in range(MT):
                        last = pe.matmul(PS[:, bank + n, :], Z[:, k, i * P:(i + 1) * P],
                                         w2[k // 4][:, k % 4, n * NCOL:(n + 1) * NCOL],
                                         start=k == 0, stop=k == MT - 1)
                last.then_inc(wo_done, 1)

            def router_tile(i):
                bank = 4 - 4 * (i % 2)
                pe.wait_ge(h_ready, i + 1)
                if i >= 2:
                    pe.wait_ge(logit_done, i - 1)
                for j in range(4):
                    for k in range(4):
                        kt = 4 * j + k
                        last = pe.transpose(PS[:, bank + j, k * P:(k + 1) * P], h1[:, i, kt * P:(kt + 1) * P],
                                            ident[:])
                    last.then_inc(ht_done, 1)
                pe.wait_ge(xt_act, KT // 2 + 2 * (i + 1))
                pe.wait_ge(xt_dve, KT // 2 + 2 * (i + 1))
                for kt in range(KT):
                    last = pe.matmul(PS[:, bank, 0:E1], hT[:, i % 2, kt, :], rw[:, kt, :],
                                     start=kt == 0, stop=kt == KT - 1)
                last.then_inc(logit_done, 1)

            pe.wait_ge(glu_ready, MT)
            pe.wait_ge(y_copied, 8)
            pe.wait_ge(w2_loaded, 16 * MT)
            pe.wait_ge(ln_loaded, 96)
            out_tile(0)
            out_tile(1)
            router_tile(0)
            pe.wait_ge(logit_read, 1)
            out_tile(2)
            router_tile(1)
            pe.wait_ge(logit_read, 2)
            out_tile(3)
            router_tile(2)
            router_tile(3)
            pe.wait_ge(onehot_ready, 1)
            pe.wait_ge(iota_ready, 2)
            for i in range(TT):
                for k in range(i):
                    pe.matmul(PS[:, 5, i * NE:(i + 1) * NE], ones, one[:, k, :], start=k == 0, stop=False)
                pe.matmul(PS[:, 5, i * NE:(i + 1) * NE], tri, one[:, i, :], start=i == 0, stop=True)
            for i in range(TT):
                last = pe.matmul(PS[:, 5, TT * NE:(TT + 1) * NE], ones, one[:, i, :], start=i == 0, stop=i == TT - 1)
            last.then_inc(rank_done, 1)

            def rows_T(n, b):
                pe.wait_ge(xg_loaded, n * 16 + 16)
                pe.nop().then_inc(pe_turn, 1)
                for kt in range(KT):
                    last = pe.transpose(PS[:, 2 + kt // 8, (kt % 8) * SLOTS:(kt % 8 + 1) * SLOTS],
                                        xg[b].rearrange("p (d k) -> p k d", k=KT)[:, kt, :],
                                        ident[0:SLOTS, 0:SLOTS])
                last.then_inc(xg_t, 1)

            def expert(n, b, last_pass):
                pe.wait_ge(xgT_act, n + 1)
                pe.wait_ge(xgT_dve, n + 1)
                for c in range(WQ):
                    pe.wait_ge(wg_loaded[c], n * 16 + 16)
                    pe.wait_ge(wu_loaded[c], n * 16 + 16)
                    for kt in range(4 * c, 4 * c + 4):
                        for m, w in enumerate((wg, wu)):
                            last = pe.matmul(PS[m * SLOTS:(m + 1) * SLOTS, b, :], xgT[b][:, kt, :], w[:, kt, :],
                                             start=kt == 0, stop=kt == KT - 1)
                            if kt % 4 == 3:
                                last.then_inc(w_used, 1)
                pe.wait_ge(w_used, n * 12 + 8)
                pe.nop().then_inc(gu_done, 1)
                if not last_pass:
                    rows_T(n + 1, 1 - b)
                pe.wait_ge(hid_ready, n + 1)
                pe.nop().then_inc(pe_turn, 1)
                for k in range(FT):
                    last = pe.transpose(PS[:, 4, k * SLOTS:(k + 1) * SLOTS],
                                        hid.rearrange("p (f k) -> p k f", k=FT)[:, k, :], ident[0:SLOTS, 0:SLOTS])
                last.then_inc(hid_t, 1)
                pe.wait_ge(hidT_ready, n + 1)
                return last

            def down(n, after):
                if after:
                    pe.wait_ge(ye_act, n)
                    pe.wait_ge(ye_dve, n)
                for k in range(FT):
                    pe.wait_ge(wd_loaded[k], n * 16 + 16)
                    for c in range(2):
                        for m in range(2):
                            last = pe.matmul(PS[m * SLOTS:(m + 1) * SLOTS, 5 + c, :], hidT[:, k, :],
                                             wd[:, k, (2 * m + c) * NCOL:(2 * m + c + 1) * NCOL],
                                             start=k == 0, stop=k == FT - 1)
                    last.then_inc(w_used, 1)
                pe.wait_ge(w_used, n * 12 + 12)
                pe.nop().then_inc(down_done, 1)

            pe.wait_ge(table_ready, 1)
            for k in range(2):
                for i in range(TT):
                    last = pe.matmul(PS[:, 6, 0:NE], rank_eq[:, k, i, :], val_e[:, k, i, :],
                                     start=(k == 0 and i == 0), stop=(k == 1 and i == TT - 1))
            last.then_inc(table_done, 1)
            rows_T(0, 0)
            expert(0, 0, False)
            down(0, False)
            expert(1, 1, False)
            down(1, True)
            with pe.Fori(1, NE // 2 - 1) as i:
                for b in range(2):
                    expert(i * 2 + b, b, False)
                    down(i * 2 + b, True)
            expert(NE - 2, 0, False)
            down(NE - 2, True)
            expert(NE - 1, 1, True)
            down(NE - 1, True)
            pe.wait_ge(counts_ready, 1)
            pe.wait_ge(ye_act, NE)
            pe.wait_ge(ye_dve, NE)
            with pe.If(pe.value_load(max_i[0:1, 0:1], min_val=0, max_val=S) > SLOTS):
                with pe.Fori(1, ROUNDS) as r:
                    with pe.Fori(0, NE) as e:
                        with pe.If(pe.value_load(cnt_i[0:1, bass.ds(e, 1)], min_val=0, max_val=S) > r * SLOTS):
                            no = pe.value_load(extra_no[0:1, bass.ds(r * NE + e, 1)], min_val=0, max_val=16)
                            pe.wait_ge(xg2_loaded, no * 16 + 16)
                            pe.nop().then_inc(pe_turn, 1)
                            for kt in range(KT):
                                last = pe.transpose(PS[:, 2 + kt // 8, (kt % 8) * SLOTS:(kt % 8 + 1) * SLOTS],
                                                    xg[0].rearrange("p (d k) -> p k d", k=KT)[:, kt, :],
                                                    ident[0:SLOTS, 0:SLOTS])
                            last.then_inc(xpe, 1)
                            pe.wait_ge(xcopy, no * 5 + 1)
                            pe.wait_ge(xw_loaded, no * 48 + 48)
                            for kt in range(KT):
                                for m, w in enumerate((wg, wu)):
                                    last = pe.matmul(PS[m * SLOTS:(m + 1) * SLOTS, 0, :], xgT[0][:, kt, :],
                                                     w[:, kt, :], start=kt == 0, stop=kt == KT - 1)
                            last.then_inc(xpe, 1)
                            pe.wait_ge(xcopy, no * 5 + 3)
                            pe.nop().then_inc(pe_turn, 1)
                            for k in range(FT):
                                last = pe.transpose(PS[:, 4, k * SLOTS:(k + 1) * SLOTS],
                                                    hid.rearrange("p (f k) -> p k f", k=FT)[:, k, :],
                                                    ident[0:SLOTS, 0:SLOTS])
                            last.then_inc(xpe, 1)
                            pe.wait_ge(xcopy, no * 5 + 4)
                            for k in range(FT):
                                for c in range(2):
                                    for m in range(2):
                                        last = pe.matmul(PS[m * SLOTS:(m + 1) * SLOTS, 5 + c, :], hidT[:, k, :],
                                                         wd[:, k, (2 * m + c) * NCOL:(2 * m + c + 1) * NCOL],
                                                         start=k == 0, stop=k == FT - 1)
                            last.then_inc(xpe, 1)

        @block.vector
        def _(dve):
            chain = [0]

            def link(ins):
                chain[0] += 1
                ins.then_inc(dve_chain, 1)
                dve.wait_ge(dve_chain, chain[0])

            def tt(o, a, b, op):
                return dve.tensor_tensor(o, a, b, op)

            def ts(o, a, s1, s2, op0, op1=ALU.bypass):
                return dve.tensor_scalar(o, a, s1, s2, op0, op1)

            lr, li, lrdt, sin_in = (pre[:, j, :] for j in range(4))
            mag, sin, cos, cos_in = (pre[:, j, :] for j in range(4, 8))
            t0, t1 = pre[:, 8, :], pre[:, 9, :]
            ar, ai, zr, zi = (pre[:, 10 + j, :] for j in range(4))
            dve.wait_ge(pre_act, 1)
            for q in range(2):
                n = slice(q * NST, (q + 1) * NST)
                ts(t0[:, n], li[:, n], pdt[:, 2 + q:3 + q], None, ALU.mult)
                last = ts(lrdt[:, n], lr[:, n], pdt[:, 2 + q:3 + q], None, ALU.mult)
            last.then_inc(pre_dve, 1)
            dve.wait_ge(pre_dve, 1)
            magic = 12582912.0
            link(ts(t1, t0, 1.0 / (2.0 * math.pi), magic, ALU.mult, ALU.add))
            link(ts(t1, t1, magic, None, ALU.subtract))
            c1 = 6.28125
            c2 = 8.0 * round((2.0 * math.pi - c1) * 2 ** 19 / 8.0) / 2 ** 19
            c3 = 2.0 * math.pi - c1 - c2
            for cc in (c1, c2, c3):
                link(dve.scalar_tensor_tensor(out=t0, in0=t1, scalar=-cc, in1=t0, op0=ALU.mult, op1=ALU.add))
            link(ts(sin_in, t0, 3.1415925, -3.1415925, ALU.min, ALU.max))
            link(ts(t1, sin_in, -1.0, None, ALU.mult))
            link(tt(t1, t1, sin_in, ALU.max))
            ts(cos_in, t1, -1.0, math.pi / 2.0, ALU.mult, ALU.add).then_inc(pre_dve, 1)
            link(tt(t0, lr, lr, ALU.mult))
            link(tt(t1, li, li, ALU.mult))
            link(tt(t0, t0, t1, ALU.add))
            link(dve.reciprocal(t0, t0))
            dve.wait_ge(pre_act, 4)
            link(tt(ar, mag, cos, ALU.mult))
            link(tt(ai, mag, sin, ALU.mult))
            link(ts(mag, ar, -1.0, None, ALU.add))
            tt(zr, mag, lr, ALU.mult)
            tt(t1, ai, li, ALU.mult)
            tt(zi, ai, lr, ALU.mult)
            link(tt(sin, mag, li, ALU.mult))
            tt(zr, zr, t1, ALU.add)
            link(tt(zi, zi, sin, ALU.subtract))
            tt(zr, zr, t0, ALU.mult)
            tt(zi, zi, t0, ALU.mult).then_inc(pre_ready, 1)
            for i in range(TT):
                for j in range(1, 4, 2):
                    dve.wait_ge(xt_done, 4 * i + j + 1)
                    dve.tensor_copy(xT[:, 4 * j:4 * j + 4, i * P:(i + 1) * P],
                                    PS[:, j, :].rearrange("p (k t) -> p k t", k=4)).then_inc(xt_dve, 1)

            wide = S + 2 * PAD
            tA, tB = tmp[:, 0, :], tmp[:, 1, :]

            def pool_tile(m):
                w = WINDOWS[m // PGT]
                bank = 4 + m % 2
                dve.wait_ge(ring_used, m + 1)
                dve.memset(tA[:, 0:PAD], 0.0)
                dve.memset(tA[:, PAD + S:wide], 0.0)
                link(dve.tensor_copy(tA[:, PAD:PAD + S], PS[:, bank, :]))
                src, dst, sh, lo, hi = tA, tB, None, 1, wide - 1
                span = 2
                while True:
                    back, ahead = (1, 0) if span == 2 else (span // 4, span // 4)
                    if span == w:
                        link(tt(pd[:, m, :], src[:, PAD - back:PAD - back + S],
                                src[:, PAD + ahead:PAD + ahead + S], ALU.add))
                        break
                    link(tt(dst[:, lo:hi], src[:, lo - back:hi - back], src[:, lo + ahead:hi + ahead], ALU.add))
                    src, dst = dst, src
                    lo, hi, span = lo + span // 2, hi - span // 2, 2 * span
                q = m // PGT
                tt(pd[:, m, 0:w // 2], pd[:, m, 0:w // 2], edge[:, q, 0:w // 2], ALU.mult).then_inc(dve_chain, 1)
                chain[0] += 1
                if w > 2:
                    tt(pd[:, m, S - w // 2 + 1:S], pd[:, m, S - w // 2 + 1:S], edge[:, q, w // 2:w - 1],
                       ALU.mult).then_inc(dve_chain, 1)
                    chain[0] += 1
                dve.wait_ge(dve_chain, chain[0])
                dve.scalar_tensor_tensor(out=pd[:, m, :], in0=pd[:, m, :], scalar=1.0 / w, in1=PS[:, bank, :],
                                         op0=ALU.mult, op1=ALU.subtract).then_inc(pool_read, 1)

            dve.wait_ge(edge_ready, 1)
            pool_tile(0)
            pool_tile(1)

            dve.wait_ge(par_t, 1)
            dve.tensor_copy(par[:].rearrange("p q d g -> p (q d g)"), PS[:, 6, 0:4 * 2 * GP]).then_inc(par_ready, 1)
            dve.wait_ge(par_ready, 1)
            dve.wait_ge(b_loaded, 64)
            shape = [P, 2 * GP, C]

            def per_pair(q):
                return par[:, q, :, :].rearrange("p d g -> p (d g)").unsqueeze(2).to_broadcast(shape)

            def flat(v, r):
                return v[:, r].rearrange("p d g c -> p (d g) c")

            w0 = pw[:, 0, 0, :].rearrange("p (a c) -> p a c", c=C)
            w1 = pw[:, 0, 1, :].rearrange("p (a c) -> p a c", c=C)
            w2 = pw[:, 1, 0, :].rearrange("p (a c) -> p a c", c=C)
            w3 = pw[:, 1, 1, :].rearrange("p (a c) -> p a c", c=C)
            for hf in range(2):
                sl = slice(hf * GP, (hf + 1) * GP)
                sh = [P, GP, C]
                z_r = par[:, 2, hf, :].unsqueeze(2).to_broadcast(sh)
                z_i = par[:, 3, hf, :].unsqueeze(2).to_broadcast(sh)
                br_, bi_ = braw[:, 0, hf], braw[:, 1, hf]
                tt(w0, br_, z_r, ALU.mult)
                tt(w1, bi_, z_i, ALU.mult)
                tt(w2, bi_, z_r, ALU.mult)
                link(tt(w3, br_, z_i, ALU.mult))
                tt(bbar[:, 0, hf], w0, w1, ALU.subtract)
                link(tt(bbar[:, 1, hf], w2, w3, ALU.add))

            def b_powers(d):
                sh4 = [P, 2, GP, C]
                a_r = par[:, 0, d, :].unsqueeze(1).unsqueeze(3).to_broadcast(sh4)
                a_i = par[:, 1, d, :].unsqueeze(1).unsqueeze(3).to_broadcast(sh4)
                T1 = pw[:, 0].rearrange("p r (g c) -> p r g c", c=C)
                T2 = pw[:, 1].rearrange("p r (g c) -> p r g c", c=C)
                slot = (lambda q: q) if d == 0 else (lambda q: L - 1 - q)
                link(dve.tensor_copy(BT[:, :, :, slot(0), :], bbar[:, :, d]))
                for q in range(1, L):
                    v = BT[:, :, :, slot(q - 1), :]
                    tt(T1, v, a_r, ALU.mult)
                    link(tt(T2, v, a_i, ALU.mult))
                    tt(BT[:, 0, :, slot(q), :], T1[:, 0], T2[:, 1], ALU.subtract)
                    last = tt(BT[:, 1, :, slot(q), :], T1[:, 1], T2[:, 0], ALU.add)
                    if q < L - 1:
                        link(last)
                last.then_inc(bt_ready, 1)

            def c_blocks(d):
                for q in range(2):
                    rows = slice(q * NST, (q + 1) * NST)
                    last = dve.tensor_copy(FB[rows, :, :, q, :], FC[rows, :, d, :, :])
                last.then_inc(fb_ready, 1)

            dve.memset(r_ssm[:, 2048:4096], 0.0).then_inc(fb_clear, 1)
            dve.wait_ge(fb_clear, 1)
            dve.wait_ge(fc_ready, 4)
            c_blocks(0)
            b_powers(0)
            for m in range(2, MT):
                pool_tile(m)

            def lags_out(d):
                dve.wait_ge(lag_done, d + 1)
                for h in range(2):
                    gs = slice(h * (GP // 2), (h + 1) * (GP // 2))
                    last = dve.tensor_copy(ksb[:, d, :, :, gs],
                                           PS[:, 6 + h, :].rearrange("p (g q c) -> p c q g", q=2, c=C))
                last.then_inc(lag_copied, 1)

            lags_out(0)
            c_blocks(1)
            dve.wait_ge(btt_done, GP // 2)
            b_powers(1)
            lags_out(1)

            def add_out(n, count, bank, first):
                dve.wait_ge(wo_done, count)
                for i in range(TT):
                    cols = h1[:, i, n * NCOL:(n + 1) * NCOL]
                    if first:
                        dve.scalar_tensor_tensor(out=cols, in0=cols, scalar=ALPHA, in1=PS[:, bank + i, :],
                                                 op0=ALU.mult, op1=ALU.add).then_inc(wo_read, 1)
                    else:
                        tt(cols, cols, PS[:, bank + i, :], ALU.add).then_inc(wo_read, 1)

            pa = par[:].rearrange("p q d g -> p q (d g)")
            cr, ci = coef[:, 0, 0, :], coef[:, 0, 1, :]
            s0, s1 = tmp[:, 0, 0:2 * GP], tmp[:, 0, 2 * GP:4 * GP]
            s2 = tmp[:, 0, 4 * GP:6 * GP]
            pr, pi_ = tmp[:, 1, 0:2 * GP], tmp[:, 1, 2 * GP:4 * GP]
            dve.tensor_copy(pr, pa[:, 0, :])
            link(dve.tensor_copy(pi_, pa[:, 1, :]))
            for _ in range(int(math.log2(L))):
                tt(s0, pr, pr, ALU.mult)
                tt(s1, pi_, pi_, ALU.mult)
                link(tt(s2, pr, pi_, ALU.mult))
                tt(pr, s0, s1, ALU.subtract)
                link(ts(pi_, s2, 2.0, None, ALU.mult))
            dve.tensor_copy(coef[:, 0, 0, :], pr)
            dve.tensor_copy(coef[:, 0, 1, :], pr)
            dve.tensor_copy(coef[:, 1, 0, :], pi_)
            link(ts(coef[:, 1, 1, :], pi_, -1.0, None, ALU.mult))
            for j in range(1, GP // 2, 2):
                dve.wait_ge(z_done, j + 1)
                for d, order in ((0, 1), (1, -1)):
                    src = PS[:, 4 + j % 4, :].rearrange("p (g r d k) -> p d k r g", g=2, r=2, d=2)[:, d]
                    dve.tensor_copy(st[:, ::order, :, d, 2 * j:2 * j + 2], src).then_inc(z_dve, 1)
            dve.wait_ge(z_dve, GP // 2)
            dve.wait_ge(z_act, GP // 2)
            sT = tmp[:, 0, 0:8 * GP].rearrange("p (q r e) -> p q r e", q=2, r=2)
            sS = tmp[:, 1, 0:4 * GP].rearrange("p (r e) -> p r e", r=2)

            def scan(prev, cur, count):
                tt(sT, prev.unsqueeze(1).to_broadcast([P, 2, 2, 2 * GP]), coef[:], ALU.mult).then_inc(scan_step, 1)
                dve.wait_ge(scan_step, count + 1)
                tt(sS, sT[:, 0], sT[:, 1, ::-1, :], ALU.add).then_inc(scan_step, 1)
                dve.wait_ge(scan_step, count + 2)
                tt(cur, cur, sS, ALU.add).then_inc(scan_step, 1)
                dve.wait_ge(scan_step, count + 3)

            UN = 7

            def scan_part(lo, hi):
                with dve.Fori(lo, hi) as i:
                    for j in range(UN):
                        prev = st_flat[:, bass.ds(i * UN + j, 1)].rearrange("p o r e -> p (o r) e")
                        cur = st_flat[:, bass.ds(i * UN + (j + 1), 1)].rearrange("p o r e -> p (o r) e")
                        scan(prev, cur, i * (3 * UN) + 3 * j)

            scan_part(0, 5)
            dve.wait_ge(xr_loaded, 16)
            add_out(0, 1, 0, True)
            scan_part(5, (NCH - 1) // UN)
            dve.memset(sS, 0.0).then_inc(scan_ready, 1)

            def c_powers(half_no):
                gs = slice(half_no * (GP // 2), (half_no + 1) * (GP // 2))
                sh4 = [P, 2, GP // 2, C]
                T1 = tmp[:, 0, 0:512].rearrange("p (r g c) -> p r g c", r=2, c=C)
                T2 = tmp[:, 1, 0:512].rearrange("p (r g c) -> p r g c", r=2, c=C)
                for d in range(2):
                    a_r = par[:, 0, d, gs].unsqueeze(1).unsqueeze(3).to_broadcast(sh4)
                    a_i = par[:, 1, d, gs].unsqueeze(1).unsqueeze(3).to_broadcast(sh4)
                    slot = (lambda q: q - 1) if d == 0 else (lambda q: L - q)
                    for q in range(1, L + 1):
                        v = FC[:, :, d, gs, :] if q == 1 else EC[:, :, d, :, slot(q - 1), :]
                        tt(T1, v, a_r, ALU.mult)
                        link(tt(T2, v, a_i, ALU.mult))
                        tt(EC[:, 0, d, :, slot(q), :], T1[:, 0], T2[:, 1], ALU.add)
                        last = tt(EC[:, 1, d, :, slot(q), :], T1[:, 1], T2[:, 0], ALU.subtract)
                        if not (d == 1 and q == L):
                            link(last)
                last.then_inc(ec_ready, 1)

            dve.wait_ge(scan_ready, 1)
            c_powers(0)
            add_out(1, 2, 4, True)
            add_out(2, 3, 0, True)
            dve.wait_ge(y_done, 2)
            dve.wait_ge(ec_ready, 1)
            c_powers(1)
            add_out(3, 4, 0, True)

            dve.wait_ge(vec_loaded, 48)
            dve.wait_ge(y_loaded, 16 * MT)
            for m in range(MT):
                dve.scalar_tensor_tensor(out=uT[:, m, :], in0=uT[:, m, :], scalar=vecs[:, 1, m:m + 1],
                                         in1=Z[:, m, :], op0=ALU.mult, op1=ALU.add).then_inc(skip_done, 1)
            for m in range(MT):
                dve.wait_ge(sig_ready, m + 1)
                tt(Z[:, m, :].rearrange("p (k s) -> p s k", s=L),
                   tmp[:, m % 2, 0:S].rearrange("p (s k) -> p s k", s=L),
                   uT[:, m, :].rearrange("p (s k) -> p s k", s=L), ALU.mult).then_inc(glu_ready, 1)
            def norm_stats(i, lt, asked):
                for q in range(4):
                    last = dve.bn_stats(stats[:, q, :], h1[:, i, q * NCOL:(q + 1) * NCOL])
                link(last)
                link(dve.bn_aggr(lt[:, 4:6], stats[:]))
                ts(lt[:, 0:1], lt[:, 5:6], EPS, None, ALU.add).then_inc(std_asked, 1)
                dve.wait_ge(std_ready, asked)
                link(dve.reciprocal(lt[:, 2:3], lt[:, 1:2]))
                link(tt(lt[:, 3:4], lt[:, 2:3], lt[:, 2:3], ALU.mult))
                link(tt(lt[:, 3:4], lt[:, 3:4], lt[:, 0:1], ALU.mult))
                link(ts(lt[:, 3:4], lt[:, 3:4], -0.5, 1.5, ALU.mult, ALU.add))
                link(tt(lt[:, 2:3], lt[:, 3:4], lt[:, 2:3], ALU.mult))

            def norm(i, gain, bias, asked):
                row, lt = h1[:, i, :], lnt[:, 0]
                norm_stats(i, lt, asked)
                link(ts(row, row, lt[:, 4:5], lt[:, 2:3], ALU.subtract, ALU.mult))
                link(tt(row, row, gain, ALU.mult))
                return tt(row, row, bias, ALU.add)

            def router_copies(i):
                bank = 4 - 4 * (i % 2)
                for j in range(1, 4, 2):
                    dve.wait_ge(ht_done, 4 * i + j + 1)
                    dve.tensor_copy(hT[:, i % 2, 4 * j:4 * j + 4, :].rearrange("p k t -> p (k t)"),
                                    PS[:, bank + j, :]).then_inc(xt_dve, 1)
                dve.wait_ge(logit_done, i + 1)
                tt(lg[:, i, :], PS[:, bank, 0:E1], rbias, ALU.add).then_inc(logit_read, 1)

            def ln1_tile(i):
                dve.wait_ge(wo_done, NN + i + 1)
                for n in range(NN):
                    cols = h1[:, i, n * NCOL:(n + 1) * NCOL]
                    tt(cols, cols, PS[:, 4 - 4 * (i % 2) + n, :], ALU.add).then_inc(wo_read, 1)
                dve.wait_ge(wo_read, (NN + i + 1) * NN)
                norm(i, ln1g, ln1b, i + 1).then_inc(h_ready, 1)

            dve.wait_ge(ln_loaded, 96)
            ln1_tile(0)
            ln1_tile(1)
            router_copies(0)
            ln1_tile(2)
            router_copies(1)
            ln1_tile(3)
            router_copies(2)
            router_copies(3)

            dve.wait_ge(iota_ready, 2)
            dve.wait_ge(logit_read, TT)
            sg = [P, TT, NG]
            link(dve.tensor_reduce(gmax, lg[:, :, 0:NG], AX, ALU.max))
            tt(gd, lg[:, :, 0:NG], gmax.unsqueeze(2).to_broadcast(sg), ALU.subtract).then_inc(exp_asked, 1)
            dve.wait_ge(exp_asked, 1)
            link(ts(gv, gd, 0.0, None, ALU.is_equal))
            link(tt(gv, gv, iota_g.unsqueeze(1).to_broadcast(sg), ALU.mult))
            link(dve.tensor_reduce(vmax, gv, AX, ALU.max))
            link(tt(gm, gv, vmax.unsqueeze(2).to_broadcast(sg), ALU.is_equal))
            link(tt(prod, lg[:, :, NG:E1].rearrange("p i (g j) -> p i g j", g=NG),
                    gm.unsqueeze(3).to_broadcast([P, TT, NG, EPG]), ALU.mult))
            link(dve.tensor_reduce(sel, prod.rearrange("p i g j -> p i j g"), AX, ALU.add))
            for i in range(TT):
                last = dve.max(top[:, i, :], sel[:, i, :])
            link(last)
            for i in range(TT):
                last = dve.max_index(topi[:, i, :], top[:, i, :], sel[:, i, :])
            link(last)
            tt(gap, top[:, :, 1], top[:, :, 0], ALU.subtract).then_inc(exp_asked, 1)
            link(ts(gbase, vmax, -float(EPG), float(NG * EPG), ALU.mult, ALU.add))
            link(dve.tensor_copy(topf, topi))
            for k in range(2):
                last = tt(eid[:, k, :], topf[:, :, k], gbase, ALU.add)
            link(last)
            se = [P, TT, NE]
            ie = iota_e.unsqueeze(1).to_broadcast(se)
            for k in range(2):
                last = tt(onek[:, k], ie, eid[:, k, :].unsqueeze(2).to_broadcast(se), ALU.is_equal)
            link(last)
            tt(one, onek[:, 0], onek[:, 1], ALU.add).then_inc(onehot_ready, 1)
            dve.wait_ge(rank_done, 1)
            for k in range(2):
                link(tt(prod2, PS[:, 5, 0:TT * NE].rearrange("p (i e) -> p i e", i=TT), onek[:, k], ALU.mult))
                link(dve.tensor_reduce(rank_k[:, k, :], prod2, AX, ALU.add))
            for k in range(2):
                for i in range(TT):
                    ts(rank_eq[:, k, i, :], iota_m, rank_k[:, k, i:i + 1], None, ALU.is_equal)
                last = tt(val_e[:, k], onek[:, k], val_f[:, :, k].unsqueeze(2).to_broadcast(se), ALU.mult)
            last.then_inc(table_ready, 1)
            def slot_rows(value, rows, halves):
                dve.tensor_scalar(rows, value, 1, None, ALU.logical_shift_right)
                return ts(halves, value, 2.0, half[:, 0:1], ALU.mult, ALU.add)

            dve.wait_ge(table_done, 1)
            link(ts(slot_i, PS[:, 6, 0:NE], float(EMPTY), None, ALU.add))
            slot_rows(slot_i, slot_g, slot_s).then_inc(slots_ready, 1)
            dve.wait_ge(exp_ready, 2)
            link(dve.tensor_reduce(gsum, ge, AX, ALU.add))
            link(dve.reciprocal(pgrp, gsum))
            link(ts(epl, egap, 1.0, None, ALU.add))
            link(dve.reciprocal(epl, epl))
            link(tt(gate[:, 0, :], pgrp, epl, ALU.mult))
            link(tt(gate[:, 1, :], gate[:, 0, :], egap, ALU.mult))
            link(ts(pos, rank_k, float(NE), None, ALU.mult))
            link(tt(pos, pos, eid, ALU.add))
            dve.tensor_copy(pos_i, pos).then_inc(pos_ready, 1)
            link(dve.tensor_copy(cnt, PS[:, 5, TT * NE:(TT + 1) * NE]))
            dve.tensor_copy(cnt_i, cnt)
            link(dve.tensor_reduce(max_f, cnt, AX, ALU.max))
            dve.tensor_copy(max_i, max_f)
            dve.memset(extra_flag[:, 0:NE], 0.0)
            for r in range(1, ROUNDS):
                last = ts(extra_flag[:, r * NE:(r + 1) * NE], cnt, float(r * SLOTS), None, ALU.is_gt)
            link(last)
            link(dve.tensor_tensor_scan(extra_scan, ones[:, 0:1].to_broadcast([P, ROUNDS * NE]), extra_flag, 0.0,
                                        ALU.mult, ALU.add))
            link(tt(extra_flag, extra_scan, extra_flag, ALU.subtract))
            link(dve.tensor_copy(extra_flag[:, 0:1], extra_scan[:, ROUNDS * NE - 1:ROUNDS * NE]))
            dve.tensor_copy(extra_no, extra_flag).then_inc(counts_ready, 1)


            def rows_copied(n, b):
                dve.wait_ge(xg_t, n + 1)
                dve.tensor_copy(xgT[b][:, 8:16, :].rearrange("p k t -> p (k t)"), PS[:, 3, :]).then_inc(xgT_dve, 1)

            def expert(n, b, after, last_pass):
                dve.wait_ge(silu_ready, n + 1)
                tt(hid, sil, PS[SLOTS:P, b, :], ALU.mult).then_inc(hid_ready, 1)
                dve.wait_ge(hid_t, n + 1)
                dve.tensor_copy(hidT.rearrange("p k t -> p (k t)"), PS[:, 4, 0:FT * SLOTS]).then_inc(hidT_ready, 1)
                if not last_pass:
                    rows_copied(n + 1, 1 - b)
                dve.wait_ge(down_done, n + 1)
                if after:
                    dve.wait_ge(ye_stored, n * 16 - 16)
                dve.tensor_copy(yb[b][:, NCOL:2 * NCOL], PS[:, 6, :]).then_inc(ye_dve, 1)

            rows_copied(0, 0)
            expert(0, 0, False, False)
            expert(1, 1, False, False)
            with dve.Fori(1, NE // 2 - 1) as i:
                for b in range(2):
                    expert(i * 2 + b, b, True, False)
            expert(NE - 2, 0, True, False)
            expert(NE - 1, 1, True, True)
            dve.wait_ge(h_stored, 16 * TT)
            for i in range(TT):
                ts(h1[:, i, :], h1[:, i, :], ALPHA, None, ALU.mult).then_inc(h_scaled, 1)
            with dve.If(dve.value_load(max_i[0:1, 0:1], min_val=0, max_val=S) > SLOTS):
                with dve.Fori(1, ROUNDS) as r:
                    with dve.Fori(0, NE) as e:
                        with dve.If(dve.value_load(cnt_i[0:1, bass.ds(e, 1)], min_val=0, max_val=S) > r * SLOTS):
                            no = dve.value_load(extra_no[0:1, bass.ds(r * NE + e, 1)], min_val=0, max_val=16)
                            dve.wait_ge(xs_loaded, no * 32 + 32)
                            slot_rows(xslot, xgi, xsi).then_inc(xs_ready, 1)
                            dve.wait_ge(xpe, no * 4 + 1)
                            dve.tensor_copy(xgT[0].rearrange("p (a k) t -> p a (k t)", a=2), PS[:, 2:4, :]
                                            ).then_inc(xcopy, 1)
                            dve.wait_ge(xcopy, no * 5 + 2)
                            tt(hid, sil, PS[SLOTS:P, 0, :], ALU.mult).then_inc(xcopy, 1)
                            dve.wait_ge(xpe, no * 4 + 3)
                            dve.tensor_copy(hidT.rearrange("p k t -> p (k t)"), PS[:, 4, 0:FT * SLOTS]
                                            ).then_inc(xcopy, 1)
                            dve.wait_ge(xpe, no * 4 + 4)
                            dve.tensor_copy(yb[0].rearrange("p (a n) -> p a n", a=2), PS[:, 5:7, :]).then_inc(xcopy, 1)

            dve.wait_ge(h_scaled, TT)
            dve.wait_ge(ln2_loaded, 32)

            def combine(i):
                dve.wait_ge(res_loaded[i], 16)
                for k in range(2):
                    link(dve.scalar_tensor_tensor(out=h1[:, i, :], in0=res[i][:, k * D:(k + 1) * D],
                                                  scalar=gate[:, k, i:i + 1], in1=h1[:, i, :],
                                                  op0=ALU.mult, op1=ALU.add))
                norm_stats(i, lnt[:, i], TT + i + 1)
                dve.scalar_tensor_tensor(out=lnt[:, i, 6:7], in0=lnt[:, i, 4:5], scalar=-1.0, in1=lnt[:, i, 2:3],
                                         op0=ALU.mult, op1=ALU.mult).then_inc(scale_ready, 1)

            def gain(i):
                dve.wait_ge(normed, i + 1)
                tt(h1[:, i, :], h1[:, i, :], ln2g, ALU.mult).then_inc(gained, 1)

            combine(0)
            for i in range(1, TT):
                combine(i)
                gain(i - 1)
            gain(TT - 1)


_INS = ["x", "w_in", "pool_w", "pool_scale", "ssm_a_re", "ssm_a_im", "ssm_log_dt", "ssm_b_re", "ssm_b_im",
        "ssm_c_re", "ssm_c_im", "ssm_d", "glu_w", "glu_b", "w_out", "ln1_g", "ln1_b", "router_g_w", "router_g_b",
        "router_e_w", "router_e_b", "w_gate", "w_up", "w_down", "ln2_g", "ln2_b"]


def kernel(**inputs):
    import numpy as np
    import concourse.bacc as bacc
    from concourse.bass_utils import run_bass_kernel_spmd

    nc = bacc.Bacc("TRN2", target_bir_lowering=False, num_devices=1)
    arrays, args = {}, []
    for name in _INS:
        a = np.ascontiguousarray(inputs[name])[0]
        arrays[f"in_{name}"] = a
        args.append(nc.dram_tensor(f"in_{name}", a.shape, mybir.dt.from_np(a.dtype), kind="ExternalInput").ap())
    args.append(nc.dram_tensor("out_h", (S, D), F32, kind="ExternalOutput").ap())
    build(nc, *args)
    r = run_bass_kernel_spmd(nc, [arrays], core_ids=[0])
    return r.results[0]["out_h"].reshape(1, S, D)
```

```python
import math
from contextlib import ExitStack

import concourse.bass as bass
from concourse import mybir

F32 = mybir.dt.float32
I32 = mybir.dt.int32
U32 = mybir.dt.uint32
ALU = mybir.AluOpType
ACT = mybir.ActivationFunctionType
AX = mybir.AxisListType.X

P = 128
S = 512
D = 2048
KT = D // P
TT = S // P
NCOL = 512
NN = D // NCOL
CH = D // 2
MT = CH // P
WINDOWS = (2, 4, 8, 16)
PGT = MT // len(WINDOWS)
G = 64
C = 16
NST = 64
GP = G // 2
L = P // C
NCH = S // L
NG = 4
EPG = 8
NE = NG * EPG
F = 512
FT = F // P
SLOTS = 64
ROUNDS = S // SLOTS
EMPTY = 2 * S
PAD = 8
ALPHA = 2.0 ** 0.25
EPS = 1e-5
WQ = 4
CHUNK = 2048


def build(nc, x, w_in, pool_w, pool_scale, a_re, a_im, log_dt, b_re, b_im, c_re, c_im, ssm_d, glu_w, glu_b,
          w_out, ln1_g, ln1_b, rg_w, rg_b, re_w, re_b, w_gate, w_up, w_down, ln2_g, ln2_b, out):
    u_dram = nc.dram_tensor("u_scratch", (CH, L, NCH), F32, kind="Internal").ap()
    lag_dram = nc.dram_tensor("lag_scratch", ((2 * L - 1) * C, G * C), F32, kind="Internal").ap()
    h_dram = nc.dram_tensor("h_scratch", (S, D), F32, kind="Internal").ap()
    slot_dram = nc.dram_tensor("slot_scratch", (S * NE, 1), I32, kind="Internal").ap()
    ye_dram = nc.dram_tensor("ye_scratch", (4 * S, D // 2), F32, kind="Internal").ap()

    with ExitStack() as ctx:
        def sb(name, shape, dt=F32):
            return ctx.enter_context(nc.sbuf_tensor(name, shape, dt))

        def sem(name):
            return ctx.enter_context(nc.semaphore(name))

        PS = ctx.enter_context(nc.psum_tensor("PS", [P, 8, NCOL], F32))

        r_x = sb("r_x", [P, (NCH + 1) * 4 * GP])
        r_bm0 = sb("r_bm0", [P, 8192])
        r_bm1 = sb("r_bm1", [P, 8192])
        r_t = sb("r_t", [P, 8192])
        r_ssm = sb("r_ssm", [P, 4096])
        r_u = sb("r_u", [P, 4096])
        r_pool = sb("r_pool", [P, 4096])
        r_c = sb("r_c", [P, 2048])
        ring = sb("ring", [P, 2, CHUNK])
        tmp = sb("tmp", [P, 2, S + 2 * PAD])
        ident = sb("ident", [P, P])
        par = sb("par", [P, 4, 2, GP])
        coef = sb("coef", [P, 2, 2, 2 * GP])
        edge = sb("edge", [P, len(WINDOWS), 16])
        vecs = sb("vecs", [P, 3, MT])
        neg_one = sb("neg_one", [P, 1])

        xT = r_x[:, 0:8192].rearrange("p (k t) -> p k t", k=KT)
        xrows = r_bm0[:].rearrange("p (i d) -> p i d", i=TT)
        st = r_x[:].rearrange("p (t r d g) -> p t r d g", t=NCH + 1, r=2, d=2)
        BM = [b[:].rearrange("p (g r m) -> p g r m", g=GP, r=2) for b in (r_bm0, r_bm1)]
        BT = r_t[:].rearrange("p (r g s c) -> p r g s c", r=2, g=GP, s=L)
        TP = r_t[:].rearrange("p (s c q g) -> p (s c) q g", s=L, c=C, q=2)
        EC = r_bm0[:].rearrange("p (r d g s c) -> p r d g s c", r=2, d=2, g=GP // 2, s=L)
        h1 = r_bm1[:].rearrange("p (i d) -> p i d", i=TT)
        pw = r_bm1[:, 0:2048].rearrange("p (q r e) -> p q r e", q=2, r=2)
        craw = r_bm1[:, 4096:6144].rearrange("p (r d b n) -> p r d b n", r=2, d=2, b=4)
        braw = r_bm1[:, 2048:4096].rearrange("p (r d g c) -> p r d g c", r=2, d=2, g=GP)
        pre = r_bm1[0:2 * GP, 6144:6144 + 14 * P].rearrange("p (q n) -> p q n", q=14)
        pdt = r_bm1[0:2 * GP, 6144 + 14 * P:6144 + 14 * P + 4]
        bbar = r_u[:, 0:2048].rearrange("p (r d g c) -> p r d g c", r=2, d=2, g=GP)
        ksb = r_u[:, 2048:4096].rearrange("p (d c q g) -> p d c q g", d=2, c=C, q=2)
        uT = r_ssm[:].rearrange("p (m t) -> p m t", m=MT)
        U = r_u[:].rearrange("p (g k) -> p g k", g=G)
        Y = r_u[:].rearrange("p (j s g c) -> p j s g c", j=4, s=L, c=C)
        Z = r_u[:].rearrange("p (m t) -> p m t", m=MT)
        pd = r_pool[:].rearrange("p (m t) -> p m t", m=MT)
        FB = r_ssm[:, 2048:4096].rearrange("p (r g q c) -> p r g q c", r=2, g=GP, q=2)
        FC = r_c[:].rearrange("p (r d g c) -> p r d g c", r=2, d=2, g=GP)

        lag_rows = tmp[:].rearrange("p b t -> p (b t)")[:, 0:8 * P].rearrange("p (b t) -> p b t", b=8)

        ident_ready, edge_ready, ones_ready = sem("ident_ready"), sem("edge_ready"), sem("ones_ready")
        x_loaded = [sem(f"x_loaded{i}") for i in range(TT)]
        par_loaded, b_loaded, c_loaded = sem("par_loaded"), sem("b_loaded"), sem("c_loaded")
        vec_loaded = sem("vec_loaded")
        ring_loaded = [sem("ring_loaded0"), sem("ring_loaded1")]
        ring_used = sem("ring_used")
        xt_done = sem("xt_done")
        xt_act, xt_dve = sem("xt_act"), sem("xt_dve")
        pool_read = sem("pool_read")
        ssm_read = sem("ssm_read")
        u_stored, u_loaded = sem("u_stored"), sem("u_loaded")
        pre_act, pre_dve = sem("pre_act"), sem("pre_dve")
        pre_ready = sem("pre_ready")
        par_t, par_ready = sem("par_t"), sem("par_ready")
        ct_done, fc_ready, fb_clear, fb_ready = sem("ct_done"), sem("fc_ready"), sem("fb_clear"), sem("fb_ready")
        dve_chain = sem("dve_chain")
        bt_ready = sem("bt_ready")
        btt_done, bm_ready = sem("btt_done"), sem("bm_ready")
        lag_done, lag_mid, lag_t, lag_copied = sem("lag_done"), sem("lag_mid"), sem("lag_t"), sem("lag_copied")
        lag_stored, t_loaded = sem("lag_stored"), sem("t_loaded")
        pmix_done, pmix_ready = sem("pmix_done"), sem("pmix_ready")
        z_done, z_act, z_dve = sem("z_done"), sem("z_act"), sem("z_dve")
        scan_step, scan_ready = sem("scan_step"), sem("scan_ready")
        xr_loaded, w2_loaded, logit_read = sem("xr_loaded"), sem("w2_loaded"), sem("logit_read")
        wo_done, wo_read = sem("wo_done"), sem("wo_read")
        ec_pool, ec_dve = sem("ec_pool"), sem("ec_dve")
        pool_chain = sem("pool_chain")
        y_done, y_copied, yt_done = sem("y_done"), sem("y_copied"), sem("yt_done")
        skip_done, gelu_ready = sem("skip_done"), sem("gelu_ready")
        glu_done, sig_ready, glu_ready = sem("glu_done"), sem("sig_ready"), sem("glu_ready")
        ln_loaded, ln2_loaded = sem("ln_loaded"), sem("ln2_loaded")
        std_asked, std_ready = sem("std_asked"), sem("std_ready")
        h_ready, h_stored = sem("h_ready"), sem("h_stored")
        ht_done, ht_ready = sem("ht_done"), sem("ht_ready")
        logit_done = sem("logit_done")
        exp_asked, exp_ready = sem("exp_asked"), sem("exp_ready")
        onehot_ready, rank_done, table_ready, table_done = (
            sem("onehot_ready"), sem("rank_done"), sem("table_ready"), sem("table_done"))
        iota_ready, table_cleared = sem("iota_ready"), sem("table_cleared")
        pos_ready, table_written, slots_ready = sem("pos_ready"), sem("table_written"), sem("slots_ready")
        counts_ready = sem("counts_ready")
        wg_loaded = [sem(f"wg_loaded{c}") for c in range(WQ)]
        wu_loaded = [sem(f"wu_loaded{c}") for c in range(WQ)]
        wd_loaded = [sem(f"wd_loaded{c}") for c in range(WQ)]
        w_used = sem("w_used")
        sidx_ready = sem("sidx_ready")
        sel_ready, sel_lo, sel_hi = sem("sel_ready"), sem("sel_lo"), sem("sel_hi")
        xg_act, xg_dve = sem("xg_act"), sem("xg_dve")
        xg_t, xgT_act, xgT_dve = sem("xg_t"), sem("xgT_act"), sem("xgT_dve")
        gu_done, silu_ready, hid_ready = sem("gu_done"), sem("silu_ready"), sem("hid_ready")
        hid_t, hidT_ready = sem("hid_t"), sem("hidT_ready")
        down_done, ye_act, ye_dve, ye_stored = sem("down_done"), sem("ye_act"), sem("ye_dve"), sem("ye_stored")
        h_scaled, scale_ready, normed, gained = sem("h_scaled"), sem("scale_ready"), sem("normed"), sem("gained")
        pe_turn, pool_turn = sem("pe_turn"), sem("pool_turn")
        xs_loaded, xs_ready, xw_loaded, xg2_loaded = sem("xs_loaded"), sem("xs_ready"), sem("xw_loaded"), sem("xg2_loaded")
        xpe, xcopy = sem("xpe"), sem("xcopy")
        res_loaded = [sem(f"res_loaded{i}") for i in range(TT)]
        out_ready, out_stored = sem("out_ready"), sem("out_stored")

        w2 = [b[:, 0:8192].rearrange("p (k d) -> p k d", k=4) for b in (r_x, r_bm0)]
        wg = r_x[:, 0:8192].rearrange("p (k f) -> p k f", k=KT)
        wu = r_bm0[:].rearrange("p (k f) -> p k f", k=KT)
        wd = r_t[:].rearrange("p (k d) -> p k d", k=FT)
        ln1g = r_c[:]
        ln1b = r_pool[:, 0:2048]
        rw = r_pool[:, 2048:2048 + KT * (NG + NE)].rearrange("p (k e) -> p k e", k=KT)
        rbias = r_pool[:, 2700:2700 + NG + NE]
        hT = ring[:].rearrange("p b (k t) -> p b k t", k=KT)
        ln2g, ln2b = ring[:, 0, :], ring[:, 1, :]
        xg = r_u[:, 0:D // 2]
        xg_rows = r_u[0:SLOTS, 0:D]
        pick = [r_u[:, D + b * TT * SLOTS:D + (b + 1) * TT * SLOTS].rearrange("p (i t) -> p i t", i=TT)
               for b in range(2)]
        place = r_u[:, D + 2 * TT * SLOTS:D + 2 * TT * SLOTS + TT * NE].rearrange("p (i e) -> p i e", i=TT)
        yb = [r_pool[:, 0:1024], r_pool[:, 1024:2048]]
        sil = r_pool[0:SLOTS, 2048:2560]
        hid = r_pool[0:SLOTS, 2560:3072]
        hidT = r_pool[:, 3072:3072 + FT * SLOTS].rearrange("p (k t) -> p k t", k=FT)
        route = r_ssm
        xgT = [tmp[:].rearrange("p b t -> p (b t)")[:, 0:KT * SLOTS].rearrange("p (k t) -> p k t", k=KT),
               r_c[:, 0:KT * SLOTS].rearrange("p (k t) -> p k t", k=KT)]
        res = [r_x[:, 0:4096], r_x[:, 4096:8192], r_bm0[:, 0:4096], r_bm0[:, 4096:8192]]

        at = [0]

        def small(n, dt=F32):
            v = route[:, at[0]:at[0] + n]
            at[0] += n
            return v if dt is F32 else v.bitcast(dt)

        E1 = NG + NE
        lg = small(TT * E1).rearrange("p (i e) -> p i e", i=TT)
        gmax, gsum, pgrp, vmax = (small(TT) for _ in range(4))
        gd, ge, gv, gm = (small(TT * NG).rearrange("p (i e) -> p i e", i=TT) for _ in range(4))
        prod = small(TT * NE).rearrange("p (i g j) -> p i g j", i=TT, g=NG)
        prod2 = small(TT * NE).rearrange("p (i e) -> p i e", i=TT)
        sel = small(TT * EPG).rearrange("p (i j) -> p i j", i=TT)
        top = small(TT * 8).rearrange("p (i j) -> p i j", i=TT)
        topi = small(TT * 8, U32).rearrange("p (i j) -> p i j", i=TT)
        topf = small(TT * 8).rearrange("p (i j) -> p i j", i=TT)
        gap, egap, epl = small(TT), small(TT), small(TT)
        gate = small(2 * TT).rearrange("p (k i) -> p k i", k=2)
        eid = small(2 * TT).rearrange("p (k i) -> p k i", k=2)
        onek = small(2 * TT * NE).rearrange("p (k i e) -> p k i e", k=2, i=TT)
        one = small(TT * NE).rearrange("p (i e) -> p i e", i=TT)
        one_sum = small(NE)
        gbase = small(TT)
        rank_row = small(TT * NE).rearrange("p (i e) -> p i e", i=TT)
        pos = small(2 * TT).rearrange("p (k i) -> p k i", k=2)
        pos_i = small(2 * TT, I32).rearrange("p (k i) -> p k i", k=2)
        val_i = small(2 * TT, I32).rearrange("p (i k) -> p i k", k=2)
        val_f = small(2 * TT).rearrange("p (i k) -> p i k", k=2)
        iota_m = small(P)
        rank_k = small(2 * TT).rearrange("p (k i) -> p k i", k=2)
        rank_eq = small(2 * TT * P).rearrange("p (k i m) -> p k i m", k=2, i=TT)
        val_e = small(2 * TT * NE).rearrange("p (k i e) -> p k i e", k=2, i=TT)
        iota_e = small(NE)
        iota_g = small(NG)
        tri = small(P)
        ones = small(P)
        cnt = small(NE)
        cnt_i = small(NE, I32)
        extra_flag = small(ROUNDS * NE)
        extra_scan = small(ROUNDS * NE)
        extra_no = small(ROUNDS * NE, I32)
        max_i = small(1, I32)
        max_f = small(1)
        slot_i = small(NE, I32)
        slot_s = small(NE, I32)
        iota_s = small(SLOTS)
        half = small(1)
        sidx = small(2, I32)
        xslot, xgi, xsi = small(1, I32), small(1, I32), small(1, I32)
        stats = small(4 * 6).rearrange("p (q s) -> p q s", q=4)
        lnt = small(8 * TT).rearrange("p (i s) -> p i s", i=TT)
        empties = small(P, I32)
        assert at[0] <= 4096

        def group(gp, q):
            return 16 * (gp // 8) + 8 * q + gp % 8

        def c_powers(eng, link, gs, T, ready):
            n = gs.stop - gs.start
            es = slice(gs.start % (GP // 2), gs.start % (GP // 2) + n)
            sh4 = [P, 2, n, C]
            T2 = T[:, 0:2 * n * C].rearrange("p (r g c) -> p r g c", r=2, c=C)
            for d in range(2):
                a_r = par[:, 0, d, gs].unsqueeze(1).unsqueeze(3).to_broadcast(sh4)
                a_i = par[:, 1, d, gs].unsqueeze(1).unsqueeze(3).to_broadcast(sh4)
                slot = (lambda q: q - 1) if d == 0 else (lambda q: L - q)
                for q in range(1, L + 1):
                    v = FC[:, :, d, gs, :] if q == 1 else EC[:, :, d, es, slot(q - 1), :]
                    e = EC[:, :, d, es, slot(q), :]
                    eng.tensor_tensor(e, v, a_r, ALU.mult)
                    link(eng.tensor_tensor(T2, v, a_i, ALU.mult))
                    eng.tensor_tensor(e[:, 0], e[:, 0], T2[:, 1], ALU.add)
                    last = eng.tensor_tensor(e[:, 1], e[:, 1], T2[:, 0], ALU.subtract)
                    if not (d == 1 and q == L):
                        link(last)
            last.then_inc(ready, 1)

        DVE_PAIRS = slice(GP // 2, GP // 2 + 11)
        POOL_PAIRS = slice(GP // 2 + 11, GP)

        block = ctx.enter_context(nc.Block())

        def ring_view(b, k, n):
            return ring[:, b, 0:k * n].rearrange("p (k n) -> p k n", k=k)

        w_in_v = w_in.rearrange("(k p) c -> p k c", p=P)
        N_IN = KT
        N_WO = 2 * NN
        FIRST_WO = N_IN + 1
        FIRST_GLU = FIRST_WO + N_WO
        N_GLU = MT // 2
        END = FIRST_GLU + N_GLU

        def ring_source(n):
            b = n % 2
            if n == N_IN:
                return (ring[:, b, :].rearrange("p (q d) -> p q d", d=256),
                        pool_w.rearrange("g (k p) d -> p (g k) d", p=P))
            if FIRST_GLU <= n:
                j = n - FIRST_GLU
                return ring_view(b, MT, 256), glu_w.rearrange("(k p) c -> p k c", p=P)[:, :, 256 * j:256 * j + 256]
            col, part = (n - FIRST_WO) // 2, (n - FIRST_WO) % 2
            rows = w_out[part * NCOL:(part + 1) * NCOL, NCOL * col:NCOL * col + NCOL]
            return ring_view(b, 4, NCOL), rows.rearrange("(k p) c -> p k c", p=P)

        def expert_quarter(m, e, c):
            w, t, k = ((w_gate, wg, KT), (w_up, wu, KT), (w_down, wd, FT))[m]
            q = k // WQ
            src = w[bass.ds(e, 1)].rearrange("o (p k) f -> p (o k) f", k=k)[:, c * q:(c + 1) * q, :]
            return t[:, c * q:(c + 1) * q, :], src

        ORDER = [(m, c) for c in range(WQ) for m in (0, 1)] + [(2, c) for c in range(WQ)]
        LOADED = (wg_loaded, wu_loaded, wd_loaded)

        @block.sync
        def _(sp):
            for i in range(TT):
                sp.dma_start(xrows[:, i, :], x[i * P:(i + 1) * P, :]).then_inc(x_loaded[i], 16)
            for b in range(2):
                sp.dma_start(ring_view(b, KT, P), w_in_v[:, :, b * P:(b + 1) * P]).then_inc(ring_loaded[b], 16)
            with sp.Fori(1, N_IN // 2) as i:
                for b in range(2):
                    sp.wait_ge(ring_used, 2 * i + (b - 1))
                    sp.dma_start(ring_view(b, KT, P), w_in_v[:, :, bass.ds(i * (2 * P) + b * P, P)]
                                 ).then_inc(ring_loaded[b], 16)
            for n in range(N_IN, END):
                sp.wait_ge(ring_used, n - 1)
                dst, src = ring_source(n)
                sp.dma_start(dst, src).then_inc(ring_loaded[n % 2], 16)
                if n == FIRST_WO + 1:
                    sp.wait_ge(z_done, GP // 2)
                    sp.dma_start(h1[:, :, :], x.rearrange("(i p) d -> p i d", p=P)).then_inc(xr_loaded, 16)
                if n == FIRST_GLU + 1:
                    sp.wait_ge(y_done, 4)
                if n >= FIRST_GLU + 1:
                    for k in range(4 * (n - FIRST_GLU - 1), min(4 * (n - FIRST_GLU), MT)):
                        sp.dma_start(w2[k // 4][:, k % 4, :], w_out[CH + k * P:CH + (k + 1) * P, :]
                                     ).then_inc(w2_loaded, 16)
            first = [(2, c) for c in range(WQ)] + [mc for mc in ORDER if mc[0] != 2]
            for j, (m, c) in enumerate(first):
                if j == WQ:
                    sp.wait_ge(wo_done, NN + TT)
                dst, src = expert_quarter(m, 0, c)
                sp.dma_start(dst, src).then_inc(LOADED[m][c], 16)
            sp.wait_ge(h_ready, TT)
            sp.dma_start(h_dram[(TT - 1) * P:TT * P, :], h1[:, TT - 1, :]).then_inc(h_stored, 16)
            sp.wait_ge(logit_done, TT)
            sp.dma_start(ln2g, ln2_g.partition_broadcast(P)).then_inc(ln2_loaded, 16)
            sp.dma_start(ln2b, ln2_b.partition_broadcast(P)).then_inc(ln2_loaded, 16)
            with sp.Fori(1, NE) as e:
                for j, (m, c) in enumerate(ORDER):
                    sp.wait_ge(w_used, e * 12 + (j + 1 - 12))
                    dst, src = expert_quarter(m, e, c)
                    sp.dma_start(dst, src).then_inc(LOADED[m][c], 16)
            sp.wait_ge(counts_ready, 1)
            sp.wait_ge(w_used, 12 * NE)
            with sp.If(sp.value_load(max_i[0:1, 0:1], min_val=0, max_val=S) > SLOTS):
                sp.wait_ge(table_written, 16 * 2 * TT)
                with sp.Fori(1, ROUNDS) as r:
                    with sp.Fori(0, NE) as e:
                        with sp.If(sp.value_load(cnt_i[0:1, bass.ds(e, 1)], min_val=0, max_val=S) > r * SLOTS):
                            no = sp.value_load(extra_no[0:1, bass.ds(r * NE + e, 1)], min_val=0, max_val=16)
                            sp.wait_ge(ye_stored, no * 16 + 16 * NE)
                            for h in range(2):
                                sp.dma_start(xslot[h * SLOTS:(h + 1) * SLOTS, :],
                                             slot_dram.rearrange("(r e) o -> r (e o)", e=NE)[
                                                 bass.ds(r * SLOTS, SLOTS), bass.ds(e, 1)],
                                             allow_slow_non_contiguous=True).then_inc(xs_loaded, 16)
                            for m in range(3):
                                w, t, k = ((w_gate, wg, KT), (w_up, wu, KT), (w_down, wd, FT))[m]
                                sp.dma_start(t, w[bass.ds(e, 1)].rearrange("o (p k) f -> p (o k) f", k=k)
                                             ).then_inc(xw_loaded, 16)
            n_extra = sp.value_load(extra_no[0:1, 0:1], min_val=0, max_val=16)
            sp.wait_ge(ye_stored, n_extra * 16 + 16 * NE)
            for i in range(TT):
                sp.dma_start(res[i].rearrange("p (k d) -> p k d", k=2),
                             ye_dram.rearrange("(i p k h) d -> i p k (h d)", i=TT, p=P, k=2)[i]
                             ).then_inc(res_loaded[i], 16)
            for i in range(TT):
                sp.wait_ge(out_ready, i + 1)
                sp.dma_start(out[i * P:(i + 1) * P, :], h1[:, i, :]).then_inc(out_stored, 16)
            sp.wait_ge(out_stored, 16 * TT)

        @block.gpsimd
        def _(pool):
            pool.memset(ident[:], 0.0).then_inc(ident_ready, 1)
            pool.wait_ge(ident_ready, 1)
            pool.affine_select(out=ident[:], in_=ident[:], compare_op=ALU.not_equal, fill=1.0, base=0,
                               pattern=[[-1, P]], channel_multiplier=1).then_inc(ident_ready, 1)
            for q, w in enumerate(WINDOWS):
                for j in range(w // 2):
                    pool.memset(edge[:, q, j:j + 1], w / (w // 2 + j))
                for j in range(1, w // 2):
                    at_col = w // 2 + (w // 2 - 1 - j)
                    pool.memset(edge[:, q, at_col:at_col + 1], w / (w // 2 + j))
            pool.memset(neg_one[:], -1.0).then_inc(edge_ready, 1)
            lags = lambda d: ksb[:, d].rearrange("p c q g -> p (c q g)")
            pool.wait_ge(lag_copied, 1)
            pool.dma_start(lag_dram[L * C:(2 * L - 1) * C, :], lags(0)[C:P, :]).then_inc(lag_stored, 16)
            pool.wait_ge(lag_copied, 2)
            pool.dma_start(lag_dram[0:L * C, :], lags(1)).then_inc(lag_stored, 16)
            pool.wait_ge(lag_stored, 32)
            pool.dma_start(lag_dram[(L - 1) * C:L * C, :], ksb[0:C, 0].rearrange("p c q g -> p (c q g)"),
                           accum_op=ALU.add).then_inc(lag_stored, 16)

            links = [0]

            def link(ins):
                links[0] += 1
                ins.then_inc(pool_chain, 1)
                pool.wait_ge(pool_chain, links[0])

            pool.wait_ge(par_ready, 1)
            pool.wait_ge(fc_ready, 4)
            pool.wait_ge(z_done, GP // 2)
            c_powers(pool, link, slice(0, GP // 2), tmp[:, 1, :], ec_pool)
            pool.wait_ge(y_done, 2)
            pool.wait_ge(ec_pool, 1)
            c_powers(pool, link, POOL_PAIRS, tmp[:, 1, :], ec_pool)

            pool.wait_ge(glu_ready, MT)
            pool.memset(tri, 0.0)
            pool.memset(ones, 1.0)
            pool.iota(iota_e, [[1, NE]], base=0, channel_multiplier=0, allow_small_or_imprecise_dtypes=True)
            pool.iota(iota_g, [[-1, NG]], base=NG, channel_multiplier=0, allow_small_or_imprecise_dtypes=True)
            pool.iota(val_i, [[2 * P, TT], [1, 2]], base=0, channel_multiplier=2)
            pool.iota(val_f, [[2 * P, TT], [1, 2]], base=-EMPTY, channel_multiplier=2,
                      allow_small_or_imprecise_dtypes=True)
            pool.iota(iota_m, [[0, 2], [1, SLOTS]], base=0, channel_multiplier=0, allow_small_or_imprecise_dtypes=True)
            pool.iota(iota_s, [[1, SLOTS]], base=1, channel_multiplier=0, allow_small_or_imprecise_dtypes=True)
            pool.memset(half, 0.0)
            pool.memset(empties, EMPTY).then_inc(iota_ready, 1)
            pool.wait_ge(iota_ready, 1)
            pool.affine_select(out=tri, in_=tri, compare_op=ALU.is_ge, fill=1.0, base=0,
                               pattern=[[-1, P]], channel_multiplier=1)
            pool.affine_select(out=half, in_=half, compare_op=ALU.is_gt, fill=1.0, base=SLOTS,
                               pattern=[[0, 1]], channel_multiplier=-1).then_inc(iota_ready, 1)
            def scatter(b, ready, idx):
                pool.indirect_dma_start(
                    out=ye_dram, out_offset=bass.IndirectOffsetOnAxis(ap=idx, axis=0),
                    in_=yb[b], in_offset=None, bounds_check=4 * S - 1, oob_is_err=False).then_inc(ready, 16)

            pool.wait_ge(slots_ready, 1)

            def results(n, b, after):
                if after:
                    pool.wait_ge(ye_stored, n * 16)
                pool.tensor_copy(sidx[:, b:b + 1], slot_s[:, bass.ds(n, 1)]).then_inc(sidx_ready, 1)
                pool.wait_ge(sidx_ready, n + 1)
                pool.wait_ge(ye_act, n + 1)
                pool.wait_ge(ye_dve, n + 1)
                pool.nop().then_inc(pool_turn, 1)
                scatter(b, ye_stored, sidx[:, b:b + 1])

            results(0, 0, False)
            results(1, 1, True)
            with pool.Fori(1, NE // 2) as i:
                for b in range(2):
                    results(i * 2 + b, b, True)
            pool.wait_ge(ye_stored, 16 * NE)
            pool.wait_ge(counts_ready, 1)
            with pool.If(pool.value_load(max_i[0:1, 0:1], min_val=0, max_val=S) > SLOTS):
                pool.dma_start(slot_dram.rearrange("(p n) o -> p (n o)", p=P), empties).then_inc(table_cleared, 16)
                pool.wait_ge(table_cleared, 16)
                pool.wait_ge(pos_ready, 1)
                for k in range(2):
                    for i in range(TT):
                        pool.indirect_dma_start(
                            out=slot_dram, out_offset=bass.IndirectOffsetOnAxis(ap=pos_i[:, k, i:i + 1], axis=0),
                            in_=val_i[:, i, k:k + 1], in_offset=None).then_inc(table_written, 16)
                pool.wait_ge(h_stored, 16 * TT)
                with pool.Fori(1, ROUNDS) as r:
                    with pool.Fori(0, NE) as e:
                        with pool.If(pool.value_load(cnt_i[0:1, bass.ds(e, 1)], min_val=0, max_val=S) > r * SLOTS):
                            no = pool.value_load(extra_no[0:1, bass.ds(r * NE + e, 1)], min_val=0, max_val=16)
                            pool.wait_ge(xs_ready, no + 1)
                            pool.nop().then_inc(pool_turn, 1)
                            pool.indirect_dma_start(
                                out=xg_rows, out_offset=None, in_=h_dram,
                                in_offset=bass.IndirectOffsetOnAxis(ap=xgi[0:SLOTS, :], axis=0),
                                bounds_check=S - 1, oob_is_err=False).then_inc(xg2_loaded, 16)
                            pool.wait_ge(xcopy, no * 5 + 5)
                            pool.nop().then_inc(pool_turn, 1)
                            scatter(0, ye_stored, xsi)

            pool.wait_ge(ln2_loaded, 32)
            for i in range(TT):
                pool.wait_ge(gained, i + 1)
                pool.tensor_tensor(h1[:, i, :], h1[:, i, :], ln2b, ALU.add).then_inc(out_ready, 1)

        @block.scalar
        def _(act):
            for q in range(2):
                for j, v in enumerate((a_re, a_im)):
                    act.dma_start(pre[:, j, q * NST:(q + 1) * NST],
                                  v.rearrange("d (j q b) n -> q (d j) b n", q=2, b=8)[q]).then_inc(par_loaded, 16)
                act.dma_start(pdt[:, q:q + 1], log_dt.rearrange("d (j q b) -> q (d j) b", q=2, b=8)[q].unsqueeze(2),
                              allow_slow_non_contiguous=True).then_inc(par_loaded, 16)
            for i in range(TT):
                for j in range(0, 4, 2):
                    act.wait_ge(xt_done, 4 * i + j + 1)
                    act.copy(xT[:, 4 * j:4 * j + 4, i * P:(i + 1) * P],
                             PS[:, j, :].rearrange("p (k t) -> p k t", k=4)).then_inc(xt_act, 1)
            act.wait_ge(par_loaded, 96)
            act.activation(pdt[:, 2:4], pdt[:, 0:2], ACT.Exp).then_inc(pre_act, 1)
            act.wait_ge(pre_dve, 1)
            act.activation(pre[:, 4, :], pre[:, 2, :], ACT.Exp).then_inc(pre_act, 1)
            act.wait_ge(pre_dve, 2)
            act.activation(pre[:, 5, :], pre[:, 3, :], ACT.Sin).then_inc(pre_act, 1)
            act.activation(pre[:, 6, :], pre[:, 7, :], ACT.Sin).then_inc(pre_act, 1)
            for r, bsrc in enumerate((b_re, b_im)):
                for d in range(2):
                    for q in range(2):
                        for j in range(4):
                            act.dma_start(braw[q * NST:(q + 1) * NST, r, d, 8 * j:8 * j + 8, :],
                                          bsrc[d].rearrange("(j q b) n c -> j q n b c", q=2, b=8)[j, q]
                                          ).then_inc(b_loaded, 16)
            for r, csrc in enumerate((c_re, c_im)):
                for d in range(2):
                    for blk in range(4):
                        for q in range(2):
                            src = csrc[d].rearrange("(b q g) c n -> b q (g c) n", b=4, q=2)[blk, q]
                            act.dma_start(craw[:, r, d, blk, q * NST:(q + 1) * NST], src).then_inc(c_loaded, 16)
            with nc.allow_non_contiguous_dma(reason="a few vectors, one value per partition"):
                for j, v in enumerate((pool_scale, ssm_d, glu_b)):
                    act.dma_start(vecs[:, j, :], v.rearrange("(m p) -> p m", p=P)).then_inc(vec_loaded, 16)
            for j, (r, d) in enumerate(((0, 0), (0, 1), (1, 0), (1, 1))):
                act.wait_ge(ct_done, j + 1)
                act.activation(FC[:, r, d, :, :].rearrange("p g c -> p (g c)"), PS[:, j, :], ACT.Copy,
                               scale=1.0 if r == 0 else -1.0).then_inc(fc_ready, 1)

            def b_matrices(d):
                for j in range(GP // 2):
                    act.wait_ge(btt_done, d * (GP // 2) + j + 1)
                    act.copy(BM[d][:, 2 * j:2 * j + 2, :, :].rearrange("p g r m -> p (g r m)"), PS[:, j % 4, :]
                             ).then_inc(bm_ready, 1)

            def ssm_tile(m, b):
                act.wait_ge(ring_used, MT + 1 + m)
                act.activation(uT[:, bass.ds(m, 1), :].rearrange("p o (s k) -> p (o s) k", s=L),
                               PS[:, 4 + b, :].rearrange("p (k s) -> p s k", s=L), ACT.Copy).then_inc(ssm_read, 1)
                act.wait_ge(ssm_read, m + 1)
                act.dma_start(u_dram[bass.ds(m * P, P), :, :].rearrange("p s k -> p (s k)"),
                              uT[:, bass.ds(m, 1), :].rearrange("p o t -> p (o t)")).then_inc(u_stored, 16)

            b_matrices(0)
            with act.Fori(0, 2) as i:
                for b in range(2):
                    ssm_tile(i * 2 + b, b)
            b_matrices(1)
            with act.Fori(2, 4) as i:
                for b in range(2):
                    ssm_tile(i * 2 + b, b)
            act.wait_ge(u_stored, 16 * MT)
            act.wait_ge(lag_stored, 48)
            for s in range(L):
                j = L - 1 - s
                act.dma_start(U[j * C:(j + 1) * C, :, :], u_dram.rearrange("(g c) s k -> s c g k", c=C)[s]
                              ).then_inc(u_loaded, 16)
            act.dma_start(r_t[:].rearrange("p (s n) -> p s n", s=L), bass.AP(tensor=lag_dram.tensor, offset=0,
                                               ap=[[G * C, P], [C * G * C, L], [1, G * C]])).then_inc(t_loaded, 16)
            for g in range(len(WINDOWS)):
                act.wait_ge(pmix_done, g + 1)
                if g == 0:
                    act.wait_ge(vec_loaded, 48)
                for h in range(PGT):
                    m = g * PGT + h
                    act.activation(pd[:, m, :], PS[:, 2 * (g % 2) + h, :], ACT.Copy,
                                   scale=vecs[:, 0, m:m + 1]).then_inc(pmix_ready, 1)
            for j in range(0, GP // 2, 2):
                act.wait_ge(z_done, j + 1)
                for d in range(2):
                    src = PS[:, 4 + j % 4, :].rearrange("p (g r d k) -> p d k r g", g=2, r=2, d=2)[:, d]
                    act.activation(st[:, 1 - d:NCH + 1 - d, :, d, 2 * j:2 * j + 2], src, ACT.Copy).then_inc(z_act, 1)
            for j in range(4):
                act.wait_ge(y_done, j + 1)
                for h in range(2):
                    act.activation(Y[:, j, :, 4 * h:4 * h + 4, :].rearrange("p s g c -> p g s c"),
                                   PS[:, 4 + 2 * (j % 2) + h, :].rearrange("p (g s c) -> p g s c", s=L, c=C), ACT.Copy
                                   ).then_inc(y_copied, 1)
                if j % 2 == 1:
                    for m in range(4 * (j // 2), 4 * (j // 2) + 4):
                        act.wait_ge(skip_done, m + 1)
                        act.activation(uT[:, m, :], uT[:, m, :], ACT.Gelu_apprx_tanh).then_inc(gelu_ready, 1)
            act.wait_ge(ec_pool, 2)
            act.wait_ge(ec_dve, 1)
            act.dma_start(ln1g, ln1_g.partition_broadcast(P)).then_inc(ln_loaded, 16)
            act.wait_ge(wo_done, NN)
            act.dma_start(ln1b, ln1_b.partition_broadcast(P)).then_inc(ln_loaded, 16)
            act.dma_start(rw[:, :, 0:NG], rg_w.rearrange("(k p) e -> p k e", p=P)).then_inc(ln_loaded, 16)
            act.dma_start(rw[:, :, NG:E1], re_w.rearrange("(k p) e -> p k e", p=P)).then_inc(ln_loaded, 16)
            act.dma_start(rbias[:, 0:NG], rg_b.partition_broadcast(P)).then_inc(ln_loaded, 16)
            act.dma_start(rbias[:, NG:E1], re_b.partition_broadcast(P)).then_inc(ln_loaded, 16)
            for m in range(MT):
                act.wait_ge(glu_done, m + 1)
                if m >= 2:
                    act.wait_ge(glu_ready, m - 1)
                act.activation(tmp[:, m % 2, 0:S], PS[:, m % 2, :], ACT.Sigmoid, bias=vecs[:, 2, m:m + 1]
                               ).then_inc(sig_ready, 1)
            def router_rows(i):
                for j in range(4):
                    act.wait_ge(ht_done, 4 * i + j + 1)
                    act.copy(hT[:, i % 2, 4 * j:4 * j + 4, :].rearrange("p k t -> p (k t)"),
                             PS[:, 4 - 4 * (i % 2) + j, :]).then_inc(ht_ready, 1)

            def router_logits(i):
                act.wait_ge(logit_done, i + 1)
                act.copy(lg[:, i, :], PS[:, 4 - 4 * (i % 2), 0:E1]).then_inc(logit_read, 1)

            for i in range(TT + 1):
                if i >= 1:
                    router_rows(i - 1)
                if i < TT:
                    act.wait_ge(std_asked, i + 1)
                    act.activation(lnt[:, 0, 1:2], lnt[:, 0, 0:1], ACT.Sqrt).then_inc(std_ready, 1)
                if i >= 1:
                    router_logits(i - 1)
                if i < TT - 1:
                    act.wait_ge(h_ready, i + 1)
                    act.dma_start(h_dram[i * P:(i + 1) * P, :], h1[:, i, :]).then_inc(h_stored, 16)
            act.wait_ge(exp_asked, 1)
            act.activation(ge[:], gd[:], ACT.Exp).then_inc(exp_ready, 1)
            act.wait_ge(exp_asked, 2)
            act.activation(egap, gap, ACT.Exp).then_inc(exp_ready, 1)

            def rows_copied(n):
                act.wait_ge(sel_lo, n + 1)
                act.copy(xg[:, 0:NCOL], PS[:, 1, :]).then_inc(xg_act, 1)

            def rows_T_copied(n, b):
                act.wait_ge(xg_t, n + 1)
                act.copy(xgT[b][:, 0:8, :].rearrange("p k t -> p (k t)"), PS[:, 2, :]).then_inc(xgT_act, 1)

            def expert(n, b, after, last_pass=False):
                act.wait_ge(gu_done, n + 1)
                if after:
                    act.wait_ge(hid_ready, n)
                act.activation(sil, PS[0:SLOTS, 0, :], ACT.Silu).then_inc(silu_ready, 1)
                if not last_pass:
                    rows_copied(n + 1)
                    rows_T_copied(n + 1, 1 - b)
                act.wait_ge(down_done, n + 1)
                if after == 2:
                    act.wait_ge(ye_stored, n * 16 - 16)
                act.copy(yb[b][:, 0:NCOL], PS[:, 5, :]).then_inc(ye_act, 1)

            rows_copied(0)
            rows_T_copied(0, 0)
            expert(0, 0, 0)
            expert(1, 1, 1)
            with act.Fori(1, NE // 2 - 1) as i:
                for b in range(2):
                    expert(i * 2 + b, b, 2)
            expert(NE - 2, 0, 2)
            expert(NE - 1, 1, 2, True)
            act.wait_ge(counts_ready, 1)
            with act.If(act.value_load(max_i[0:1, 0:1], min_val=0, max_val=S) > SLOTS):
                with act.Fori(1, ROUNDS) as r:
                    with act.Fori(0, NE) as e:
                        with act.If(act.value_load(cnt_i[0:1, bass.ds(e, 1)], min_val=0, max_val=S) > r * SLOTS):
                            no = act.value_load(extra_no[0:1, bass.ds(r * NE + e, 1)], min_val=0, max_val=16)
                            act.wait_ge(xpe, no * 4 + 2)
                            act.wait_ge(xcopy, no * 5 + 1)
                            act.activation(sil, PS[0:SLOTS, 0, :], ACT.Silu).then_inc(xcopy, 1)
            def normalise(i):
                act.wait_ge(scale_ready, i + 1)
                act.activation(h1[:, i, :], h1[:, i, :], ACT.Identity, scale=lnt[:, i, 2:3], bias=lnt[:, i, 6:7]
                               ).then_inc(normed, 1)

            for i in range(TT):
                act.wait_ge(std_asked, TT + i + 1)
                act.activation(lnt[:, i, 1:2], lnt[:, i, 0:1], ACT.Sqrt).then_inc(std_ready, 1)
                if i >= 1:
                    normalise(i - 1)
            normalise(TT - 1)

        @block.tensor
        def _(pe):
            pe.wait_ge(ident_ready, 2)
            for i in range(TT):
                pe.wait_ge(x_loaded[i], 16)
                for j in range(4):
                    if i >= 1:
                        pe.wait_ge((xt_act, xt_dve)[j % 2], 2 * (i - 1) + j // 2 + 1)
                    for k in range(4):
                        kt = 4 * j + k
                        last = pe.transpose(PS[:, j, k * P:(k + 1) * P], xrows[:, i, kt * P:(kt + 1) * P], ident[:])
                    last.then_inc(xt_done, 1)
            pe.wait_ge(xt_act, KT // 2)
            pe.wait_ge(xt_dve, KT // 2)

            def project(i, b):
                pe.wait_ge(ring_loaded[b], i * 16 + 16)
                for kt in range(KT):
                    last = pe.matmul(PS[:, 4 + b, :], ring_view(b, KT, P)[:, kt, :], xT[:, kt, :],
                                     start=kt == 0, stop=kt == KT - 1)
                last.then_inc(ring_used, 1)

            def b_side(d):
                pe.wait_ge(bt_ready, d + 1)
                pe.wait_ge(fb_ready, d + 1)
                if d == 0:
                    pe.wait_ge(par_ready, 1)
                else:
                    pe.wait_ge(lag_copied, 1)
                for b in range(GP // 4):
                    for r in range(2):
                        for a in range(4):
                            g = 4 * b + a
                            last = pe.matmul(PS[a * 2 * C:(a + 1) * 2 * C, 6 + b // 4, (b % 4) * P:(b % 4 + 1) * P],
                                             FB[:, r, g, :, :].rearrange("p q c -> p (q c)"),
                                             BT[:, r, g, :, :].rearrange("p s c -> p (s c)"),
                                             start=r == 0, stop=r == 1, skip_group_check=True)
                last.then_inc(lag_done, 1)
                pe.wait_ge(fc_ready, 4)
                for j in range(GP // 2):
                    if j >= 4 or d == 1:
                        pe.wait_ge(bm_ready, d * (GP // 2) + max(j - 4, -1) + 1)
                    for g in range(2):
                        for r in range(2):
                            last = pe.transpose(PS[:, j % 4, (2 * g + r) * P:(2 * g + r + 1) * P],
                                                BT[:, r, 2 * j + g, :, :].rearrange("p s c -> p (s c)"), ident[:])
                    last.then_inc(btt_done, 1)
                pe.wait_ge(lag_mid, d + 1)
                for b in range(GP // 4):
                    last = pe.transpose(PS[:, 6 + b // 4, (b % 4) * P:(b % 4 + 1) * P], lag_rows[:, b, :], ident[:])
                last.then_inc(lag_t, 1)

            project(0, 0)
            project(0, 1)
            pe.wait_ge(pre_ready, 1)
            for j in range(4):
                last = pe.transpose(PS[:, 6, j * 64:(j + 1) * 64], pre[:, 10 + j, :], ident[0:2 * GP, 0:2 * GP])
            last.then_inc(par_t, 1)
            for b in range(2):
                pe.wait_ge(pool_read, 1 + b)
                project(1, b)
            pe.wait_ge(c_loaded, 16 * 32)
            for j, (r, d) in enumerate(((0, 0), (0, 1), (1, 0), (1, 1))):
                for blk in range(4):
                    last = pe.transpose(PS[:, j, blk * P:(blk + 1) * P], craw[:, r, d, blk, :], ident[:])
                last.then_inc(ct_done, 1)
            with pe.Fori(2, 4) as i:
                for b in range(2):
                    pe.wait_ge(pool_read, i * 2 + (b - 1))
                    project(i, b)
            b_side(0)
            for b in range(2):
                pe.wait_ge(pool_read, MT - 1 + b)
                project(4, b)
            with pe.Fori(5, 6) as i:
                for b in range(2):
                    pe.wait_ge(ssm_read, i * 2 + (b - 1 - MT))
                    project(i, b)
            b_side(1)
            with pe.Fori(6, 8) as i:
                for b in range(2):
                    pe.wait_ge(ssm_read, i * 2 + (b - 1 - MT))
                    project(i, b)

            pe.wait_ge(ring_loaded[0], 16 * (N_IN // 2 + 1))
            pe.wait_ge(bm_ready, GP)
            pe.wait_ge(pool_read, MT)
            for g in range(len(WINDOWS)):
                if g >= 2:
                    pe.wait_ge(pmix_ready, 2 * (g - 1))
                for h in range(PGT):
                    for k in range(PGT):
                        last = pe.matmul(PS[:, 2 * (g % 2) + h, :],
                                         ring[:, 0, :].rearrange("p (q d) -> p q d", d=256)[:, 2 * g + k, h * P:(h + 1) * P],
                                         pd[:, 2 * g + k, :], start=k == 0, stop=k == 1)
                last.then_inc(pmix_done, 1)

            pe.wait_ge(u_loaded, 16 * L)
            pe.wait_ge(ssm_read, MT)
            pe.wait_ge(lag_copied, 2)
            for j in range(GP // 2):
                if j >= 4:
                    pe.wait_ge((z_act, z_dve)[j % 2], 2 * ((j - 4) // 2) + 2)
                for g in range(2):
                    for r in range(2):
                        for d in range(2):
                            for q in range(2):
                                gp = 2 * j + g
                                col = ((g * 2 + r) * 2 + d) * NCH
                                last = pe.matmul(PS[q * NST:(q + 1) * NST, 4 + j % 4, col:col + NCH],
                                                 BM[d][:, gp, r, q * NST:(q + 1) * NST], U[:, group(gp, q), :],
                                                 start=True, stop=True)
                last.then_inc(z_done, 1)

            def out_pool(n, bank):
                for part in range(2):
                    slot = FIRST_WO + 2 * n + part
                    pe.wait_ge(ring_loaded[slot % 2], 16 * (slot // 2 + 1))
                    for k in range(4):
                        for i in range(TT):
                            last = pe.matmul(PS[:, bank + i, :], pd[:, 4 * part + k, i * P:(i + 1) * P],
                                             ring_view(slot % 2, 4, NCOL)[:, k, :],
                                             start=(part == 0 and k == 0), stop=(part == 1 and k == 3))
                    if part == 0:
                        last.then_inc(ring_used, 1)
                    else:
                        last.then_inc(wo_done, 1)
                pe.wait_ge(wo_done, n + 1)
                pe.nop().then_inc(ring_used, 1)

            def outputs(j):
                for h in range(2):
                    bank = 4 + 2 * (j % 2) + h
                    for g in range(4):
                        gp = 8 * j + 4 * h + g
                        for q in range(2):
                            pe.matmul(PS[q * NCH:(q + 1) * NCH, bank, g * P:(g + 1) * P], U[:, group(gp, q), :],
                                      TP[:, :, q, gp], start=g == 0, stop=False, skip_group_check=True)
                    for g in range(4):
                        gp = 8 * j + 4 * h + g
                        for r in range(2):
                            for d in range(2):
                                for q in range(2):
                                    rows = slice(q * NST, (q + 1) * NST)
                                    last = pe.matmul(
                                        PS[q * NCH:(q + 1) * NCH, bank, g * P:(g + 1) * P],
                                        st[rows, d:NCH + d, r, d, gp],
                                        EC[rows, r, d, gp % (GP // 2), :, :].rearrange("p s c -> p (s c)"),
                                        start=False, stop=(g == 3 and r == 1 and d == 1), skip_group_check=True)
                last.then_inc(y_done, 1)

            def outputs_T(j):
                pe.wait_ge(y_copied, 2 * j + 2)
                for s in range(L):
                    last = pe.transpose(PS[:, 4 + 2 * (j % 2) + s // 4, (s % 4) * P:(s % 4 + 1) * P],
                                        Y[:, j, s, :, :].rearrange("p g c -> p (g c)"), ident[:])
                last.then_inc(yt_done, 1)

            pe.wait_ge(pmix_ready, MT)
            pe.nop().then_inc(ring_used, 1)
            out_pool(0, 0)
            pe.wait_ge(z_act, GP // 2)
            pe.wait_ge(z_dve, GP // 2)
            out_pool(1, 4)
            pe.wait_ge(wo_read, TT)
            out_pool(2, 0)
            pe.wait_ge(wo_read, 2 * TT)
            pe.wait_ge(t_loaded, 16)
            pe.wait_ge(ec_pool, 1)
            pe.wait_ge(scan_ready, 1)
            outputs(0)
            outputs(1)
            outputs_T(0)
            outputs_T(1)
            pe.wait_ge(wo_read, 3 * TT)
            out_pool(3, 0)
            pe.wait_ge(ec_pool, 2)
            pe.wait_ge(ec_dve, 1)
            pe.wait_ge(skip_done, 2)
            outputs(2)
            pe.wait_ge(skip_done, 4)
            outputs(3)
            outputs_T(2)
            outputs_T(3)

            pe.wait_ge(gelu_ready, MT)
            pe.wait_ge(wo_read, NN * TT)
            for m in range(MT):
                slot = FIRST_GLU + m // 2
                pe.wait_ge(ring_loaded[slot % 2], 16 * (slot // 2 + 1))
                if m >= 2:
                    pe.wait_ge(sig_ready, m - 1)
                for k in range(MT):
                    last = pe.matmul(PS[:, m % 2, :], ring_view(slot % 2, MT, 256)[:, k, (m % 2) * P:(m % 2 + 1) * P],
                                     uT[:, k, :], start=k == 0, stop=k == MT - 1)
                last.then_inc(glu_done, 1)
                if m % 2 == 1:
                    pe.wait_ge(glu_done, m + 1)
                    pe.nop().then_inc(ring_used, 1)

            def out_tile(i):
                bank = 4 - 4 * (i % 2)
                for n in range(NN):
                    for k in range(MT):
                        last = pe.matmul(PS[:, bank + n, :], Z[:, k, i * P:(i + 1) * P],
                                         w2[k // 4][:, k % 4, n * NCOL:(n + 1) * NCOL],
                                         start=k == 0, stop=k == MT - 1)
                last.then_inc(wo_done, 1)

            def router_tile(i):
                bank = 4 - 4 * (i % 2)
                pe.wait_ge(h_ready, i + 1)
                if i >= 2:
                    pe.wait_ge(logit_done, i - 1)
                for j in range(4):
                    for k in range(4):
                        kt = 4 * j + k
                        last = pe.transpose(PS[:, bank + j, k * P:(k + 1) * P], h1[:, i, kt * P:(kt + 1) * P],
                                            ident[:])
                    last.then_inc(ht_done, 1)
                pe.wait_ge(ht_ready, 4 * (i + 1))
                for kt in range(KT):
                    last = pe.matmul(PS[:, bank, 0:E1], hT[:, i % 2, kt, :], rw[:, kt, :],
                                     start=kt == 0, stop=kt == KT - 1)
                last.then_inc(logit_done, 1)

            pe.wait_ge(glu_ready, MT)
            pe.wait_ge(w2_loaded, 16 * MT)
            pe.wait_ge(ln_loaded, 96)
            out_tile(0)
            out_tile(1)
            router_tile(0)
            pe.wait_ge(logit_read, 1)
            out_tile(2)
            router_tile(1)
            pe.wait_ge(logit_read, 2)
            out_tile(3)
            router_tile(2)
            router_tile(3)
            pe.wait_ge(onehot_ready, 1)
            pe.wait_ge(iota_ready, 2)
            for i in range(TT):
                for k in range(i):
                    pe.matmul(PS[:, 5, i * NE:(i + 1) * NE], ones, one[:, k, :], start=k == 0, stop=False)
                pe.matmul(PS[:, 5, i * NE:(i + 1) * NE], tri, one[:, i, :], start=i == 0, stop=True)
            for i in range(TT):
                last = pe.matmul(PS[:, 5, TT * NE:(TT + 1) * NE], ones, one[:, i, :], start=i == 0, stop=i == TT - 1)
            last.then_inc(rank_done, 1)

            def select(h, b):
                for i in range(TT):
                    for a in range(2):
                        cols = h1[:, i, :].rearrange("p (d k) -> p d k", k=KT)[:, h * 64:(h + 1) * 64, 8 * a:8 * a + 8]
                        last = pe.matmul(PS[a * SLOTS:(a + 1) * SLOTS, (1, 7)[h], :], pick[b][:, i, :], cols,
                                         start=i == 0, stop=i == TT - 1)
                last.then_inc((sel_lo, sel_hi)[h], 1)

            def rows_T(n):
                pe.wait_ge(xg_act, n + 1)
                pe.wait_ge(xg_dve, n + 1)
                pe.nop().then_inc(pe_turn, 1)
                for k in range(8):
                    last = pe.transpose(PS[:, 2 + k // 4, (k % 4) * P:(k % 4 + 1) * P],
                                        xg.rearrange("p (d k) -> p k d", k=8)[:, k, :], ident[:])
                last.then_inc(xg_t, 1)

            def expert(n, b, after, last_pass):
                pe.wait_ge(xgT_act, n + 1)
                pe.wait_ge(xgT_dve, n + 1)
                for c in range(WQ):
                    pe.wait_ge(wg_loaded[c], n * 16 + 16)
                    pe.wait_ge(wu_loaded[c], n * 16 + 16)
                    for kt in range(4 * c, 4 * c + 4):
                        for m, w in enumerate((wg, wu)):
                            last = pe.matmul(PS[m * SLOTS:(m + 1) * SLOTS, 0, :], xgT[b][:, kt % 8 * 2 + kt // 8, :],
                                             w[:, kt, :], start=kt == 0, stop=kt == KT - 1)
                            if kt % 4 == 3:
                                last.then_inc(w_used, 1)
                pe.wait_ge(w_used, n * 12 + 8)
                pe.nop().then_inc(gu_done, 1)
                if not last_pass:
                    pe.wait_ge(sel_ready, n + 2)
                    select(0, 1 - b)
                pe.wait_ge(hid_ready, n + 1)
                pe.nop().then_inc(pe_turn, 1)
                for k in range(FT):
                    last = pe.transpose(PS[:, 4, k * SLOTS:(k + 1) * SLOTS],
                                        hid.rearrange("p (f k) -> p k f", k=FT)[:, k, :], ident[0:SLOTS, 0:SLOTS])
                last.then_inc(hid_t, 1)
                if not last_pass:
                    select(1, 1 - b)
                pe.wait_ge(hidT_ready, n + 1)
                if after:
                    pe.wait_ge(ye_act, n)
                    pe.wait_ge(ye_dve, n)
                for k in range(FT):
                    pe.wait_ge(wd_loaded[k], n * 16 + 16)
                    for c in range(2):
                        for m in range(2):
                            last = pe.matmul(PS[m * SLOTS:(m + 1) * SLOTS, 5 + c, :], hidT[:, k, :],
                                             wd[:, k, (2 * m + c) * NCOL:(2 * m + c + 1) * NCOL],
                                             start=k == 0, stop=k == FT - 1)
                    last.then_inc(w_used, 1)
                    if k == 1 and not last_pass:
                        rows_T(n + 1)
                pe.wait_ge(w_used, n * 12 + 12)
                pe.nop().then_inc(down_done, 1)

            pe.wait_ge(sel_ready, 1)
            select(0, 0)
            select(1, 0)
            rows_T(0)
            pe.wait_ge(table_ready, 1)
            for k in range(2):
                for i in range(TT):
                    last = pe.matmul(PS[:, 6, 0:NE], rank_eq[:, k, i, :], val_e[:, k, i, :],
                                     start=(k == 0 and i == 0), stop=(k == 1 and i == TT - 1))
            last.then_inc(table_done, 1)
            expert(0, 0, False, False)
            expert(1, 1, True, False)
            with pe.Fori(1, NE // 2 - 1) as i:
                for b in range(2):
                    expert(i * 2 + b, b, True, False)
            expert(NE - 2, 0, True, False)
            expert(NE - 1, 1, True, True)
            pe.wait_ge(counts_ready, 1)
            pe.wait_ge(ye_act, NE)
            pe.wait_ge(ye_dve, NE)
            with pe.If(pe.value_load(max_i[0:1, 0:1], min_val=0, max_val=S) > SLOTS):
                with pe.Fori(1, ROUNDS) as r:
                    with pe.Fori(0, NE) as e:
                        with pe.If(pe.value_load(cnt_i[0:1, bass.ds(e, 1)], min_val=0, max_val=S) > r * SLOTS):
                            no = pe.value_load(extra_no[0:1, bass.ds(r * NE + e, 1)], min_val=0, max_val=16)
                            pe.wait_ge(xg2_loaded, no * 16 + 16)
                            pe.nop().then_inc(pe_turn, 1)
                            for kt in range(KT):
                                last = pe.transpose(PS[:, 2 + kt // 8, (kt % 8) * SLOTS:(kt % 8 + 1) * SLOTS],
                                                    xg_rows.rearrange("p (d k) -> p k d", k=KT)[:, kt, :],
                                                    ident[0:SLOTS, 0:SLOTS])
                            last.then_inc(xpe, 1)
                            pe.wait_ge(xcopy, no * 5 + 1)
                            pe.wait_ge(xw_loaded, no * 48 + 48)
                            for kt in range(KT):
                                for m, w in enumerate((wg, wu)):
                                    last = pe.matmul(PS[m * SLOTS:(m + 1) * SLOTS, 0, :], xgT[0][:, kt, :],
                                                     w[:, kt, :], start=kt == 0, stop=kt == KT - 1)
                            last.then_inc(xpe, 1)
                            pe.wait_ge(xcopy, no * 5 + 3)
                            pe.nop().then_inc(pe_turn, 1)
                            for k in range(FT):
                                last = pe.transpose(PS[:, 4, k * SLOTS:(k + 1) * SLOTS],
                                                    hid.rearrange("p (f k) -> p k f", k=FT)[:, k, :],
                                                    ident[0:SLOTS, 0:SLOTS])
                            last.then_inc(xpe, 1)
                            pe.wait_ge(xcopy, no * 5 + 4)
                            for k in range(FT):
                                for c in range(2):
                                    for m in range(2):
                                        last = pe.matmul(PS[m * SLOTS:(m + 1) * SLOTS, 5 + c, :], hidT[:, k, :],
                                                         wd[:, k, (2 * m + c) * NCOL:(2 * m + c + 1) * NCOL],
                                                         start=k == 0, stop=k == FT - 1)
                            last.then_inc(xpe, 1)

        @block.vector
        def _(dve):
            chain = [0]

            def link(ins):
                chain[0] += 1
                ins.then_inc(dve_chain, 1)
                dve.wait_ge(dve_chain, chain[0])

            def tt(o, a, b, op):
                return dve.tensor_tensor(o, a, b, op)

            def ts(o, a, s1, s2, op0, op1=ALU.bypass):
                return dve.tensor_scalar(o, a, s1, s2, op0, op1)

            for i in range(TT):
                for j in range(1, 4, 2):
                    dve.wait_ge(xt_done, 4 * i + j + 1)
                    dve.tensor_copy(xT[:, 4 * j:4 * j + 4, i * P:(i + 1) * P],
                                    PS[:, j, :].rearrange("p (k t) -> p k t", k=4)).then_inc(xt_dve, 1)

            lr, li, lrdt, sin_in = (pre[:, j, :] for j in range(4))
            mag, sin, cos, cos_in = (pre[:, j, :] for j in range(4, 8))
            t0, t1 = pre[:, 8, :], pre[:, 9, :]
            ar, ai, zr, zi = (pre[:, 10 + j, :] for j in range(4))
            dve.wait_ge(pre_act, 1)
            for q in range(2):
                n = slice(q * NST, (q + 1) * NST)
                ts(t0[:, n], li[:, n], pdt[:, 2 + q:3 + q], None, ALU.mult)
                last = ts(lrdt[:, n], lr[:, n], pdt[:, 2 + q:3 + q], None, ALU.mult)
            last.then_inc(pre_dve, 1)
            dve.wait_ge(pre_dve, 1)
            magic = 12582912.0
            link(ts(t1, t0, 1.0 / (2.0 * math.pi), magic, ALU.mult, ALU.add))
            link(ts(t1, t1, magic, None, ALU.subtract))
            c1 = 6.28125
            c2 = 8.0 * round((2.0 * math.pi - c1) * 2 ** 19 / 8.0) / 2 ** 19
            c3 = 2.0 * math.pi - c1 - c2
            for cc in (c1, c2, c3):
                link(dve.scalar_tensor_tensor(out=t0, in0=t1, scalar=-cc, in1=t0, op0=ALU.mult, op1=ALU.add))
            link(ts(sin_in, t0, 3.1415925, -3.1415925, ALU.min, ALU.max))
            link(ts(t1, sin_in, -1.0, None, ALU.mult))
            link(tt(t1, t1, sin_in, ALU.max))
            ts(cos_in, t1, -1.0, math.pi / 2.0, ALU.mult, ALU.add).then_inc(pre_dve, 1)
            link(tt(t0, lr, lr, ALU.mult))
            link(tt(t1, li, li, ALU.mult))
            link(tt(t0, t0, t1, ALU.add))
            link(dve.reciprocal(t0, t0))
            dve.wait_ge(pre_act, 4)
            link(tt(ar, mag, cos, ALU.mult))
            link(tt(ai, mag, sin, ALU.mult))
            link(ts(mag, ar, -1.0, None, ALU.add))
            tt(zr, mag, lr, ALU.mult)
            tt(t1, ai, li, ALU.mult)
            tt(zi, ai, lr, ALU.mult)
            link(tt(sin, mag, li, ALU.mult))
            tt(zr, zr, t1, ALU.add)
            link(tt(zi, zi, sin, ALU.subtract))
            tt(zr, zr, t0, ALU.mult)
            tt(zi, zi, t0, ALU.mult).then_inc(pre_ready, 1)
            wide = S + 2 * PAD
            tA, tB = tmp[:, 0, :], tmp[:, 1, :]

            def pool_tile(m):
                w = WINDOWS[m // PGT]
                bank = 4 + m % 2
                dve.wait_ge(ring_used, m + 1)
                dve.memset(tA[:, 0:PAD], 0.0)
                dve.memset(tA[:, PAD + S:wide], 0.0)
                link(dve.tensor_copy(tA[:, PAD:PAD + S], PS[:, bank, :]))
                src, dst, sh, lo, hi = tA, tB, None, 1, wide - 1
                span = 2
                while True:
                    back, ahead = (1, 0) if span == 2 else (span // 4, span // 4)
                    if span == w:
                        link(tt(pd[:, m, :], src[:, PAD - back:PAD - back + S],
                                src[:, PAD + ahead:PAD + ahead + S], ALU.add))
                        break
                    link(tt(dst[:, lo:hi], src[:, lo - back:hi - back], src[:, lo + ahead:hi + ahead], ALU.add))
                    src, dst = dst, src
                    lo, hi, span = lo + span // 2, hi - span // 2, 2 * span
                q = m // PGT
                tt(pd[:, m, 0:w // 2], pd[:, m, 0:w // 2], edge[:, q, 0:w // 2], ALU.mult).then_inc(dve_chain, 1)
                chain[0] += 1
                if w > 2:
                    tt(pd[:, m, S - w // 2 + 1:S], pd[:, m, S - w // 2 + 1:S], edge[:, q, w // 2:w - 1],
                       ALU.mult).then_inc(dve_chain, 1)
                    chain[0] += 1
                dve.wait_ge(dve_chain, chain[0])
                dve.scalar_tensor_tensor(out=pd[:, m, :], in0=pd[:, m, :], scalar=1.0 / w, in1=PS[:, bank, :],
                                         op0=ALU.mult, op1=ALU.subtract).then_inc(pool_read, 1)

            dve.wait_ge(edge_ready, 1)
            pool_tile(0)
            pool_tile(1)

            dve.wait_ge(par_t, 1)
            dve.tensor_copy(par[:].rearrange("p q d g -> p (q d g)"), PS[:, 6, 0:4 * 2 * GP]).then_inc(par_ready, 1)
            dve.wait_ge(par_ready, 1)
            dve.wait_ge(b_loaded, 16 * 32)
            shape = [P, 2 * GP, C]

            def per_pair(q):
                return par[:, q, :, :].rearrange("p d g -> p (d g)").unsqueeze(2).to_broadcast(shape)

            def flat(v, r):
                return v[:, r].rearrange("p d g c -> p (d g) c")

            w0 = pw[:, 0, 0, :].rearrange("p (a c) -> p a c", c=C)
            w1 = pw[:, 0, 1, :].rearrange("p (a c) -> p a c", c=C)
            w2 = pw[:, 1, 0, :].rearrange("p (a c) -> p a c", c=C)
            w3 = pw[:, 1, 1, :].rearrange("p (a c) -> p a c", c=C)
            for hf in range(2):
                sl = slice(hf * GP, (hf + 1) * GP)
                sh = [P, GP, C]
                z_r = par[:, 2, hf, :].unsqueeze(2).to_broadcast(sh)
                z_i = par[:, 3, hf, :].unsqueeze(2).to_broadcast(sh)
                br_, bi_ = braw[:, 0, hf], braw[:, 1, hf]
                tt(w0, br_, z_r, ALU.mult)
                tt(w1, bi_, z_i, ALU.mult)
                tt(w2, bi_, z_r, ALU.mult)
                link(tt(w3, br_, z_i, ALU.mult))
                tt(bbar[:, 0, hf], w0, w1, ALU.subtract)
                link(tt(bbar[:, 1, hf], w2, w3, ALU.add))

            def b_powers(d, tiles):
                sh4 = [P, 2, GP, C]
                a_r = par[:, 0, d, :].unsqueeze(1).unsqueeze(3).to_broadcast(sh4)
                a_i = par[:, 1, d, :].unsqueeze(1).unsqueeze(3).to_broadcast(sh4)
                T1 = pw[:, 0].rearrange("p r (g c) -> p r g c", c=C)
                T2 = pw[:, 1].rearrange("p r (g c) -> p r g c", c=C)
                slot = (lambda q: q) if d == 0 else (lambda q: L - 1 - q)
                link(dve.tensor_copy(BT[:, :, :, slot(0), :], bbar[:, :, d]))
                for q in range(1, L):
                    v = BT[:, :, :, slot(q - 1), :]
                    tt(T1, v, a_r, ALU.mult)
                    link(tt(T2, v, a_i, ALU.mult))
                    tt(BT[:, 0, :, slot(q), :], T1[:, 0], T2[:, 1], ALU.subtract)
                    last = tt(BT[:, 1, :, slot(q), :], T1[:, 1], T2[:, 0], ALU.add)
                    if q < L - 1:
                        link(last)
                    if q in tiles:
                        pool_tile(tiles[q])
                last.then_inc(bt_ready, 1)

            def c_blocks(d):
                for q in range(2):
                    rows = slice(q * NST, (q + 1) * NST)
                    last = dve.tensor_copy(FB[rows, :, :, q, :], FC[rows, :, d, :, :])
                last.then_inc(fb_ready, 1)

            dve.memset(r_ssm[:, 2048:4096], 0.0).then_inc(fb_clear, 1)
            b_powers(0, {1: 2, 3: 3, 5: 4})
            dve.wait_ge(fb_clear, 1)
            dve.wait_ge(fc_ready, 4)
            c_blocks(0)
            for m in range(5, MT):
                pool_tile(m)

            def lags_in(d):
                dve.wait_ge(lag_done, d + 1)
                dve.tensor_copy(lag_rows.rearrange("p (h b) t -> p h (b t)", h=2), PS[:, 6:8, :]).then_inc(lag_mid, 1)

            def lags_out(d):
                dve.wait_ge(lag_t, d + 1)
                for h in range(2):
                    gs = slice(h * (GP // 2), (h + 1) * (GP // 2))
                    last = dve.tensor_copy(ksb[:, d, :, :, gs],
                                           PS[:, 6 + h, :].rearrange("p (g q c) -> p c q g", q=2, c=C))
                last.then_inc(lag_copied, 1)

            lags_in(0)
            c_blocks(1)
            lags_out(0)
            dve.wait_ge(btt_done, GP // 2)
            b_powers(1, {})
            lags_in(1)
            lags_out(1)

            def add_out(n, count, bank, first):
                dve.wait_ge(wo_done, count)
                for i in range(TT):
                    cols = h1[:, i, n * NCOL:(n + 1) * NCOL]
                    if first:
                        dve.scalar_tensor_tensor(out=cols, in0=cols, scalar=ALPHA, in1=PS[:, bank + i, :],
                                                 op0=ALU.mult, op1=ALU.add).then_inc(wo_read, 1)
                    else:
                        tt(cols, cols, PS[:, bank + i, :], ALU.add).then_inc(wo_read, 1)

            pa = par[:].rearrange("p q d g -> p q (d g)")
            cr, ci = coef[:, 0, 0, :], coef[:, 0, 1, :]
            s0, s1 = tmp[:, 0, 0:2 * GP], tmp[:, 0, 2 * GP:4 * GP]
            s2 = tmp[:, 0, 4 * GP:6 * GP]
            pr, pi_ = tmp[:, 1, 0:2 * GP], tmp[:, 1, 2 * GP:4 * GP]
            dve.tensor_copy(pr, pa[:, 0, :])
            link(dve.tensor_copy(pi_, pa[:, 1, :]))
            for _ in range(int(math.log2(L))):
                tt(s0, pr, pr, ALU.mult)
                tt(s1, pi_, pi_, ALU.mult)
                link(tt(s2, pr, pi_, ALU.mult))
                tt(pr, s0, s1, ALU.subtract)
                link(ts(pi_, s2, 2.0, None, ALU.mult))
            dve.tensor_copy(coef[:, 0, 0, :], pr)
            dve.tensor_copy(coef[:, 0, 1, :], pr)
            dve.tensor_copy(coef[:, 1, 0, :], pi_)
            link(ts(coef[:, 1, 1, :], pi_, -1.0, None, ALU.mult))
            for j in range(1, GP // 2, 2):
                dve.wait_ge(z_done, j + 1)
                for d in range(2):
                    src = PS[:, 4 + j % 4, :].rearrange("p (g r d k) -> p d k r g", g=2, r=2, d=2)[:, d]
                    dve.tensor_copy(st[:, 1 - d:NCH + 1 - d, :, d, 2 * j:2 * j + 2], src).then_inc(z_dve, 1)
            dve.wait_ge(z_dve, GP // 2)
            dve.wait_ge(z_act, GP // 2)
            sT = tmp[:, 0, 0:8 * GP].rearrange("p (d q r g) -> p d q r g", d=2, q=2, r=2)
            sS = tmp[:, 0, 8 * GP:12 * GP].rearrange("p (d r g) -> p d r g", d=2, r=2)
            dve.memset(st[:, 0, :, 0, :], 0.0)
            dve.memset(st[:, NCH, :, 1, :], 0.0)

            def entry(t, d):
                return st[:, bass.ds(t, 1), :, d, :].rearrange("p o r g -> p (o r) g")

            def scan(i, j, count):
                last = [entry(i * UN + (j + 1), 0), entry(i * -UN + (NCH - 1 - j), 1)]
                cur = [entry(i * UN + (j + 2), 0), entry(i * -UN + (NCH - 2 - j), 1)]
                for d in range(2):
                    if count is not None:
                        dve.wait_ge(scan_step, count - 1 + d)
                    c = coef[:, :, :, d * GP:(d + 1) * GP]
                    tt(sT[:, d], last[d].unsqueeze(1).to_broadcast([P, 2, 2, GP]), c, ALU.mult).then_inc(scan_step, 1)
                at = i * (6 * UN) + 6 * j
                for d in range(2):
                    dve.wait_ge(scan_step, at + (1 + d))
                    tt(sS[:, d], sT[:, d, 0], sT[:, d, 1, ::-1, :], ALU.add).then_inc(scan_step, 1)
                for d in range(2):
                    dve.wait_ge(scan_step, at + (3 + d))
                    tt(cur[d], cur[d], sS[:, d], ALU.add).then_inc(scan_step, 1)

            UN = 7

            def scan_part(lo, hi):
                with dve.Fori(lo, hi) as i:
                    for j in range(UN):
                        scan(i, j, i * (6 * UN) + 6 * j if j > 0 else None)
                    dve.wait_ge(scan_step, i * (6 * UN) + 6 * UN)

            scan_part(0, 5)
            dve.wait_ge(xr_loaded, 16)
            add_out(0, 1, 0, True)
            scan_part(5, (NCH - 1) // UN)
            dve.memset(sS, 0.0).then_inc(scan_ready, 1)

            def skips(lo, hi):
                for m in range(lo, hi):
                    j, q = m // 2, m % 2
                    dve.wait_ge(yt_done, j + 1)
                    bank = 4 + 2 * (j % 2)
                    u = uT[:, m, :].rearrange("p (s k) -> p s k", s=L)
                    dve.scalar_tensor_tensor(
                        out=u, in0=u, scalar=vecs[:, 1, m:m + 1],
                        in1=PS[:, bank:bank + 2, :].rearrange("p b (s q k) -> p q (b s) k", q=2, k=NCH)[:, q],
                        op0=ALU.mult, op1=ALU.add).then_inc(skip_done, 1)

            dve.wait_ge(scan_ready, 1)
            add_out(1, 2, 4, True)
            add_out(2, 3, 0, True)
            dve.wait_ge(ec_pool, 1)
            dve.wait_ge(y_done, 2)
            c_powers(dve, link, DVE_PAIRS, tmp[:, 0, :], ec_dve)
            dve.wait_ge(vec_loaded, 48)
            skips(0, 4)
            add_out(3, 4, 0, True)
            skips(4, MT)

            for m in range(MT):
                dve.wait_ge(sig_ready, m + 1)
                tt(Z[:, m, :].rearrange("p (k s) -> p s k", s=L),
                   tmp[:, m % 2, 0:S].rearrange("p (s k) -> p s k", s=L),
                   uT[:, m, :].rearrange("p (s k) -> p s k", s=L), ALU.mult).then_inc(glu_ready, 1)
            def norm_stats(i, lt, asked, meanwhile=None):
                for q in range(4):
                    last = dve.bn_stats(stats[:, q, :], h1[:, i, q * NCOL:(q + 1) * NCOL])
                link(last)
                link(dve.bn_aggr(lt[:, 4:6], stats[:]))
                ts(lt[:, 0:1], lt[:, 5:6], EPS, None, ALU.add).then_inc(std_asked, 1)
                if meanwhile:
                    meanwhile()
                dve.wait_ge(std_ready, asked)
                link(dve.reciprocal(lt[:, 2:3], lt[:, 1:2]))
                link(tt(lt[:, 3:4], lt[:, 2:3], lt[:, 2:3], ALU.mult))
                link(tt(lt[:, 3:4], lt[:, 3:4], lt[:, 0:1], ALU.mult))
                link(ts(lt[:, 3:4], lt[:, 3:4], -0.5, 1.5, ALU.mult, ALU.add))
                link(tt(lt[:, 2:3], lt[:, 3:4], lt[:, 2:3], ALU.mult))

            def ln1_tile(i):
                row, lt = h1[:, i, :], lnt[:, 0]
                dve.wait_ge(wo_done, NN + i + 1)
                for n in range(NN):
                    cols = h1[:, i, n * NCOL:(n + 1) * NCOL]
                    tt(cols, cols, PS[:, 4 - 4 * (i % 2) + n, :], ALU.add).then_inc(wo_read, 1)
                dve.wait_ge(wo_read, (NN + i + 1) * NN)
                norm_stats(i, lt, i + 1, lambda: dve.scalar_tensor_tensor(
                    out=row, in0=row, scalar=lt[:, 4:5], in1=ln1g, op0=ALU.subtract, op1=ALU.mult))
                dve.scalar_tensor_tensor(out=row, in0=row, scalar=lt[:, 2:3], in1=ln1b, op0=ALU.mult, op1=ALU.add
                                         ).then_inc(h_ready, 1)

            dve.wait_ge(ln_loaded, 96)
            for i in range(TT):
                ln1_tile(i)

            dve.wait_ge(iota_ready, 2)
            dve.wait_ge(logit_read, TT)
            link(tt(lg, lg, rbias.unsqueeze(1).to_broadcast([P, TT, E1]), ALU.add))
            sg = [P, TT, NG]
            link(dve.tensor_reduce(gmax, lg[:, :, 0:NG], AX, ALU.max))
            tt(gd, lg[:, :, 0:NG], gmax.unsqueeze(2).to_broadcast(sg), ALU.subtract).then_inc(exp_asked, 1)
            dve.wait_ge(exp_asked, 1)
            link(ts(gv, gd, 0.0, None, ALU.is_equal))
            link(tt(gv, gv, iota_g.unsqueeze(1).to_broadcast(sg), ALU.mult))
            link(dve.tensor_reduce(vmax, gv, AX, ALU.max))
            link(tt(gm, gv, vmax.unsqueeze(2).to_broadcast(sg), ALU.is_equal))
            link(tt(prod, lg[:, :, NG:E1].rearrange("p i (g j) -> p i g j", g=NG),
                    gm.unsqueeze(3).to_broadcast([P, TT, NG, EPG]), ALU.mult))
            link(dve.tensor_reduce(sel, prod.rearrange("p i g j -> p i j g"), AX, ALU.add))
            for i in range(TT):
                last = dve.max(top[:, i, :], sel[:, i, :])
            link(last)
            for i in range(TT):
                last = dve.max_index(topi[:, i, :], top[:, i, :], sel[:, i, :])
            link(last)
            tt(gap, top[:, :, 1], top[:, :, 0], ALU.subtract).then_inc(exp_asked, 1)
            link(ts(gbase, vmax, -float(EPG), float(NG * EPG), ALU.mult, ALU.add))
            link(dve.tensor_copy(topf, topi))
            for k in range(2):
                last = tt(eid[:, k, :], topf[:, :, k], gbase, ALU.add)
            link(last)
            se = [P, TT, NE]
            ie = iota_e.unsqueeze(1).to_broadcast(se)
            for k in range(2):
                last = tt(onek[:, k], ie, eid[:, k, :].unsqueeze(2).to_broadcast(se), ALU.is_equal)
            link(last)
            tt(one, onek[:, 0], onek[:, 1], ALU.add).then_inc(onehot_ready, 1)
            def rows_copied(n):
                dve.wait_ge(sel_hi, n + 1)
                dve.tensor_copy(xg[:, NCOL:2 * NCOL], PS[:, 7, :]).then_inc(xg_dve, 1)

            def rows_T_copied(n, b):
                dve.wait_ge(xg_t, n + 1)
                dve.tensor_copy(xgT[b][:, 8:16, :].rearrange("p k t -> p (k t)"), PS[:, 3, :]).then_inc(xgT_dve, 1)

            dve.wait_ge(rank_done, 1)
            link(dve.scalar_tensor_tensor(out=place.rearrange("p i e -> p (i e)"), in0=PS[:, 5, 0:TT * NE], scalar=1.0,
                                          in1=one.rearrange("p i e -> p (i e)"), op0=ALU.add, op1=ALU.mult))

            def selection(e, b):
                s3 = [P, TT, SLOTS]
                tt(pick[b], iota_s.unsqueeze(1).to_broadcast(s3), place[:, :, bass.ds(e, 1)].to_broadcast(s3),
                   ALU.is_equal).then_inc(sel_ready, 1)

            selection(0, 0)
            selection(1, 1)
            for k in range(2):
                link(tt(prod2, PS[:, 5, 0:TT * NE].rearrange("p (i e) -> p i e", i=TT), onek[:, k], ALU.mult))
                link(dve.tensor_reduce(rank_k[:, k, :], prod2, AX, ALU.add))
            for k in range(2):
                for i in range(TT):
                    ts(rank_eq[:, k, i, :], iota_m, rank_k[:, k, i:i + 1], None, ALU.is_equal)
                last = tt(val_e[:, k], onek[:, k], val_f[:, :, k].unsqueeze(2).to_broadcast(se), ALU.mult)
            last.then_inc(table_ready, 1)
            rows_copied(0)
            rows_T_copied(0, 0)
            dve.wait_ge(table_done, 1)
            link(ts(slot_i, PS[:, 6, 0:NE], float(EMPTY), None, ALU.add))
            ts(slot_s, slot_i, 2.0, half[:, 0:1], ALU.mult, ALU.add).then_inc(slots_ready, 1)
            dve.wait_ge(exp_ready, 2)
            link(dve.tensor_reduce(gsum, ge, AX, ALU.add))
            link(dve.reciprocal(pgrp, gsum))
            link(ts(epl, egap, 1.0, None, ALU.add))
            link(dve.reciprocal(epl, epl))
            link(tt(gate[:, 0, :], pgrp, epl, ALU.mult))
            link(tt(gate[:, 1, :], gate[:, 0, :], egap, ALU.mult))
            link(ts(pos, rank_k, float(NE), None, ALU.mult))
            link(tt(pos, pos, eid, ALU.add))
            dve.tensor_copy(pos_i, pos).then_inc(pos_ready, 1)
            link(dve.tensor_copy(cnt, PS[:, 5, TT * NE:(TT + 1) * NE]))
            dve.tensor_copy(cnt_i, cnt)
            link(dve.tensor_reduce(max_f, cnt, AX, ALU.max))
            dve.tensor_copy(max_i, max_f)
            dve.memset(extra_flag[:, 0:NE], 0.0)
            for r in range(1, ROUNDS):
                last = ts(extra_flag[:, r * NE:(r + 1) * NE], cnt, float(r * SLOTS), None, ALU.is_gt)
            link(last)
            link(dve.tensor_tensor_scan(extra_scan, ones[:, 0:1].to_broadcast([P, ROUNDS * NE]), extra_flag, 0.0,
                                        ALU.mult, ALU.add))
            link(tt(extra_flag, extra_scan, extra_flag, ALU.subtract))
            link(dve.tensor_copy(extra_flag[:, 0:1], extra_scan[:, ROUNDS * NE - 1:ROUNDS * NE]))
            dve.tensor_copy(extra_no, extra_flag).then_inc(counts_ready, 1)


            def expert(n, b, after, last_pass, more):
                dve.wait_ge(silu_ready, n + 1)
                tt(hid, sil, PS[SLOTS:P, 0, :], ALU.mult).then_inc(hid_ready, 1)
                dve.wait_ge(hid_t, n + 1)
                dve.tensor_copy(hidT.rearrange("p k t -> p (k t)"), PS[:, 4, 0:FT * SLOTS]).then_inc(hidT_ready, 1)
                if not last_pass:
                    rows_copied(n + 1)
                    if more:
                        selection(n + 2, b)
                    rows_T_copied(n + 1, 1 - b)
                dve.wait_ge(down_done, n + 1)
                if after:
                    dve.wait_ge(ye_stored, n * 16 - 16)
                dve.tensor_copy(yb[b][:, NCOL:2 * NCOL], PS[:, 6, :]).then_inc(ye_dve, 1)

            expert(0, 0, False, False, True)
            expert(1, 1, False, False, True)
            with dve.Fori(1, NE // 2 - 1) as i:
                for b in range(2):
                    expert(i * 2 + b, b, True, False, True)
            expert(NE - 2, 0, True, False, False)
            expert(NE - 1, 1, True, True, False)
            dve.wait_ge(h_stored, 16 * TT)
            for i in range(TT):
                ts(h1[:, i, :], h1[:, i, :], ALPHA, None, ALU.mult).then_inc(h_scaled, 1)
            with dve.If(dve.value_load(max_i[0:1, 0:1], min_val=0, max_val=S) > SLOTS):
                with dve.Fori(1, ROUNDS) as r:
                    with dve.Fori(0, NE) as e:
                        with dve.If(dve.value_load(cnt_i[0:1, bass.ds(e, 1)], min_val=0, max_val=S) > r * SLOTS):
                            no = dve.value_load(extra_no[0:1, bass.ds(r * NE + e, 1)], min_val=0, max_val=16)
                            dve.wait_ge(xs_loaded, no * 32 + 32)
                            dve.tensor_scalar(xgi, xslot, 1, None, ALU.logical_shift_right)
                            ts(xsi, xslot, 2.0, half[:, 0:1], ALU.mult, ALU.add).then_inc(xs_ready, 1)
                            dve.wait_ge(xpe, no * 4 + 1)
                            dve.tensor_copy(xgT[0].rearrange("p (a k) t -> p a (k t)", a=2), PS[:, 2:4, :]
                                            ).then_inc(xcopy, 1)
                            dve.wait_ge(xcopy, no * 5 + 2)
                            tt(hid, sil, PS[SLOTS:P, 0, :], ALU.mult).then_inc(xcopy, 1)
                            dve.wait_ge(xpe, no * 4 + 3)
                            dve.tensor_copy(hidT.rearrange("p k t -> p (k t)"), PS[:, 4, 0:FT * SLOTS]
                                            ).then_inc(xcopy, 1)
                            dve.wait_ge(xpe, no * 4 + 4)
                            dve.tensor_copy(yb[0].rearrange("p (a n) -> p a n", a=2), PS[:, 5:7, :]).then_inc(xcopy, 1)

            dve.wait_ge(h_scaled, TT)
            dve.wait_ge(ln2_loaded, 32)

            def combine(i):
                dve.wait_ge(res_loaded[i], 16)
                for k in range(2):
                    link(dve.scalar_tensor_tensor(out=h1[:, i, :], in0=res[i][:, k * D:(k + 1) * D],
                                                  scalar=gate[:, k, i:i + 1], in1=h1[:, i, :],
                                                  op0=ALU.mult, op1=ALU.add))
                norm_stats(i, lnt[:, i], TT + i + 1)
                dve.scalar_tensor_tensor(out=lnt[:, i, 6:7], in0=lnt[:, i, 4:5], scalar=-1.0, in1=lnt[:, i, 2:3],
                                         op0=ALU.mult, op1=ALU.mult).then_inc(scale_ready, 1)

            def gain(i):
                dve.wait_ge(normed, i + 1)
                tt(h1[:, i, :], h1[:, i, :], ln2g, ALU.mult).then_inc(gained, 1)

            combine(0)
            for i in range(1, TT):
                combine(i)
                gain(i - 1)
            gain(TT - 1)


_INS = ["x", "w_in", "pool_w", "pool_scale", "ssm_a_re", "ssm_a_im", "ssm_log_dt", "ssm_b_re", "ssm_b_im",
        "ssm_c_re", "ssm_c_im", "ssm_d", "glu_w", "glu_b", "w_out", "ln1_g", "ln1_b", "router_g_w", "router_g_b",
        "router_e_w", "router_e_b", "w_gate", "w_up", "w_down", "ln2_g", "ln2_b"]


def kernel(**inputs):
    import numpy as np
    import concourse.bacc as bacc
    from concourse.bass_utils import run_bass_kernel_spmd

    nc = bacc.Bacc("TRN2", target_bir_lowering=False, num_devices=1)
    arrays, args = {}, []
    for name in _INS:
        a = np.ascontiguousarray(inputs[name])[0]
        arrays[f"in_{name}"] = a
        args.append(nc.dram_tensor(f"in_{name}", a.shape, mybir.dt.from_np(a.dtype), kind="ExternalInput").ap())
    args.append(nc.dram_tensor("out_h", (S, D), F32, kind="ExternalOutput").ap())
    build(nc, *args)
    r = run_bass_kernel_spmd(nc, [arrays], core_ids=[0])
    return r.results[0]["out_h"].reshape(1, S, D)
```
